# Optimizing a Trainium2 kernel written in Bass

```python
import math
import jax, jax.numpy as jnp
from jax import lax
import numpy as np

D_MODEL = 1024
BATCH = 1
SEQ = 256
DEPTH = 1

N_MEM = 256
D_MIX = D_MODEL
N_HEADS_A = 8
N_KV_A = 2
HEAD_DIM_A = 64
GQA_GROUP = N_HEADS_A // N_KV_A
WINDOW = 128
BLOCK = 128
NUM_BUCKETS = 32
MAX_EXACT = NUM_BUCKETS // 2
MAX_DISTANCE = 128
N_HEADS_B = 4
HEAD_DIM_B = 128
CHUNK = 128
CONV_WIDTH = 4
N_HEADS_X = 4
HEAD_DIM_X = D_MODEL // N_HEADS_X
N_GROUPS = 4
EXPERTS_PER_GROUP = 8
N_EXPERTS = N_GROUPS * EXPERTS_PER_GROUP
TOP_K = 2
D_EXPERT = 512
EPS = 1e-6
NEG_INF = -1e30

W_A_Q = N_HEADS_A * HEAD_DIM_A
W_A_KV = N_KV_A * HEAD_DIM_A
W_B = N_HEADS_B * HEAD_DIM_B
IN_WIDTHS = (W_A_Q, W_A_KV, W_A_KV, W_B, W_B, W_B, W_B, N_HEADS_B, N_HEADS_B)
D_IN = sum(IN_WIDTHS)
IN_SPLITS = tuple(int(c) for c in np.cumsum(IN_WIDTHS)[:-1])

kernel_name = 'hymba_swa_mlstm_hmoe_layer'

def rmsnorm(x, g):
    xf = x.astype(jnp.float32)
    y = xf * lax.rsqrt(jnp.mean(xf * xf, axis=-1, keepdims=True) + EPS)
    return (y * g.astype(jnp.float32)).astype(x.dtype)

def t5_band_bias(table):
    i = jnp.arange(BLOCK)[:, None]
    j = jnp.arange(2 * BLOCK)[None, :]
    n = jnp.maximum(i + BLOCK - j, 0)
    nf = jnp.maximum(n, 1).astype(jnp.float32)
    large = MAX_EXACT + (jnp.log(nf / MAX_EXACT) / math.log(MAX_DISTANCE / MAX_EXACT)
                         * (NUM_BUCKETS - MAX_EXACT)).astype(jnp.int32)
    large = jnp.minimum(large, NUM_BUCKETS - 1)
    bucket = jnp.where(n < MAX_EXACT, n, large)
    bias = table.astype(jnp.float32)[bucket]
    return jnp.transpose(bias, (2, 0, 1)).reshape(N_KV_A, GQA_GROUP, BLOCK, 2 * BLOCK)

def swa_sink_attention(q, k, v, sinks, rel_bias):
    B, S = q.shape[0], q.shape[1]
    nb = S // BLOCK
    qb = q.reshape(B, nb, BLOCK, N_KV_A, GQA_GROUP, HEAD_DIM_A)

    def band(t):
        tp = jnp.pad(t, ((0, 0), (BLOCK, 0), (0, 0), (0, 0)))
        tp = tp.reshape(B, nb + 1, BLOCK, N_KV_A, HEAD_DIM_A)
        return jnp.concatenate([tp[:, :-1], tp[:, 1:]], axis=2)

    kb, vb = band(k), band(v)
    s = jnp.einsum('bnqkgd,bnskd->bnkgqs', qb, kb).astype(jnp.float32) * (HEAD_DIM_A ** -0.5)
    s = s + rel_bias
    i = jnp.arange(BLOCK)[:, None]
    j = jnp.arange(2 * BLOCK)[None, :]
    d = i + BLOCK - j
    band_ok = (d >= 0) & (d < WINDOW)
    first_ok = (jnp.arange(nb)[:, None, None] > 0) | (j >= BLOCK)[None]
    mask = (band_ok[None] & first_ok)[None, :, None, None]
    s = jnp.where(mask, s, NEG_INF)
    sink = sinks.astype(jnp.float32).reshape(N_KV_A, GQA_GROUP, 1)
    m = jnp.maximum(s.max(axis=-1), sink)
    p = jnp.exp(s - m[..., None])
    denom = p.sum(axis=-1) + jnp.exp(sink - m)
    p = (p / denom[..., None]).astype(v.dtype)
    o = jnp.einsum('bnkgqs,bnskd->bnqkgd', p, vb)
    return o.reshape(B, S, W_A_Q)

def causal_depthwise_conv(u, w, b):
    y = lax.conv_general_dilated(u, w.astype(u.dtype), window_strides=(1,),
                                 padding=((CONV_WIDTH - 1, 0),),
                                 dimension_numbers=('NWC', 'WIO', 'NWC'),
                                 feature_group_count=u.shape[-1])
    return y + b.astype(u.dtype)

def mlstm_chunkwise(q, k, v, i_pre, logf):
    B, S = q.shape[0], q.shape[1]
    nc = S // CHUNK

    def to_chunks(t):
        t = t.reshape((B, nc, CHUNK) + t.shape[2:])
        return jnp.moveaxis(jnp.moveaxis(t, 1, 0), 3, 2)

    xs = (to_chunks(q * (HEAD_DIM_B ** -0.5)), to_chunks(k), to_chunks(v),
          to_chunks(i_pre), to_chunks(logf))
    tri = jnp.tril(jnp.ones((CHUNK, CHUNK), dtype=bool))

    def step(carry, xc):
        C, n, m = carry
        qc, kc, vc, ic, fc = xc
        b = jnp.cumsum(fc, axis=-1)
        logD = b[..., :, None] - b[..., None, :] + ic[..., None, :]
        logD = jnp.where(tri, logD, NEG_INF)
        inter = b + m[..., None]
        m_t = jnp.maximum(inter, logD.max(axis=-1))
        a_inter = jnp.exp(inter - m_t)
        sc = jnp.einsum('bhtd,bhsd->bhts', qc, kc) * jnp.exp(logD - m_t[..., None])
        num = jnp.einsum('bhts,bhsd->bhtd', sc, vc) + a_inter[..., None] * jnp.einsum('bhvk,bhtk->bhtv', C, qc)
        den = sc.sum(axis=-1) + a_inter * jnp.einsum('bhk,bhtk->bht', n, qc)
        h = num / jnp.maximum(jnp.abs(den), jnp.exp(-m_t))[..., None]
        bL = b[..., -1]
        logw = bL[..., None] - b + ic
        m_new = jnp.maximum(bL + m, logw.max(axis=-1))
        w = jnp.exp(logw - m_new[..., None])
        decay = jnp.exp(bL + m - m_new)
        C_new = decay[..., None, None] * C + jnp.einsum('bhs,bhsv,bhsk->bhvk', w, vc, kc)
        n_new = decay[..., None] * n + jnp.einsum('bhs,bhsk->bhk', w, kc)
        return (C_new, n_new, m_new), h

    H = N_HEADS_B
    init = (jnp.zeros((B, H, HEAD_DIM_B, HEAD_DIM_B), jnp.float32),
            jnp.zeros((B, H, HEAD_DIM_B), jnp.float32),
            jnp.zeros((B, H), jnp.float32))
    _, hs = lax.scan(step, init, xs)
    hs = jnp.moveaxis(jnp.moveaxis(hs, 0, 1), 3, 2)
    return hs.reshape(B, S, H, HEAD_DIM_B)

def setup_inputs(seed: int = 0) -> dict:
    key = jax.random.key(seed)
    ks = jax.random.split(key, 32)
    f32 = jnp.float32

    def nrm(k, shape, scale):
        return jax.random.normal(k, shape, f32) * scale

    L = DEPTH
    return {
        'x': nrm(ks[0], (BATCH, SEQ, D_MODEL), 1.0),
        'mem': nrm(ks[1], (BATCH, N_MEM, D_MODEL), 1.0),
        'rel_bias_table': nrm(ks[2], (NUM_BUCKETS, N_HEADS_A), 0.5),
        'norm_mix': 1.0 + nrm(ks[3], (L, D_MODEL), 0.02),
        'w_in': nrm(ks[4], (L, D_MODEL, D_IN), D_MODEL ** -0.5),
        'attn_sinks': nrm(ks[5], (L, N_HEADS_A), 0.5),
        'conv_w': nrm(ks[6], (L, CONV_WIDTH, 1, 2 * W_B), CONV_WIDTH ** -0.5),
        'conv_b': nrm(ks[7], (L, 2 * W_B), 0.02),
        'gate_bias_i': nrm(ks[8], (L, N_HEADS_B), 0.1),
        'gate_bias_f': jnp.linspace(3.0, 6.0, N_HEADS_B, dtype=f32)[None] + nrm(ks[9], (L, N_HEADS_B), 0.1),
        'mlstm_norm': 1.0 + nrm(ks[10], (L, W_B), 0.02),
        'w_out': nrm(ks[11], (L, D_MIX, D_MODEL), D_MIX ** -0.5),
        'norm_cross': 1.0 + nrm(ks[12], (L, D_MODEL), 0.02),
        'norm_mem': 1.0 + nrm(ks[13], (L, D_MODEL), 0.02),
        'w_cq': nrm(ks[14], (L, D_MODEL, D_MODEL), D_MODEL ** -0.5),
        'w_ck': nrm(ks[15], (L, D_MODEL, D_MODEL), D_MODEL ** -0.5),
        'w_cv': nrm(ks[16], (L, D_MODEL, D_MODEL), D_MODEL ** -0.5),
        'w_co': nrm(ks[17], (L, D_MODEL, D_MODEL), D_MODEL ** -0.5),
        'norm_moe': 1.0 + nrm(ks[18], (L, D_MODEL), 0.02),
        'w_router_group': nrm(ks[19], (L, D_MODEL, N_GROUPS), D_MODEL ** -0.5),
        'b_router_group': nrm(ks[20], (L, N_GROUPS), 0.01),
        'w_router_expert': nrm(ks[21], (L, D_MODEL, N_EXPERTS), D_MODEL ** -0.5),
        'b_router_expert': nrm(ks[22], (L, N_EXPERTS), 0.01),
        'w_exp_gate': nrm(ks[23], (L, N_EXPERTS, D_MODEL, D_EXPERT), D_MODEL ** -0.5),
        'w_exp_up': nrm(ks[24], (L, N_EXPERTS, D_MODEL, D_EXPERT), D_MODEL ** -0.5),
        'w_exp_down': nrm(ks[25], (L, N_EXPERTS, D_EXPERT, D_MODEL), D_EXPERT ** -0.5),
        'norm_final': 1.0 + nrm(ks[26], (D_MODEL,), 0.02),
    }

def reference(x, mem, rel_bias_table, norm_mix, w_in, attn_sinks, conv_w, conv_b,
              gate_bias_i, gate_bias_f, mlstm_norm, w_out, norm_cross, norm_mem,
              w_cq, w_ck, w_cv, w_co, norm_moe, w_router_group, b_router_group,
              w_router_expert, b_router_expert, w_exp_gate, w_exp_up, w_exp_down,
              norm_final):
    f32 = jnp.float32
    B, S = x.shape[0], x.shape[1]
    T = B * S
    rel_bias = t5_band_bias(rel_bias_table)

    for l in range(DEPTH):
        h = rmsnorm(x, norm_mix[l])
        proj = h @ w_in[l]
        qa, ka, va, qb, kb, vb, ob, ib, fb = jnp.split(proj, IN_SPLITS, axis=-1)
        out_a = swa_sink_attention(qa.reshape(B, S, N_HEADS_A, HEAD_DIM_A),
                                   ka.reshape(B, S, N_KV_A, HEAD_DIM_A),
                                   va.reshape(B, S, N_KV_A, HEAD_DIM_A),
                                   attn_sinks[l], rel_bias)
        qk_b = jax.nn.silu(causal_depthwise_conv(jnp.concatenate([qb, kb], axis=-1),
                                                 conv_w[l], conv_b[l]))
        qb_c, kb_c = jnp.split(qk_b, 2, axis=-1)
        i_pre = ib.astype(f32) + gate_bias_i[l].astype(f32)
        logf = jax.nn.log_sigmoid(fb.astype(f32) + gate_bias_f[l].astype(f32))
        hb = mlstm_chunkwise(qb_c.astype(f32).reshape(B, S, N_HEADS_B, HEAD_DIM_B),
                             kb_c.astype(f32).reshape(B, S, N_HEADS_B, HEAD_DIM_B),
                             vb.astype(f32).reshape(B, S, N_HEADS_B, HEAD_DIM_B),
                             i_pre, logf)
        hb = jax.nn.sigmoid(ob.astype(f32)).reshape(B, S, N_HEADS_B, HEAD_DIM_B) * hb
        hb = hb * lax.rsqrt(jnp.mean(hb * hb, axis=-1, keepdims=True) + EPS)
        hb = hb * mlstm_norm[l].astype(f32).reshape(N_HEADS_B, HEAD_DIM_B)
        mix = jnp.concatenate([out_a, hb.reshape(B, S, W_B).astype(x.dtype)], axis=-1)
        x = x + mix @ w_out[l]

        hc = rmsnorm(x, norm_cross[l])
        hm = rmsnorm(mem, norm_mem[l])
        cq = (hc @ w_cq[l]).reshape(B, S, N_HEADS_X, HEAD_DIM_X)
        ck = (hm @ w_ck[l]).reshape(B, N_MEM, N_HEADS_X, HEAD_DIM_X)
        cv = (hm @ w_cv[l]).reshape(B, N_MEM, N_HEADS_X, HEAD_DIM_X)
        cs = jnp.einsum('bqhd,bkhd->bhqk', cq, ck).astype(f32) * (HEAD_DIM_X ** -0.5)
        cp = jax.nn.softmax(cs, axis=-1).astype(cv.dtype)
        co = jnp.einsum('bhqk,bkhd->bqhd', cp, cv).reshape(B, S, D_MODEL)
        x = x + co @ w_co[l]

        hz = rmsnorm(x, norm_moe[l]).reshape(T, D_MODEL)
        g_logits = (hz @ w_router_group[l]).astype(f32) + b_router_group[l].astype(f32)
        p_g = jax.nn.softmax(g_logits, axis=-1)
        g_prob, g_idx = lax.top_k(p_g, 1)
        e_logits = ((hz @ w_router_expert[l]).astype(f32) + b_router_expert[l].astype(f32))
        e_logits = e_logits.reshape(T, N_GROUPS, EXPERTS_PER_GROUP)
        e_in = jnp.take_along_axis(e_logits, g_idx[:, :, None], axis=1)[:, 0]
        p_e = jax.nn.softmax(e_in, axis=-1)
        w_top, e_idx = lax.top_k(p_e, TOP_K)
        gates = g_prob * (w_top / jnp.sum(w_top, axis=-1, keepdims=True))
        expert_ids = g_idx * EXPERTS_PER_GROUP + e_idx
        comb = jnp.sum(jax.nn.one_hot(expert_ids, N_EXPERTS, dtype=f32) * gates[..., None],
                       axis=1).astype(hz.dtype)
        y = jnp.zeros_like(hz)
        for e in range(N_EXPERTS):
            he = jax.nn.silu(hz @ w_exp_gate[l, e]) * (hz @ w_exp_up[l, e])
            y = y + comb[:, e:e + 1] * (he @ w_exp_down[l, e])
        x = x + y.reshape(B, S, D_MODEL)

    return rmsnorm(x, norm_final)


_drawn_inputs = setup_inputs


def setup_inputs(seed=0):
    import zlib

    import numpy as np

    out = dict(_drawn_inputs(seed))
    spreads = {}
    factors = {'attn_sinks': 8.0,
     'conv_b': 2.927,
     'gate_bias_i': 8.0,
     'norm_cross': 6.876,
     'norm_mem': 8.0,
     'b_router_group': 64.0,
     'b_router_expert': 24.576,
     'norm_final': 7.833,
     'norm_moe': 8.0}
    for name, (base, spread) in spreads.items():
        noise = np.random.default_rng([zlib.crc32(name.encode()), seed]).standard_normal(out[name].shape)
        drawn = base * np.exp(spread * noise) if base else spread * noise
        out[name] = __import__('jax').numpy.asarray(drawn.astype(out[name].dtype))
    for name, factor in factors.items():
        out[name] = (out[name] * factor).astype(out[name].dtype)
    return out
```

```python
from contextlib import ExitStack

import concourse.bass as bass
from concourse import mybir

F32 = mybir.dt.float32
I32 = mybir.dt.int32
ALU = mybir.AluOpType
ACT = mybir.ActivationFunctionType
AX_X = mybir.AxisListType.X

P = 128
T = 256
NT = T // P
D = 1024
KD = D // P
HA, KVA, DA = 8, 2, 64
HB, DB = 4, 128
HX, DX = 4, 256
CONV = 4
NG, EG = 4, 8
NE = NG * EG
FE = 512
SLOTS = 64
BLOCKS = T // SLOTS
NEG = -1e30
EPS = 1e-6
RING = 6
FRONT = 16

C_QA, C_KA, C_VA = 0, 512, 640
C_QB, C_KB, C_VB, C_OB, C_G = 768, 1280, 1792, 2304, 2816

K_ID, K_TRIU, K_STRICT, K_MTS, K_MST, K_ONES, K_SLOT, K_RG, K_RE = (
    0, 128, 256, 384, 512, 640, 768, 896, 900)
K_ALL = 932
R_MIX, R_CROSS, R_MEM, R_MOE, R_MLSTM, R_CW, R_CB, R_ALL = 0, 8, 16, 24, 32, 36, 68, 76
B_ALL = 8 + 8 + 36

ORDER_OF_JOBS = """
    dve rows xT0a xT0b xT1a xT1b gates    act U0    dve bcum    act U1 bias    dve R0 R1
    act U2    dve Mb0    act U3    dve Mb1    act U4 U5 U6    dve sA0a sA0b    act kct    dve sc0 sc1
    act U7    dve mT0a mT0b mT1a mT1b    act U8 U9    dve num0 den0    act tA0a tA0b U10
    dve Cst nst sA1a sA1b sA1c sA1d    act oA0    dve hb0T    act U11    dve num1 den1
    act U12 tA1a tA1b U13 tA1c tA1d    dve hb1T    act U14 oA1 U15    dve U19 U20 U21 U22 cT0a cT0b
    act U16    dve cT1a cT1b    act U23 U24 U25 U26 sX0a sX0b sX1a sX1b U17 U18 TX0 TX1 TX2 TX3
    oX0 oX1 oX2 oX3    dve U27 U28 U29 U30 zT0a zT0b zT1a zT1b logit pos"""


def list_jobs():
    turn, by, out = {True: 0, False: 0}, None, []
    for word in ORDER_OF_JOBS.split():
        if word in ("dve", "act"):
            by = word
            continue
        wide = word[0] in "UTx"
        bank = {"logit": 4, "pos": 5}.get(word, turn[wide] % 4 + (0 if wide else 4))
        turn[wide] += 1
        out.append((word, bank, by))
    return out


JOBS = list_jobs()


def job_table():
    seen, freed, last, out = {}, {}, {}, {}
    for name, bank, by in JOBS:
        out[name] = (bank, seen.get(bank, 0), last.get(bank))
        seen[bank] = seen.get(bank, 0) + 1
        freed[bank, by] = freed.get((bank, by), 0) + 1
        last[bank] = (by, freed[bank, by])
    return out, last


class Lane:

    def __init__(self, eng, chain):
        self.eng, self.chain, self.count, self.last = eng, chain, {}, None

    def did(self, ins, sem=None):
        sem = self.chain if sem is None else sem
        self.count[sem.name] = self.count.get(sem.name, 0) + 1
        ins.then_inc(sem, 1)
        self.last = (sem, self.count[sem.name])

    def settle(self):
        self.eng.wait_ge(*self.last)


def hymba_layer(nc, x, mem, rel_bias_table, w_in, w_out, w_cq, w_ck, w_cv, w_co, w_exp_gate, w_exp_up,
                w_exp_down, norm_final, vectors, biases, routers, const_tile, const_bands, out):
    jobs, last_of_bank = job_table()
    with ExitStack() as ctx:
        def sb(name, shape, dt=F32):
            return ctx.enter_context(nc.sbuf_tensor(name, shape, dt))

        def sem(name):
            return ctx.enter_context(nc.semaphore(name))

        ring = [sb(f"ring{i}", [P, 8, 512]) for i in range(RING)]
        arena = sb("arena", [P, 28300])
        used = [0]

        def take(n):
            used[0] += n
            assert used[0] <= 28300, used
            return arena[:, used[0] - n:used[0]]

        x_sb = take(2048).rearrange("p (t d) -> p t d", t=NT)
        xn_f = take(2048)
        xn = xn_f.rearrange("p (t d) -> p t d", t=NT)
        hT = take(2048).rearrange("p (k t) -> p k t", k=KD)
        hmT_f = take(2048)
        hmT = hmT_f.rearrange("p (k t) -> p k t", k=KD)
        u_f = take(2072)
        y_f = take(2048)
        T_f = take(2048)
        Z_f = take(2048)
        PT_f = take(2048)
        ckT_f = take(2048)
        ckT = ckT_f.rearrange("p (c t) -> p c t", c=8)
        cv = take(2048).rearrange("p (t d) -> p t d", t=NT)
        vb = take(1024).rearrange("p (t d) -> p t d", t=NT)
        ob = take(1024).rearrange("p (t d) -> p t d", t=NT)
        qaT = take(1024).rearrange("p (c t) -> p c t", c=4)
        kaT = take(256)
        va = take(256).rearrange("p (t d) -> p t d", t=NT)
        wg8 = take(64).rearrange("p (k c) -> p k c", k=KD)
        wr = take(8 * 36).rearrange("p (k c) -> p k c", k=KD)
        cst = take(K_ALL)
        vecs = take(R_ALL)
        tiny_f = take(400)

        mem_sb = PT_f.rearrange("p (t d) -> p t d", t=NT)
        rows = Z_f[0:R_ALL, 0:128]
        bands = Z_f[0:33, 128:512]
        table = Z_f[0:33, 512:520]
        bias_sb = Z_f[0:8, 520:904]
        silu_e = Z_f[:, 1024:2048]
        u = u_f.rearrange("p (c t) -> p c t", c=8)
        y = y_f.rearrange("p (c t) -> p c t", c=8)
        Tb = T_f.rearrange("p (h j) -> p h j", h=HA)
        Dg = [xn_f[:, 0:512], xn_f[:, 512:1024]]
        Rm = xn_f[:, 1024:1536]
        kct = xn_f[:, 1536:2048]
        Dm = [u_f[:, 0:512], u_f[:, 512:1024]]
        Pm = [u_f[:, 1024:1536], u_f[:, 1536:2048]]
        Cs = Rm
        aib = Dg[1]
        cqT = u_f[:, 0:2048].rearrange("p (c t) -> p c t", c=8)

        tiny_used = [0]

        def tiny(n):
            tiny_used[0] += n
            assert tiny_used[0] <= 400
            return tiny_f[:, tiny_used[0] - n:tiny_used[0]]

        ss, ms, rs = tiny(10), tiny(10), tiny(10)
        mhalf = tiny(8)
        small = tiny(B_ALL)
        gbias, sinks, rbias = small[:, 0:8], small[:, 8:16], small[:, 16:52]
        gl, az, lf = tiny(16), tiny(16), tiny(8)
        b_sb, bL, a_sb = tiny(8), tiny(4), tiny(8)
        M, mp1, w0 = tiny(8), tiny(4), tiny(4)
        em, dd, hss, hms, hrs = tiny(8), tiny(8), tiny(8), tiny(8), tiny(8)
        n_sb = tiny(4)
        amax, anm, asum, ask, ard = tiny(16), tiny(16), tiny(16), tiny(16), tiny(16)
        cmax, csum = tiny(8), tiny(8)

        def c3(ap, a):
            return ap.rearrange("p (a b) -> p a b", a=a)

        ident = cst[:, K_ID:K_ID + 128]
        ones = cst[:, K_ONES:K_ONES + 128]

        def over(ap, n):
            return ap.unsqueeze(2).to_broadcast([ap.shape[0], ap.shape[1], n])

        def again(ap, m):
            return ap.unsqueeze(1).to_broadcast([ap.shape[0], m, ap.shape[1]])

        bank = [ctx.enter_context(nc.psum_tensor(f"bank{i}", [P, 512], F32)) for i in range(8)]

        skew = nc.dram_tensor("skew_dram", [HA, P, 384], F32, kind="Internal").ap()

        s_x = [sem(f"s_x{t}") for t in range(NT)]
        s_mem, s_rows, s_cst, s_small = sem("s_mem"), sem("s_rows"), sem("s_cst"), sem("s_small")
        s_table = sem("s_table")
        s_wgates, s_router = sem("s_wgates"), sem("s_router")
        s_ring = [sem(f"s_ring{i}") for i in range(RING)]
        s_slot_used = sem("s_slot_used")
        s_filled = [sem(f"s_filled{i}") for i in range(8)]
        s_freed = {(i, e): sem(f"s_freed{i}_{e}") for i in range(8) for e in ("dve", "act")}
        s_skew, s_T = sem("s_skew"), sem("s_T")
        c_dve, c_act, c_pool, c_pe = sem("c_dve"), sem("c_act"), sem("c_pool"), sem("c_pe")
        s_mean, s_root = sem("s_mean"), sem("s_root")
        s_mhalf = sem("s_mhalf")
        s_xn, s_vecs, s_hT, s_memn, s_hmT = sem("s_xn"), sem("s_vecs"), sem("s_hT"), sem("s_memn"), sem("s_hmT")
        s_pad, s_table1 = sem("s_pad"), sem("s_table1")
        s_bias = sem("s_bias")
        s_unit = sem("s_unit")
        s_conv, s_silu_e, s_qk = sem("s_conv"), sem("s_silu_e"), sem("s_qk")
        s_az, s_l, s_logf = sem("s_az"), sem("s_l"), sem("s_logf")
        s_diag = sem("s_diag")
        s_dpre, s_D = sem("s_dpre"), sem("s_D")
        s_P = sem("s_P")
        s_kct, s_vw, s_q1, s_C = sem("s_kct"), sem("s_vw"), sem("s_q1"), sem("s_C")
        s_empre, s_em = sem("s_empre"), sem("s_em")
        s_sig, s_hb = sem("s_sig"), sem("s_hb")
        s_z, s_pe_a, s_pn = sem("s_z"), sem("s_pe_a"), sem("s_pn")
        s_pt, s_mixA, s_mixB = sem("s_pt"), sem("s_mixA"), sem("s_mixB")
        s_hc, s_cm, s_cp, s_cpn, s_cpt, s_co, s_x2 = (
            sem("s_hc"), sem("s_cm"), sem("s_cp"), sem("s_cpn"), sem("s_cpt"), sem("s_co"), sem("s_x2"))
        s_x1n, s_x2n, s_hz = sem("s_x1n"), sem("s_x2n"), sem("s_hz")
        s_out = sem("s_out")

        def filled(eng, name):
            b, before, _ = jobs[name]
            eng.wait_ge(s_filled[b], before + 1)
            return bank[b]

        def freed(name, by):
            assert (name, jobs[name][0], by) in JOBS
            return s_freed[jobs[name][0], by]

        def w_cols(w, c0, n):
            return w[0, :, c0:c0 + n].rearrange("(k p) n -> p k n", p=P)

        gain_f, O = T_f[:, 0:1024], T_f[:, 1024:2048]
        xe, gu = y_f[:, 0:1024].rearrange("p (k s) -> p k s", k=KD), [y_f[:, 1024:1536], y_f[:, 1536:2048]]
        E_f = [ckT_f[:, 0:256], ckT_f[:, 256:512]]
        hE = [ckT_f[:, 512:768], ckT_f[:, 768:1024]]
        ST = ckT_f[:, 1024:1280]
        Pg = ckT_f[:, 1280:1536].rearrange("p (t s) -> p t s", t=NT)
        Sg = ckT_f[:, 1536:1792].rearrange("p (t s) -> p t s", t=NT)
        posm = hmT_f[:, 0:256].rearrange("p (t n) -> p t n", t=NT)
        comb = hmT_f[:, 256:512].rearrange("p (t n) -> p t n", t=NT)
        at = [512]

        def r3(n):
            at[0] += 2 * n
            return hmT_f[:, at[0] - 2 * n:at[0]].rearrange("p (t n) -> p t n", t=NT)

        lg, gx, gq, ohg, el, eq, oh1, oh2, sel, posr = (
            r3(36), r3(4), r3(4), r3(4), r3(32), r3(32), r3(32), r3(32), r3(32), r3(32))
        gmax, gsum, mr, e1, e2, rr, g1, g2 = (r3(1) for _ in range(8))
        cnt = hmT_f[:, at[0]:at[0] + 32]
        cmaxf = hmT_f[:, at[0] + 32:at[0] + 33]
        cmaxi = sb("cmaxi", [P, 1], I32)
        zeros = vb.rearrange("p t d -> p (t d)")[:, 0:512]
        PAIRS = NE // 2

        s_zero = sem("s_zero")
        s_gain = sem("s_gain")
        s_logit_e, s_route, s_route_e, s_M, s_cnt = sem("s_logit_e"), sem("s_route"), sem("s_route_e"), sem("s_M"), sem("s_cnt")
        s_ydone = sem("s_ydone")
        s_outn = sem("s_outn")
        s_pg, s_sg = sem("s_pg"), sem("s_sg")
        s_gat, s_xe = sem("s_gat"), sem("s_xe")
        s_gu, s_gue = sem("s_gu"), sem("s_gue")
        s_t, s_ee, s_h = sem("s_t"), sem("s_ee"), sem("s_h")
        s_stt, s_st = sem("s_stt"), sem("s_st")
        s_down, s_o, s_comb = sem("s_down"), sem("s_o"), sem("s_comb")
        c_moe = [sem("c_moe_main"), sem("c_moe_more")]

        def sections(eng, one_pair, before=None, after=None):
            def section(i, g0, g1):
                if before:
                    before(i, g0)
                one_pair(i, g0, g0, first=True)
                with eng.Fori(g0 + 1, g1 - 1) as g:
                    one_pair(i, g0, g)
                one_pair(i, g0, g1 - 1, last=True)
                if after:
                    after(i, g1)

            section(0, 0, PAIRS)
            eng.wait_ge(s_cnt, 1)
            most = eng.value_load(cmaxi[0:1, 0:1], min_val=0, max_val=T)
            with eng.If(most > SLOTS):
                section(1, PAIRS, PAIRS * BLOCKS)

        def load_expert(sp, e, which, slot_i):
            w, k, n = ((w_exp_gate, 8, 512), (w_exp_up, 8, 512), (w_exp_down, 4, 1024))[which]
            src = w[0, bass.ds(e, 1)].rearrange("o (k p) n -> p (o k) n", p=P)
            dst = ring[slot_i][:, :, :].rearrange("p a b -> p (a b)").rearrange("p (k n) -> p k n", k=k)
            sp.dma_start(dst, src).then_inc(s_ring[slot_i], 16)

        def reached(eng, sem_, n):
            if not isinstance(n, int) or n > 0:
                eng.wait_ge(sem_, n)

        ORDER = ((0, 0), (0, 1), (1, 0), (1, 1), (0, 2), (1, 2))

        def moe_sync(sp):
            sp.wait_ge(s_x2, 1)
            sp.dma_start(gain_f, norm_final.partition_broadcast(P)).then_inc(s_gain, 16)

            def one_pair(G, pair, first=False):
                for j, (e, which) in enumerate(ORDER):
                    if first:
                        sp.wait_ge(s_slot_used, FRONT + j - RING + 1)
                    elif which < 2:
                        reached(sp, s_gu, 2 * G + e - 1)
                    else:
                        reached(sp, s_down, G)
                    load_expert(sp, 2 * pair + e, which, (FRONT + j) % RING)

            one_pair(0, 0, first=True)
            with sp.Fori(1, PAIRS) as pair:
                one_pair(pair, pair)
            sp.wait_ge(s_cnt, 1)
            with sp.If(sp.value_load(cmaxi[0:1, 0:1], min_val=0, max_val=T) > SLOTS):
                with sp.Fori(1, BLOCKS) as blk:
                    with sp.Fori(0, PAIRS) as pair:
                        one_pair(blk * PAIRS + pair, pair)
            for t in range(NT):
                sp.wait_ge(s_outn, t + 1)
                sp.dma_start(out[0, t * P:(t + 1) * P, :], xn[:, t, :]).then_inc(s_out, 16)
            sp.wait_ge(s_out, 32)

        def moe_act(act, lane):
            did, settle = lane.did, lane.settle
            act.wait_ge(s_route, 1)
            did(nc.scalar.activation(gq, gx, ACT.Exp), s_logit_e)
            act.wait_ge(s_route, 2)
            did(nc.scalar.activation(rr, rr, ACT.Exp), s_route_e)

            def one_pair(i, g0, G, first=False, last=False):
                for e in range(2):
                    n = 2 * G + e + 1
                    act.wait_ge(s_gu, n)
                    act.wait_ge(s_t, n)
                    nc.scalar.copy(gu[e], bank[6][:, :]).then_inc(s_gue, 1)
                    act.wait_ge(s_t, n + 2)
                    g_t = bank[7][:, :].rearrange("p (f s) -> p f s", f=4)[:, :, 0:64]
                    nc.scalar.activation(E_f[e].rearrange("p (f s) -> p f s", f=4), g_t, ACT.Exp, scale=-1.0).then_inc(s_ee, 1)
                reached(act, s_down, G + 1)
                reached(act, s_comb, G)
                nc.scalar.copy(O[:, 0:512], bank[4][:, :])
                nc.scalar.copy(O[:, 512:1024], bank[5][:, :]).then_inc(s_o, 1)

            sections(act, one_pair)

        def moe_pe(pe, open_job, close_job, transposes):
            pe.wait_ge(s_zero, 1)

            def clear_y(t):
                for i in (2 * t, 2 * t + 1):
                    before = last_of_bank[i]
                    pe.wait_ge(s_freed[i, before[0]], before[1])
                    nc.tensor.matmul(bank[i][:, :], zeros[:, 0:P], zeros, start=True, stop=True)

            for t in range(NT):
                pe.wait_ge(s_x2n, t + 1)
                for half in range(2):
                    transposes(f"zT{t}{'ab'[half]}", [xn[:, t, (4 * half + k) * P:(4 * half + k + 1) * P] for k in range(4)])
                if t == 0:
                    clear_y(0)
            pe.wait_ge(s_hz, 4)
            pe.wait_ge(s_router, 16)
            b = open_job("logit")
            for t in range(NT):
                for k in range(KD):
                    mm = nc.tensor.matmul(b[:, t * 36:(t + 1) * 36], hT[:, k, t * P:(t + 1) * P], wr[:, k, :],
                                          start=(k == 0), stop=(k == KD - 1))
            close_job("logit", mm)
            clear_y(1)
            pe.wait_ge(s_M, 1)
            b = open_job("pos")
            strict = cst[:, K_STRICT:K_STRICT + 128]
            nc.tensor.matmul(b[:, 0:32], strict, sel[:, 0, :], start=True, stop=True)
            nc.tensor.matmul(b[:, 32:64], ones, sel[:, 0, :], start=True, stop=False)
            nc.tensor.matmul(b[:, 32:64], strict, sel[:, 1, :], start=False, stop=True)
            nc.tensor.matmul(b[:, 64:96], ones, sel[:, 0, :], start=True, stop=False)
            close_job("pos", nc.tensor.matmul(b[:, 64:96], ones, sel[:, 1, :], start=False, stop=True))
            for i in (6, 7):
                before = last_of_bank[i]
                pe.wait_ge(s_freed[i, before[0]], before[1])
            for i in range(2):
                pe.nop().then_inc(s_t, 1)

            def expert_slot(G, j):
                q = FRONT + j
                pe.wait_ge(s_ring[q % RING], 16 * G + 16 * (q // RING + 1))
                return ring[q % RING]

            def gather(G):
                reached(pe, s_pg, G + 1)
                for k in range(KD):
                    for t in range(NT):
                        mm = nc.tensor.matmul(bank[4 + k // 4][:, (k % 4) * P:(k % 4 + 1) * P], xn[:, t, k * P:(k + 1) * P],
                                              Pg[:, t, :], start=(t == 0), stop=(t == NT - 1))
                mm.then_inc(s_gat, 1)

            def gate_up(G, e):
                w = [expert_slot(G, 2 * e), expert_slot(G, 2 * e + 1)]
                for k in range(KD):
                    for half in range(2):
                        mm = nc.tensor.matmul(bank[6][64 * half:64 * half + 64, :], xe[:, k, 64 * e:64 * e + 64], w[half][:, k, :],
                                              start=(k == 0), stop=(k == KD - 1))
                mm.then_inc(s_gu, 1)

            def turn(G, e):
                reached(pe, s_gue, 2 * G + e + 1)
                reached(pe, s_h, 2 * G + e)
                for f in range(4):
                    mm = nc.tensor.transpose(bank[7][:, f * P:(f + 1) * P], gu[e][:, f * P:(f + 1) * P], ident)
                mm.then_inc(s_t, 1)

            def combine(G):
                reached(pe, s_o, G + 1)
                reached(pe, s_st, G + 1)
                for t in range(NT):
                    for half in range(2):
                        mm = nc.tensor.matmul(bank[2 * t + half][:, :], ST[:, t * P:(t + 1) * P], O[:, half * 512:(half + 1) * 512],
                                              start=False, stop=False, skip_group_check=True)
                mm.then_inc(s_comb, 1)

            def before(i, g0):
                if i:
                    reached(pe, s_o, g0)
                else:
                    pe.wait_ge(s_cnt, 1)
                gather(g0)

            def one_pair(i, g0, G, first=False, last=False):
                reached(pe, s_xe, G + 1)
                reached(pe, s_st, G)
                gate_up(G, 0)
                if not last:
                    reached(pe, s_o, G)
                    gather(G + 1)
                turn(G, 0)
                gate_up(G, 1)
                turn(G, 1)
                reached(pe, s_sg, G + 1)
                for t in range(NT):
                    mm = nc.tensor.transpose(bank[6][:, t * P:(t + 1) * P], Sg[:, t, :], ident)
                mm.then_inc(s_stt, 1)
                if not first:
                    combine(G - 1)
                reached(pe, s_h, 2 * G + 2)
                if not last:
                    reached(pe, s_xe, G + 2)
                else:
                    reached(pe, s_o, G)
                w = [expert_slot(G, 4), expert_slot(G, 5)]
                for half in range(2):
                    for f in range(4):
                        for e in range(2):
                            wd = w[e][:, :, :].rearrange("p a b -> p (a b)")
                            lo = f * 1024 + half * 512
                            mm = nc.tensor.matmul(bank[4 + half][64 * e:64 * e + 64, :], hE[e][:, f * 64:(f + 1) * 64],
                                                  wd[:, lo:lo + 512], start=(f == 0), stop=(f == 3))
                mm.then_inc(s_down, 1)

            def after(i, g1):
                combine(g1 - 1)
                pe.wait_ge(s_comb, g1)

            sections(pe, one_pair, before, after)
            pe.nop().then_inc(s_ydone, 1)

        def moe_dve(dve, lane, rms_rows, to_feature_major):
            did, settle = lane.did, lane.settle
            V = nc.vector
            to_feature_major("zT", hT, R_MOE, s_hz)

            def tt(o, a, b, op, sem_=None):
                did(V.tensor_tensor(o, a, b, op), sem_)
                settle()

            def wide(ap, n):
                return ap.to_broadcast([P, NT, n])

            def first_of(values, top, ranks, onehot):
                n = values.shape[2]
                tt(onehot, values, wide(top, n), ALU.is_equal)
                tt(onehot, onehot, again(ranks, NT), ALU.mult)
                did(V.tensor_reduce(mr, onehot, AX_X, ALU.max))
                settle()
                tt(onehot, onehot, wide(mr, n), ALU.is_equal)

            ranks_g, ranks_e = cst[:, K_RG:K_RG + 4], cst[:, K_RE:K_RE + 32]
            b = filled(dve, "logit")
            did(V.tensor_tensor(lg, c3(b[:, 0:72], 2), again(rbias, NT), ALU.add), freed("logit", "dve"))
            settle()
            did(V.tensor_reduce(gmax, lg[:, :, 0:4], AX_X, ALU.max))
            settle()
            did(V.tensor_tensor(gx, lg[:, :, 0:4], wide(gmax, 4), ALU.subtract), s_route)
            first_of(lg[:, :, 0:4], gmax, ranks_g, ohg)
            did(V.tensor_scalar(ohg, ohg, 1.0, -NEG, ALU.subtract, ALU.mult))
            settle()
            for t in range(NT):
                did(V.tensor_tensor(c3(el[:, t, :], 4), c3(lg[:, t, 4:36], 4), over(ohg[:, t, :], EG), ALU.add))
            settle()
            did(V.tensor_reduce(e1, el, AX_X, ALU.max))
            settle()
            first_of(el, e1, ranks_e, oh1)
            did(V.scalar_tensor_tensor(eq, oh1, 2 * NEG, el, ALU.mult, ALU.add))
            settle()
            did(V.tensor_reduce(e2, eq, AX_X, ALU.max))
            settle()
            did(V.tensor_tensor(rr, e2, e1, ALU.subtract), s_route)
            first_of(eq, e2, ranks_e, oh2)
            tt(sel, oh1, oh2, ALU.add, s_M)
            dve.wait_ge(s_logit_e, 1)
            did(V.tensor_reduce(gsum, gq, AX_X, ALU.add))
            dve.wait_ge(s_route_e, 1)
            did(V.tensor_scalar(g1, rr, 1.0, None, ALU.add))
            settle()
            tt(g1, g1, gsum, ALU.mult)
            did(V.reciprocal(g1, g1))
            settle()
            tt(g2, g1, rr, ALU.mult)
            tt(oh1, oh1, wide(g1, 32), ALU.mult)
            tt(oh2, oh2, wide(g2, 32), ALU.mult)
            for blk in range(BLOCKS):
                did(V.tensor_tensor(comb[:, :, blk * NE:(blk + 1) * NE], oh1, oh2, ALU.add))
            b = filled(dve, "pos")
            did(V.tensor_reduce(cmaxf, b[:, 64:96], AX_X, ALU.max))
            did(V.scalar_tensor_tensor(posr, c3(b[:, 0:64], 2), 1.0, sel, ALU.add, ALU.mult))
            settle()
            for blk in range(BLOCKS):
                did(V.tensor_scalar(posm[:, :, blk * NE:(blk + 1) * NE], posr, -1.0 - blk * SLOTS, None, ALU.add))
            did(V.tensor_copy(cmaxi[:, :], cmaxf), s_cnt)
            settle()

            slots = cst[:, K_SLOT:K_SLOT + 64]

            def select(G):
                for e in range(2):
                    for t in range(NT):
                        ins = V.tensor_scalar(Pg[:, t, 64 * e:64 * e + 64], slots, posm[:, t, bass.ds(2 * G + e, 1)], None, ALU.is_equal)
                ins.then_inc(s_pg, 1)

            def evacuate_gathered(G):
                reached(dve, s_gat, G + 1)
                for half in range(2):
                    ins = V.tensor_tensor(xe[:, 4 * half:4 * half + 4, :], c3(bank[4 + half][:, :], 4),
                                          over(vecs[:, R_MOE + 4 * half:R_MOE + 4 * half + 4], P), ALU.mult)
                ins.then_inc(s_xe, 1)

            def before(i, g0):
                if i:
                    dve.wait_ge(s_gu, 2 * g0)
                    reached(dve, s_gat, g0)
                select(g0)
                evacuate_gathered(g0)

            PER = 6

            def one_pair(i, g0, G, first=False, last=False):
                step = [0]

                def chain(ins):
                    step[0] += 1
                    ins.then_inc(c_moe[i], 1)
                    dve.wait_ge(c_moe[i], PER * (G - g0) + step[0])

                if not last:
                    reached(dve, s_gat, G + 1)
                    select(G + 1)
                reached(dve, s_stt, G)
                for e in range(2):
                    for t in range(NT):
                        ins = V.tensor_scalar(Sg[:, t, 64 * e:64 * e + 64], slots, posm[:, t, bass.ds(2 * G + e, 1)],
                                              comb[:, t, bass.ds(2 * G + e, 1)], ALU.is_equal, ALU.mult)
                ins.then_inc(s_sg, 1)
                for e in range(2):
                    if e and not last:
                        reached(dve, s_gu, 2 * G + 2)
                        evacuate_gathered(G + 1)
                    reached(dve, s_ee, 2 * G + e + 1)
                    turned = bank[7][:, :].rearrange("p (f s) -> p f s", f=4)
                    E4 = E_f[e].rearrange("p (f s) -> p f s", f=4)
                    chain(V.tensor_scalar(E_f[e], E_f[e], 1.0, None, ALU.add))
                    chain(V.reciprocal(E_f[e], E_f[e]))
                    chain(V.tensor_tensor(E4, E4, turned[:, :, 0:64], ALU.mult))
                    reached(dve, s_down, G)
                    V.tensor_tensor(hE[e].rearrange("p (f s) -> p f s", f=4), E4, turned[:, :, 64:128], ALU.mult).then_inc(s_h, 1)
                reached(dve, s_stt, G + 1)
                reached(dve, s_comb, G)
                V.tensor_copy(ST, bank[6][:, 0:256]).then_inc(s_st, 1)
                assert step[0] == PER

            sections(dve, one_pair, before)
            dve.wait_ge(s_ydone, 1)

            def add_experts(t):
                for half in range(2):
                    xs = x_sb[:, t, half * 512:(half + 1) * 512]
                    did(V.tensor_tensor(xs, xs, bank[2 * t + half][:, :], ALU.add))
                settle()

            dve.wait_ge(s_gain, 16)
            rms_rows(x_sb, xn, 8, 9, s_outn, add_experts, gain_f)

        block = ctx.enter_context(nc.Block())

        @block.sync
        def _(sp):
            sp.dma_start(x_sb[:, 0, :], x[0, 0:P, :]).then_inc(s_x[0], 16)
            sp.dma_start(cst, const_tile).then_inc(s_cst, 16)
            sp.dma_start(x_sb[:, 1, :], x[0, P:T, :]).then_inc(s_x[1], 16)
            sp.dma_start(rows, vectors).then_inc(s_rows, 16)
            sp.dma_start(wg8, w_cols(w_in, C_G, 8)).then_inc(s_wgates, 16)
            sp.dma_start(small, biases.partition_broadcast(P)).then_inc(s_small, 16)
            front = [w_cols(w_in, C_QB, 512), w_cols(w_in, C_KB, 512), w_cols(w_in, C_QA, 512),
                     w_cols(w_in, C_KA, 256), w_cols(w_in, C_VB, 512), w_cols(w_in, C_OB, 512),
                     w_cols(w_ck, 0, 512), w_cols(w_ck, 512, 512), w_cols(w_cv, 0, 512),
                     w_cols(w_out, 0, 512), w_cols(w_out, 512, 512), w_cols(w_cq, 0, 512), w_cols(w_cq, 512, 512),
                     w_cols(w_cv, 512, 512), w_cols(w_co, 0, 512), w_cols(w_co, 512, 512)]
            assert len(front) == FRONT
            for q, src in enumerate(front):
                if q >= RING:
                    sp.wait_ge(s_slot_used, q - RING + 1)
                sp.dma_start(ring[q % RING][:, :, 0:src.shape[2]], src).then_inc(s_ring[q % RING], 16)
                if q == 0:
                    sp.wait_ge(s_table1, 1)
                    sp.dma_start(table[0:32, :], rel_bias_table).then_inc(s_table, 16)
                    sp.dma_start(bands, const_bands).then_inc(s_table, 16)
                    sp.dma_start(mem_sb, mem[0].rearrange("(t p) d -> p t d", p=P)).then_inc(s_mem, 16)
                if q == 3:
                    sp.dma_start(wr, routers.rearrange("(k p) c -> p k c", p=P)).then_inc(s_router, 16)
            moe_sync(sp)

        @block.scalar
        def _(act):
            lane = Lane(act, c_act)
            did, settle = lane.did, lane.settle
            act.wait_ge(s_az, 1)
            did(nc.scalar.activation(az[:, 8:16], az[:, 0:8], ACT.Exp, scale=-1.0))
            settle()
            did(nc.scalar.activation(az[:, 0:8], az[:, 8:16], ACT.Ln, bias=1.0), s_l)

            def unit(n, dst):
                b = filled(act, f"U{n}")
                did(nc.scalar.copy(dst, b[:, :].rearrange("p (a b) -> p a b", a=2) if len(dst.shape) == 3 else b[:, :]),
                    freed(f"U{n}", "act"))

            def unit_done():
                settle()
                did(act.nop(), s_unit)

            act.wait_ge(s_pad, 1)
            unit(0, u[:, 0:2, 3:259])
            unit(1, u[:, 2:4, 3:259])
            unit_done()
            bk = filled(act, "bias")
            did(nc.scalar.copy(bias_sb, bk[0:8, 0:384]), freed("bias", "act"))
            settle()
            act.dma_start(skew, bias_sb.unsqueeze(1).to_broadcast([8, P, 384])).then_inc(s_skew, 16)
            unit(2, u[:, 4:6, 3:259])
            act.wait_ge(s_conv, 1)
            did(nc.scalar.activation(silu_e, y_f[:, 0:1024], ACT.Exp, scale=-1.0), s_silu_e)
            act.wait_ge(s_dpre, 1)
            did(nc.scalar.activation(Dm[0], Dm[0], ACT.Exp), s_D)
            act.wait_ge(s_dpre, 2)
            did(nc.scalar.activation(w0, w0, ACT.Exp), s_D)
            unit(3, u[:, 6:8, 3:259])
            unit_done()
            act.wait_ge(s_skew, 16)
            act.dma_start(Tb, bass.AP(tensor=skew.tensor, offset=127,
                                      ap=[[383, P], [P * 384, HA], [1, 256]])).then_inc(s_T, 16)
            act.wait_ge(s_empre, 1)
            did(nc.scalar.activation(em, em, ACT.Exp, scale=-1.0), s_em)
            act.wait_ge(s_dpre, 3)
            did(nc.scalar.activation(Dm[1], Dm[1], ACT.Exp), s_D)
            act.wait_ge(s_dpre, 4)
            did(nc.scalar.activation(aib, aib, ACT.Exp), s_D)
            unit(4, qaT[:, 0:2, :])
            act.wait_ge(s_conv, 2)
            act.wait_ge(s_qk, 1)
            did(nc.scalar.activation(silu_e, y_f[:, 1024:2048], ACT.Exp, scale=-1.0), s_silu_e)
            unit(5, qaT[:, 2:4, :])
            b6 = filled(act, "U6")
            did(nc.scalar.copy(kaT, b6[:, 0:256]))
            did(nc.scalar.copy(va, b6[:, 256:512].rearrange("p (t d) -> p t d", t=NT)), freed("U6", "act"))
            unit_done()

            def attn_exp(t):
                act.wait_ge(s_z, t + 1)
                n = 128 if t == 0 else 256
                for h in range(HA):
                    zt = Z_f[:, h * n:(h + 1) * n]
                    did(nc.scalar.activation(zt, zt, ACT.Exp, bias=anm[:, 8 * t + h:8 * t + h + 1],
                                             accum_out=asum[:, 8 * t + h:8 * t + h + 1]))
                did(nc.scalar.activation(ask[:, 8 * t:8 * t + 8], ask[:, 8 * t:8 * t + 8], ACT.Exp), s_pe_a)

            b = filled(act, "kct")
            act.wait_ge(s_qk, 2)
            did(nc.scalar.copy(kct, b[:, :]), freed("kct", "act"))
            settle()
            did(act.nop(), s_kct)
            attn_exp(0)
            unit(7, vb[:, 0, :])
            unit(8, vb[:, 1, :])
            unit_done()

            def sigmoid_e(n, t):
                b = filled(act, f"U{n}")
                did(nc.scalar.activation(ob[:, t, :], b[:, :], ACT.Exp, scale=-1.0), freed(f"U{n}", "act"))
                settle()
                did(act.nop(), s_sig)

            sigmoid_e(9, 0)

            def pt_copy(name, dst):
                b = filled(act, name)
                did(nc.scalar.copy(dst, b[:, :]), freed(name, "act"))

            pt_copy("tA0a", PT_f[:, 0:512])
            pt_copy("tA0b", PT_f[:, 512:1024])
            settle()
            did(act.nop(), s_pt)
            sigmoid_e(10, 1)

            def mix_a(t):
                b = filled(act, f"oA{t}")
                did(nc.scalar.copy(hT[:, 0:4, t * P:(t + 1) * P], b[:, :].rearrange("p (c i) -> p c i", c=4)),
                    freed(f"oA{t}", "act"))
                settle()
                did(act.nop(), s_mixA)

            mix_a(0)
            unit(11, ckT[:, 0:2, :])
            attn_exp(1)
            unit(12, ckT[:, 2:4, :])
            pt_copy("tA1a", PT_f[:, 0:512])
            pt_copy("tA1b", PT_f[:, 512:1024])
            unit(13, ckT[:, 4:6, :])
            pt_copy("tA1c", PT_f[:, 1024:1536])
            pt_copy("tA1d", PT_f[:, 1536:2048])
            settle()
            did(act.nop(), s_pt)
            unit(14, ckT[:, 6:8, :])
            mix_a(1)
            unit(15, cv[:, 0, 0:512])
            unit(16, cv[:, 1, 0:512])
            for i in range(4):
                unit(23 + i, cqT[:, 2 * i:2 * i + 2, :])
            unit_done()
            for t in range(NT):
                for half in range(2):
                    act.wait_ge(s_cm, 2 * t + half + 1)
                    b = filled(act, f"sX{t}{'ab'[half]}")
                    for g in range(2):
                        h = 2 * half + g
                        ins = nc.scalar.activation(
                            Z_f[:, (t * 4 + h) * 256:(t * 4 + h + 1) * 256], b[:, g * 256:(g + 1) * 256], ACT.Exp,
                            bias=cmax[:, t * 4 + h:t * 4 + h + 1], scale=DX ** -0.5,
                            accum_out=csum[:, t * 4 + h:t * 4 + h + 1])
                        did(ins, freed(f"sX{t}{'ab'[half]}", "act") if g else None)
                settle()
                did(act.nop(), s_cp)
            unit(17, cv[:, 0, 512:1024])
            unit(18, cv[:, 1, 512:1024])
            unit_done()
            for i in range(4):
                pt_copy(f"TX{i}", PT_f[:, i * 512:(i + 1) * 512])
                settle()
                did(act.nop(), s_cpt)
            for i in range(4):
                b = filled(act, f"oX{i}")
                did(nc.scalar.copy(hT[:, 2 * i:2 * i + 2, :], b[:, :].rearrange("p (c i) -> p c i", c=2)),
                    freed(f"oX{i}", "act"))
            settle()
            did(act.nop(), s_co)
            moe_act(act, lane)

        @block.tensor
        def _(pe):
            def open_job(name):
                b, _, before = jobs[name]
                if before:
                    pe.wait_ge(s_freed[b, before[0]], before[1])
                return bank[b]

            def close_job(name, mm):
                mm.then_inc(s_filled[jobs[name][0]], 1)

            def slot(q):
                pe.wait_ge(s_ring[q % RING], 16 * (q // RING + 1))
                return ring[q % RING]

            def transposes(name, parts, n=128):
                b = open_job(name)
                for i, src in enumerate(parts):
                    mm = nc.tensor.transpose(b[:, i * n:(i + 1) * n], src, ident)
                close_job(name, mm)

            def unit_T(n, q, c0, src):
                w = slot(q)
                b = open_job(f"U{n}")
                for c in range(2):
                    for k in range(KD):
                        mm = nc.tensor.matmul(b[:, c * 256:(c + 1) * 256], w[:, k, c0 + c * 128:c0 + (c + 1) * 128],
                                              src[:, k, :], start=(k == 0), stop=(k == KD - 1))
                close_job(f"U{n}", mm)
                return mm

            def unit_N(n, q, t, src):
                w = slot(q)
                b = open_job(f"U{n}")
                for k in range(KD):
                    mm = nc.tensor.matmul(b[:, :], src[:, k, t * P:(t + 1) * P], w[:, k, :],
                                          start=(k == 0), stop=(k == KD - 1))
                close_job(f"U{n}", mm)

            def used_after(name, slots=1):
                b, before, _ = jobs[name]
                pe.wait_ge(s_filled[b], before + 1)
                for _ in range(slots):
                    pe.nop().then_inc(s_slot_used, 1)

            pe.wait_ge(s_cst, 16)
            pe.wait_ge(s_rows, 16)
            b = open_job("rows")
            close_job("rows", nc.tensor.transpose(b[:, 0:R_ALL], rows, ident[0:R_ALL, 0:R_ALL]))
            for t in range(NT):
                pe.wait_ge(s_xn, t + 1)
                for half in range(2):
                    transposes(f"xT{t}{'ab'[half]}", [xn[:, t, (4 * half + k) * P:(4 * half + k + 1) * P] for k in range(4)])
            pe.wait_ge(s_hT, 4)
            pe.wait_ge(s_wgates, 16)
            b = open_job("gates")
            for t in range(NT):
                for k in range(KD):
                    mm = nc.tensor.matmul(b[:, t * 8:(t + 1) * 8], hT[:, k, t * P:(t + 1) * P], wg8[:, k, :],
                                          start=(k == 0), stop=(k == KD - 1))
            close_job("gates", mm)

            def row_of(name, diag, n):
                pe.wait_ge(s_diag, n)
                b = open_job(name)
                close_job(name, nc.tensor.matmul(b[:, :], ones, diag, start=True, stop=True))

            unit_T(0, 0, 0, hT)
            pe.wait_ge(s_logf, 1)
            b = open_job("bcum")
            for t in range(NT):
                nc.tensor.matmul(b[:, t * 4:(t + 1) * 4], cst[:, K_TRIU:K_TRIU + 128], lf[:, t * 4:(t + 1) * 4],
                                 start=True, stop=True)
            close_job("bcum", nc.tensor.matmul(b[:, 8:12], ones, lf[:, 0:4], start=True, stop=True))
            unit_T(1, 0, 256, hT)
            used_after("U1")
            pe.wait_ge(s_table1, 1)
            pe.wait_ge(s_table, 32)
            b = open_job("bias")
            close_job("bias", nc.tensor.matmul(b[0:8, 0:384], table, bands, start=True, stop=True))
            row_of("R0", Dg[0], 1)
            row_of("R1", Dg[1], 2)
            unit_T(2, 1, 0, hT)
            row_of("Mb0", Dg[0], 3)
            unit_T(3, 1, 256, hT)
            used_after("U3")
            row_of("Mb1", Dg[1], 4)

            def unit_qa(n, c0):
                w = slot(2)
                b = open_job(f"U{n}")
                for c in range(2):
                    for k in range(KD):
                        for half in range(2):
                            h = 4 * half + c0 + c
                            mm = nc.tensor.matmul(b[64 * half:64 * half + 64, c * 256:(c + 1) * 256],
                                                  w[:, k, h * DA:(h + 1) * DA], hT[:, k, :],
                                                  start=(k == 0), stop=(k == KD - 1))
                close_job(f"U{n}", mm)

            unit_qa(4, 0)
            unit_qa(5, 2)
            used_after("U5")
            w = slot(3)
            b = open_job("U6")
            for k in range(KD):
                nc.tensor.matmul(b[:, 0:256], w[:, k, 0:128], hT[:, k, :], start=(k == 0), stop=(k == KD - 1))
            for t in range(NT):
                for k in range(KD):
                    mm = nc.tensor.matmul(b[:, 256 + t * P:256 + (t + 1) * P], hT[:, k, t * P:(t + 1) * P],
                                          w[:, k, 128:256], start=(k == 0), stop=(k == KD - 1))
            close_job("U6", mm)
            used_after("U6")
            pe.wait_ge(s_unit, 3)
            for g in range(2):
                name = f"sA0{'ab'[g]}"
                b = open_job(name)
                for c in range(4):
                    mm = nc.tensor.matmul(b[:, c * 128:(c + 1) * 128], qaT[64 * g:64 * g + 64, c, 0:P],
                                          kaT[64 * g:64 * g + 64, 0:P], start=True, stop=True)
                close_job(name, mm)

            def scores_b(t):
                b = open_job(f"sc{t}")
                for h in range(HB):
                    mm = nc.tensor.matmul(b[:, h * P:(h + 1) * P], y[:, 4 + h, t * P:(t + 1) * P],
                                          y[:, h, t * P:(t + 1) * P], start=True, stop=True)
                close_job(f"sc{t}", mm)

            pe.wait_ge(s_qk, 2)
            transposes("kct", [y[:, 4 + h, 0:P] for h in range(HB)])
            scores_b(0)
            scores_b(1)
            unit_N(7, 4, 0, hT)
            pe.wait_ge(s_memn, 1)
            for t in range(NT):
                for half in range(2):
                    transposes(f"mT{t}{'ab'[half]}", [mem_sb[:, t, (4 * half + k) * P:(4 * half + k + 1) * P] for k in range(4)])
            unit_N(8, 4, 1, hT)
            used_after("U8")
            unit_N(9, 5, 0, hT)

            def numerator(t):
                pe.wait_ge(s_P, t + 1)
                pe.wait_ge(s_unit, 4)
                if t:
                    pe.wait_ge(s_C, 1)
                    pe.wait_ge(s_q1, 1)
                b = open_job(f"num{t}")
                for h in range(HB):
                    mm = nc.tensor.matmul(b[:, h * P:(h + 1) * P], Pm[t][:, h * P:(h + 1) * P], vb[:, t, h * P:(h + 1) * P],
                                          start=True, stop=(t == 0))
                    if t:
                        mm = nc.tensor.matmul(b[:, h * P:(h + 1) * P], y[:, h, P:T], Cs[:, h * P:(h + 1) * P],
                                              start=False, stop=True)
                close_job(f"num{t}", mm)
                b = open_job(f"den{t}")
                for h in range(HB):
                    mm = nc.tensor.matmul(b[:, h:h + 1], Pm[t][:, h * P:(h + 1) * P], ones[:, 0:1],
                                          start=True, stop=(t == 0))
                    if t:
                        mm = nc.tensor.matmul(b[:, h:h + 1], y[:, h, P:T], n_sb[:, h:h + 1], start=False, stop=True)
                close_job(f"den{t}", mm)

            numerator(0)

            def p_transposes(names, per):
                for i, name in enumerate(names):
                    transposes(name, [Z_f[:, (4 * i + j) * P:(4 * i + j + 1) * P] for j in range(4)])

            pe.wait_ge(s_pn, 1)
            p_transposes(["tA0a", "tA0b"], 4)
            unit_N(10, 5, 1, hT)
            used_after("U10")
            pe.wait_ge(s_vw, 1)
            pe.wait_ge(s_kct, 1)
            b = open_job("Cst")
            for h in range(HB):
                mm = nc.tensor.matmul(b[:, h * P:(h + 1) * P], kct[:, h * P:(h + 1) * P], vb[:, 0, h * P:(h + 1) * P],
                                      start=True, stop=True)
            close_job("Cst", mm)
            b = open_job("nst")
            for h in range(HB):
                mm = nc.tensor.matmul(b[:, h:h + 1], kct[:, h * P:(h + 1) * P], w0[:, h:h + 1], start=True, stop=True)
            close_job("nst", mm)

            def scores_a1(i):
                name = f"sA1{'abcd'[i]}"
                b = open_job(name)
                for g in range(2):
                    h = 2 * i + g
                    lo = 64 * (h // 4)
                    mm = nc.tensor.matmul(b[:, g * 256:(g + 1) * 256], qaT[lo:lo + 64, h % 4, P:T], kaT[lo:lo + 64, :],
                                          start=True, stop=True)
                close_job(name, mm)

            def out_a(t):
                pe.wait_ge(s_pt, t + 1)
                b = open_job(f"oA{t}")
                for h in range(HA):
                    kv = h // 4
                    for j in range(t + 1):
                        blk = h if t == 0 else 2 * h + j
                        mm = nc.tensor.matmul(b[64 * (h % 2):64 * (h % 2) + 64, (h // 2) * P:(h // 2 + 1) * P],
                                              va[:, j, kv * DA:(kv + 1) * DA], PT_f[:, blk * P:(blk + 1) * P],
                                              start=(j == 0), stop=(j == t))
                close_job(f"oA{t}", mm)

            def mix_b(t):
                pe.wait_ge(s_hb, t + 1)
                transposes(f"hb{t}T", [ob[:, t, h * P:(h + 1) * P] for h in range(HB)])

            for i in range(4):
                scores_a1(i)
            out_a(0)
            mix_b(0)
            pe.wait_ge(s_hmT, 4)
            unit_T(11, 6, 0, hmT)
            numerator(1)
            unit_T(12, 6, 256, hmT)
            used_after("U12")
            pe.wait_ge(s_pn, 2)
            transposes("tA1a", [Z_f[:, j * P:(j + 1) * P] for j in range(4)])
            transposes("tA1b", [Z_f[:, (4 + j) * P:(5 + j) * P] for j in range(4)])
            unit_T(13, 7, 0, hmT)
            transposes("tA1c", [Z_f[:, (8 + j) * P:(9 + j) * P] for j in range(4)])
            transposes("tA1d", [Z_f[:, (12 + j) * P:(13 + j) * P] for j in range(4)])
            mix_b(1)
            unit_T(14, 7, 256, hmT)
            used_after("U14")
            out_a(1)
            unit_N(15, 8, 0, hmT)
            pe.wait_ge(s_mixA, 2)
            pe.wait_ge(s_mixB, 2)
            for i, (q, t) in enumerate(((9, 0), (10, 0), (9, 1), (10, 1))):
                unit_N(19 + i, q, t, hT)

            def c_transposes(t):
                pe.wait_ge(s_x1n, t + 1)
                for half in range(2):
                    transposes(f"cT{t}{'ab'[half]}", [xn[:, t, (4 * half + k) * P:(4 * half + k + 1) * P] for k in range(4)])

            c_transposes(0)
            unit_N(16, 8, 1, hmT)
            used_after("U16", 3)
            c_transposes(1)
            pe.wait_ge(s_hc, 4)
            for i, (q, c) in enumerate(((11, 0), (11, 256), (12, 0), (12, 256))):
                unit_T(23 + i, q, c, hT)
                if c:
                    used_after(f"U{23 + i}")
            pe.wait_ge(s_unit, 5)
            for t in range(NT):
                for half in range(2):
                    name = f"sX{t}{'ab'[half]}"
                    b = open_job(name)
                    for g in range(2):
                        h = 2 * half + g
                        for c in range(2):
                            mm = nc.tensor.matmul(b[:, g * 256:(g + 1) * 256], cqT[:, 2 * h + c, t * P:(t + 1) * P],
                                                  ckT[:, 2 * h + c, :], start=(c == 0), stop=(c == 1))
                    close_job(name, mm)
            unit_N(17, 13, 0, hmT)
            unit_N(18, 13, 1, hmT)
            used_after("U18")
            for i in range(4):
                j, hp = i % 2, i // 2
                if i == 0:
                    pe.wait_ge(s_cpn, 2)
                transposes(f"TX{i}", [Z_f[:, (t * 4 + 2 * hp + g) * 256 + j * P:(t * 4 + 2 * hp + g) * 256 + (j + 1) * P]
                                      for g in range(2) for t in range(NT)])
            pe.wait_ge(s_unit, 6)
            for h in range(HX):
                pe.wait_ge(s_cpt, 2 * (h // 2) + 2)
                name = f"oX{h}"
                b = open_job(name)
                for c in range(2):
                    for j in range(NT):
                        i = 2 * (h // 2) + j
                        mm = nc.tensor.matmul(b[:, c * 256:(c + 1) * 256], cv[:, j, h * DX + c * P:h * DX + (c + 1) * P],
                                              PT_f[:, i * 512 + (h % 2) * 256:i * 512 + (h % 2 + 1) * 256],
                                              start=(j == 0), stop=(j == NT - 1))
                close_job(name, mm)
            pe.wait_ge(s_co, 1)
            for i, (q, t) in enumerate(((14, 0), (15, 0), (14, 1), (15, 1))):
                unit_N(27 + i, q, t, hT)
                if t:
                    used_after(f"U{27 + i}")
            moe_pe(pe, open_job, close_job, transposes)

        @block.gpsimd
        def _(pool):
            nc.gpsimd.memset(mhalf, -0.5).then_inc(s_mhalf, 1)
            nc.gpsimd.memset(table, 1.0).then_inc(s_table1, 1)
            nc.gpsimd.memset(u[:, :, 0:3], 0.0).then_inc(s_pad, 1)
            pool.wait_ge(s_mhalf, 1)
            roots = [(ms, rs, 0, 1), (ms, rs, 1, 1), (ms, rs, 2, 2), (hms, hrs, 0, 4), (hms, hrs, 4, 4)]
            roots += [(ms, rs, i, 1) for i in range(4, 10)]
            for i, (src, dst, lo, n) in enumerate(roots):
                pool.wait_ge(s_mean, i + 1)
                nc.gpsimd.tensor_tensor(dst[:, lo:lo + n], src[:, lo:lo + n], mhalf[:, 0:n], ALU.pow).then_inc(s_root, 1)

        @block.vector
        def _(dve):
            lane = Lane(dve, c_dve)
            did, settle = lane.did, lane.settle
            V = nc.vector

            def rms_rows(src, dst, lo, roots_before, data_sem, ready, gain=None):
                for t in range(NT):
                    ready(t)
                    did(V.tensor_tensor_reduce(dst[:, t, :], src[:, t, :], src[:, t, :], 1.0, 0.0, ALU.mult, ALU.add,
                                               ss[:, lo + t:lo + t + 1]))
                    settle()
                    did(V.tensor_scalar(ms[:, lo + t:lo + t + 1], ss[:, lo + t:lo + t + 1], 1.0 / D, EPS, ALU.mult, ALU.add), s_mean)
                    dve.wait_ge(s_root, roots_before + t + 1)
                    if gain is None:
                        did(V.tensor_scalar(dst[:, t, :], src[:, t, :], rs[:, lo + t:lo + t + 1], None, ALU.mult), data_sem)
                    else:
                        did(V.scalar_tensor_tensor(dst[:, t, :], src[:, t, :], rs[:, lo + t:lo + t + 1], gain, ALU.mult, ALU.mult),
                            data_sem)

            def to_feature_major(names, dst, r, data_sem):
                for t in range(NT):
                    for half in range(2):
                        name = names + f"{t}{'ab'[half]}"
                        b = filled(dve, name)
                        did(V.tensor_tensor(dst[:, 4 * half:4 * half + 4, t * P:(t + 1) * P], c3(b[:, :], 4),
                                            over(vecs[:, r + 4 * half:r + 4 * half + 4], P), ALU.mult), freed(name, "dve"))
                        settle()
                        did(dve.nop(), data_sem)

            rms_rows(x_sb, xn, 0, 0, s_xn, lambda t: dve.wait_ge(s_x[t], 16))
            b = filled(dve, "rows")
            did(V.tensor_copy(vecs, b[:, 0:R_ALL]), freed("rows", "dve"))
            settle()
            to_feature_major("xT", hT, R_MIX, s_hT)
            dve.wait_ge(s_small, 16)
            b = filled(dve, "gates")
            did(V.tensor_tensor(c3(gl, 2), c3(b[:, 0:16], 2), again(gbias, 2), ALU.add), freed("gates", "dve"))
            settle()
            did(V.scalar_tensor_tensor(c3(az[:, 0:8], 2), c3(gl, 2)[:, :, 4:8], -1.0, c3(gl, 2)[:, :, 4:8], ALU.mult, ALU.max), s_az)
            dve.wait_ge(s_l, 1)
            did(V.scalar_tensor_tensor(c3(lf, 2), c3(gl, 2)[:, :, 4:8], 0.0, c3(az[:, 0:8], 2), ALU.min, ALU.subtract), s_logf)
            b = filled(dve, "bcum")
            did(V.tensor_copy(b_sb, b[:, 0:8]))
            did(V.tensor_copy(bL, b[:, 8:12]), freed("bcum", "dve"))
            settle()
            did(V.tensor_tensor(c3(a_sb, 2), c3(gl, 2)[:, :, 0:4], c3(b_sb, 2), ALU.subtract))
            settle()
            for t in range(NT):
                did(V.tensor_tensor(c3(Dg[t], 4), again(ident, 4), over(a_sb[:, 4 * t:4 * t + 4], P), ALU.mult), s_diag)
            dve.wait_ge(s_mem, 16)
            for t in range(NT):
                did(V.tensor_tensor_reduce(Z_f[:, 1024:2048], mem_sb[:, t, :], mem_sb[:, t, :], 1.0, 0.0, ALU.mult, ALU.add,
                                           ss[:, 2 + t:3 + t]))
                settle()
            did(V.tensor_scalar(ms[:, 2:4], ss[:, 2:4], 1.0 / D, EPS, ALU.mult, ALU.add), s_mean)
            dve.wait_ge(s_root, 3)
            for t in range(NT):
                did(V.tensor_scalar(mem_sb[:, t, :], mem_sb[:, t, :], rs[:, 2 + t:3 + t], None, ALU.mult))
            settle()
            did(dve.nop(), s_memn)

            def conv(c0, n):
                dve.wait_ge(s_unit, n)
                for c in range(c0, c0 + 4):
                    did(V.tensor_scalar(y[:, c, :], u[:, c, 0:256], vecs[:, R_CW + c:R_CW + c + 1],
                                        vecs[:, R_CB + c:R_CB + c + 1], ALU.mult, ALU.add))
                for w in range(1, CONV):
                    settle()
                    for c in range(c0, c0 + 4):
                        did(V.scalar_tensor_tensor(y[:, c, :], u[:, c, w:w + 256],
                                                   vecs[:, R_CW + 8 * w + c:R_CW + 8 * w + c + 1], y[:, c, :],
                                                   ALU.mult, ALU.add))
                settle()
                did(dve.nop(), s_conv)

            def silu(c0, n, scale):
                yy = y_f[:, c0 * 256:(c0 + 4) * 256]
                dve.wait_ge(s_silu_e, n)
                did(V.tensor_scalar(silu_e, silu_e, 1.0, None, ALU.add))
                settle()
                did(V.reciprocal(silu_e, silu_e))
                settle()
                did(V.scalar_tensor_tensor(yy, yy, scale, silu_e, ALU.mult, ALU.mult))
                settle()
                did(dve.nop(), s_qk)

            def row_max(t):
                b = filled(dve, f"R{t}")
                did(V.tensor_tensor(c3(Rm, 4), c3(b[:, :], 4), again(cst[:, K_MTS:K_MTS + 128], 4), ALU.add), freed(f"R{t}", "dve"))
                settle()
                did(V.tensor_reduce(M[:, 4 * t:4 * t + 4], c3(Rm, 4), AX_X, ALU.max))
                settle()

            row_max(0)
            did(V.tensor_scalar(M[:, 0:4], M[:, 0:4], 0.0, None, ALU.max))
            settle()
            did(V.tensor_tensor(c3(Dg[0], 4), again(ident, 4), over(M[:, 0:4], P), ALU.mult), s_diag)
            row_max(1)
            conv(0, 1)
            def decay_pre(t):
                b = filled(dve, f"Mb{t}")
                did(V.scalar_tensor_tensor(c3(Dm[t], 4), c3(b[:, :], 4), -1.0, again(cst[:, K_MST:K_MST + 128], 4),
                                           ALU.mult, ALU.add))
                settle()
                did(V.tensor_tensor(c3(Dm[t], 4), c3(Dm[t], 4), over(a_sb[:, 4 * t:4 * t + 4], P), ALU.add), s_dpre)
                return b

            b = decay_pre(0)
            mlast = c3(b[:, :], 4)[:, :, 127]
            did(V.tensor_tensor(w0, a_sb[:, 0:4], mlast, ALU.subtract), s_dpre)
            did(V.tensor_tensor(mp1, bL, mlast, ALU.add), freed("Mb0", "dve"))
            settle()
            did(V.tensor_tensor(M[:, 4:8], M[:, 4:8], mp1, ALU.max))
            settle()
            did(V.tensor_tensor(c3(Dg[1], 4), again(ident, 4), over(M[:, 4:8], P), ALU.mult), s_diag)
            did(V.tensor_tensor(em, b_sb, M, ALU.add), s_empre)
            silu(0, 1, DB ** -0.5)
            b = decay_pre(1)
            did(V.scalar_tensor_tensor(c3(aib, 4), c3(b[:, :], 4), -1.0, over(mp1, P), ALU.mult, ALU.add), freed("Mb1", "dve"))
            settle()
            did(dve.nop(), s_dpre)
            conv(4, 2)
            silu(4, 2, 1.0)

            def attn_z(name, lo, n, heads):
                b = filled(dve, name)
                did(V.scalar_tensor_tensor(Z_f[:, lo:lo + 512].rearrange("p (h j) -> p h j", j=n), b[:, :].rearrange("p (h j) -> p h j", j=n),
                                           DA ** -0.5, Tb[:, heads:heads + 512 // n, 256 - n:256], ALU.mult, ALU.add), freed(name, "dve"))

            def attn_max(t, n):
                settle()
                o = 8 * t
                did(V.tensor_reduce(amax[:, o:o + 8], Z_f[:, 0:8 * n].rearrange("p (h j) -> p h j", j=n), AX_X, ALU.max))
                settle()
                did(V.tensor_tensor(amax[:, o:o + 8], amax[:, o:o + 8], sinks, ALU.max))
                settle()
                did(V.tensor_scalar(anm[:, o:o + 8], amax[:, o:o + 8], -1.0, None, ALU.mult))
                did(V.tensor_tensor(ask[:, o:o + 8], sinks, amax[:, o:o + 8], ALU.subtract))
                settle()
                did(dve.nop(), s_z)

            def attn_normalise(t, n):
                dve.wait_ge(s_pe_a, t + 1)
                o = 8 * t
                did(V.tensor_tensor(ard[:, o:o + 8], asum[:, o:o + 8], ask[:, o:o + 8], ALU.add))
                settle()
                did(V.reciprocal(ard[:, o:o + 8], ard[:, o:o + 8]))
                settle()
                z = Z_f[:, 0:8 * n].rearrange("p (h j) -> p h j", j=n)
                did(V.tensor_tensor(z, z, over(ard[:, o:o + 8], n), ALU.mult))
                settle()
                did(dve.nop(), s_pn)

            dve.wait_ge(s_T, 16)
            attn_z("sA0a", 0, 128, 0)
            attn_z("sA0b", 512, 128, 4)
            attn_max(0, 128)

            def weights_b(t, n):
                dve.wait_ge(s_D, n)
                b = filled(dve, f"sc{t}")
                did(V.tensor_tensor(Pm[t], b[:, :], Dm[t], ALU.mult), freed(f"sc{t}", "dve"))
                settle()
                did(dve.nop(), s_P)

            weights_b(0, 1)
            weights_b(1, 3)
            dve.wait_ge(s_D, 4)
            q1 = y[:, 0:4, P:T]
            did(V.tensor_tensor(q1, q1, c3(aib, 4), ALU.mult), s_q1)
            to_feature_major("mT", hmT, R_MEM, s_hmT)
            attn_normalise(0, 128)

            b0 = filled(dve, "num0")
            did(V.tensor_tensor(c3(vb[:, 0, :], 4), c3(vb[:, 0, :], 4), over(w0, P), ALU.mult), s_vw)

            def head_out(t, sig_done):
                o = ob[:, t, :]
                dve.wait_ge(s_sig, t + 1)
                did(V.tensor_scalar(o, o, 1.0, None, ALU.add))
                settle()
                did(V.reciprocal(o, o))
                nb = filled(dve, f"num{t}")
                db = filled(dve, f"den{t}")
                dve.wait_ge(s_em, 1)
                h4 = slice(4 * t, 4 * t + 4)
                did(V.tensor_copy(dd[:, h4], db[:, 0:4]), freed(f"den{t}", "dve"))
                settle()
                did(V.scalar_tensor_tensor(dd[:, h4], dd[:, h4], -1.0, dd[:, h4], ALU.mult, ALU.max))
                settle()
                did(V.tensor_tensor(dd[:, h4], dd[:, h4], em[:, h4], ALU.max))
                settle()
                did(V.reciprocal(dd[:, h4], dd[:, h4]))
                settle()
                did(V.tensor_tensor(c3(o, 4), c3(o, 4), over(dd[:, h4], P), ALU.mult))
                settle()
                did(V.tensor_tensor(o, o, nb[:, :], ALU.mult), freed(f"num{t}", "dve"))
                settle()
                did(V.tensor_tensor(Dg[0], o, o, ALU.mult))
                settle()
                did(V.tensor_reduce(hss[:, h4], c3(Dg[0], 4), AX_X, ALU.add))
                settle()
                did(V.tensor_scalar(hms[:, h4], hss[:, h4], 1.0 / DB, EPS, ALU.mult, ALU.add), s_mean)
                dve.wait_ge(s_root, 4 + t)
                did(V.tensor_tensor(c3(o, 4), c3(o, 4), over(hrs[:, h4], P), ALU.mult), s_hb)

            head_out(0, 1)
            b = filled(dve, "Cst")
            did(V.tensor_copy(Cs, b[:, :]), freed("Cst", "dve"))
            b = filled(dve, "nst")
            did(V.tensor_copy(n_sb, b[:, 0:4]), freed("nst", "dve"))
            settle()
            did(dve.nop(), s_C)
            dve.wait_ge(s_filled[jobs["tA0b"][0]], jobs["tA0b"][1] + 1)
            attn_z("sA1a", 0, 256, 0)
            attn_z("sA1b", 512, 256, 2)
            attn_z("sA1c", 1024, 256, 4)
            attn_z("sA1d", 1536, 256, 6)
            attn_max(1, 256)

            def mix_b(t):
                name = f"hb{t}T"
                b = filled(dve, name)
                did(V.tensor_tensor(hT[:, 4:8, t * P:(t + 1) * P], c3(b[:, :], 4), over(vecs[:, R_MLSTM:R_MLSTM + 4], P),
                                    ALU.mult), freed(name, "dve"))
                settle()
                did(dve.nop(), s_mixB)

            mix_b(0)
            attn_normalise(1, 256)
            head_out(1, 2)
            mix_b(1)
            did(V.memset(zeros, 0.0), s_zero)

            def residual(n0, t):
                for half in range(2):
                    name = f"U{n0 + 2 * t + half}"
                    b = filled(dve, name)
                    xs = x_sb[:, t, half * 512:(half + 1) * 512]
                    did(V.tensor_tensor(xs, xs, b[:, :], ALU.add), freed(name, "dve"))
                settle()

            rms_rows(x_sb, xn, 4, 5, s_x1n, lambda t: residual(19, t))
            to_feature_major("cT", hT, R_CROSS, s_hc)
            for t in range(NT):
                for half in range(2):
                    b = filled(dve, f"sX{t}{'ab'[half]}")
                    o = slice(t * 4 + 2 * half, t * 4 + 2 * half + 2)
                    did(V.tensor_reduce(cmax[:, o], c3(b[:, :], 2), AX_X, ALU.max))
                    settle()
                    did(V.tensor_scalar(cmax[:, o], cmax[:, o], -DX ** -0.5, None, ALU.mult), s_cm)
            for t in range(NT):
                dve.wait_ge(s_cp, t + 1)
                o = slice(t * 4, t * 4 + 4)
                did(V.reciprocal(csum[:, o], csum[:, o]))
                settle()
                z = Z_f[:, t * 1024:(t + 1) * 1024].rearrange("p (h j) -> p h j", h=HX)
                did(V.tensor_tensor(z, z, over(csum[:, o], 256), ALU.mult), s_cpn)
            rms_rows(x_sb, xn, 6, 7, s_x2n, lambda t: residual(27, t))
            did(dve.nop(), s_x2)
            moe_dve(dve, lane, rms_rows, to_feature_major)


_INS = ["x", "mem", "rel_bias_table", "w_in", "w_out", "w_cq", "w_ck", "w_cv", "w_co",
        "w_exp_gate", "w_exp_up", "w_exp_down", "norm_final"]


def constants():
    import math
    import numpy as np

    i, j = np.arange(P)[:, None], np.arange(P)[None, :]
    c = np.zeros((P, K_ALL), np.float32)
    c[:, K_ID:K_ID + 128] = i == j
    c[:, K_TRIU:K_TRIU + 128] = i <= j
    c[:, K_STRICT:K_STRICT + 128] = i < j
    c[:, K_MTS:K_MTS + 128] = np.where(j <= i, 0.0, NEG)
    c[:, K_MST:K_MST + 128] = np.where(i <= j, 0.0, NEG)
    c[:, K_ONES:K_ONES + 128] = 1.0
    c[:, K_SLOT:K_SLOT + 128] = j % SLOTS
    c[:, K_RG:K_RG + 4] = NG - np.arange(NG)
    c[:, K_RE:K_RE + 32] = NE - np.arange(NE)
    bands = np.zeros((33, 384), np.float32)
    for m in range(384):
        n = 255 - m
        if 0 <= n < 128:
            big = 16 + int(np.float32(np.log(np.float32(max(n, 1)) / np.float32(16))) / np.float32(math.log(8.0)) * np.float32(16))
            bands[n if n < 16 else min(big, 31), m] = 1.0
        else:
            bands[32, m] = NEG
    return c, bands


def kernel(**inputs):
    import numpy as _np
    import concourse.bacc as _bacc
    from concourse import mybir as _mybir
    from concourse.bass_utils import run_bass_kernel_spmd as _run

    nc = _bacc.Bacc("TRN2", target_bir_lowering=False, num_devices=1)
    arrays, args = {}, []
    flat = {name: _np.asarray(inputs[name]).reshape(-1) for name in inputs}
    groups = {
        "vectors": _np.concatenate([flat[n] for n in ("norm_mix", "norm_cross", "norm_mem", "norm_moe", "mlstm_norm",
                                                      "conv_w", "conv_b")]).reshape(R_ALL, P),
        "biases": _np.concatenate([flat[n] for n in ("gate_bias_i", "gate_bias_f", "attn_sinks", "b_router_group",
                                                     "b_router_expert")]),
        "routers": _np.concatenate([_np.asarray(inputs["w_router_group"])[0], _np.asarray(inputs["w_router_expert"])[0]], axis=1),
    }
    for name in [*_INS, *groups]:
        a = _np.ascontiguousarray(groups[name] if name in groups else inputs[name])
        arrays[f"in_{name}_dram"] = a
        args.append(nc.dram_tensor(f"in_{name}_dram", a.shape, _mybir.dt.from_np(a.dtype), kind="ExternalInput").ap())
    for name, a in zip(("tile", "bands"), constants()):
        arrays[f"const_{name}_dram"] = a
        args.append(nc.dram_tensor(f"const_{name}_dram", a.shape, _mybir.dt.from_np(a.dtype), kind="ExternalInput").ap())
    args.append(nc.dram_tensor("out_0_dram", (1, T, D), _mybir.dt.from_np(_np.dtype("float32")), kind="ExternalOutput").ap())
    hymba_layer(nc, *args)
    r = _run(nc, [arrays], core_ids=[0])
    return r.results[0]["out_0_dram"]
```

```python
from contextlib import ExitStack

import concourse.bass as bass
from concourse import mybir

F32 = mybir.dt.float32
I32 = mybir.dt.int32
ALU = mybir.AluOpType
ACT = mybir.ActivationFunctionType
AX_X = mybir.AxisListType.X

P = 128
T = 256
NT = T // P
D = 1024
KD = D // P
HA, KVA, DA = 8, 2, 64
HB, DB = 4, 128
HX, DX = 4, 256
CONV = 4
NG, EG = 4, 8
NE = NG * EG
FE = 512
SLOTS = 64
BLOCKS = T // SLOTS
NEG = -1e30
EPS = 1e-6
RING = 6
FRONT = 16

C_QA, C_KA, C_VA = 0, 512, 640
C_QB, C_KB, C_VB, C_OB, C_G = 768, 1280, 1792, 2304, 2816

K_ID, K_TRIU, K_STRICT, K_MTS, K_MST, K_ONES, K_SLOT, K_RG, K_RE = (
    0, 128, 256, 384, 512, 640, 768, 896, 900)
K_ALL = 932
R_MIX, R_CROSS, R_MEM, R_MOE, R_MLSTM, R_CW, R_CB, R_ALL = 0, 8, 16, 24, 32, 36, 68, 76
B_ALL = 8 + 8 + 36

ORDER_OF_JOBS = """
    dve rows xT0a xT0b xT1a xT1b gates    act U0    dve bcum    act U1 bias    dve R0 R1
    act U2    dve Mb0    act U3    dve Mb1    act U4 U5 U6    dve sA0a sA0b    act kct    dve sc0 sc1
    act U7    dve mT0a mT0b mT1a mT1b    act U8 U9    dve num0 den0    act tA0a tA0b U10
    dve Cst nst sA1a sA1b sA1c sA1d    act oA0    dve hb0T    act U11    dve num1 den1
    act U12 tA1a tA1b U13 tA1c tA1d    dve hb1T    act U14 oA1 U15    dve U19 U20 U21 U22 cT0a cT0b
    act U16    dve cT1a cT1b    act U23 U24 U25 U26 sX0a sX0b sX1a sX1b U17 U18 TX0 TX1 TX2 TX3
    oX0 oX1 oX2 oX3    dve U27 U28 U29 U30 zT0a zT0b zT1a zT1b logit pos"""


def list_jobs():
    turn, by, out = {True: 0, False: 0}, None, []
    for word in ORDER_OF_JOBS.split():
        if word in ("dve", "act"):
            by = word
            continue
        wide = word[0] in "UTx"
        bank = {"logit": 4, "pos": 5}.get(word, turn[wide] % 4 + (0 if wide else 4))
        turn[wide] += 1
        out.append((word, bank, by))
    return out


JOBS = list_jobs()


def job_table():
    seen, freed, last, out = {}, {}, {}, {}
    for name, bank, by in JOBS:
        out[name] = (bank, seen.get(bank, 0), last.get(bank))
        seen[bank] = seen.get(bank, 0) + 1
        freed[bank, by] = freed.get((bank, by), 0) + 1
        last[bank] = (by, freed[bank, by])
    return out, last


class Lane:

    def __init__(self, eng, chain):
        self.eng, self.chain, self.count, self.last = eng, chain, {}, None

    def did(self, ins, sem=None):
        sem = self.chain if sem is None else sem
        self.count[sem.name] = self.count.get(sem.name, 0) + 1
        ins.then_inc(sem, 1)
        self.last = (sem, self.count[sem.name])

    def settle(self):
        self.eng.wait_ge(*self.last)


def hymba_layer(nc, x, mem, rel_bias_table, w_in, w_out, w_cq, w_ck, w_cv, w_co, w_exp_gate, w_exp_up,
                w_exp_down, norm_final, vectors, biases, routers, const_tile, const_bands, out):
    jobs, last_of_bank = job_table()
    with ExitStack() as ctx:
        def sb(name, shape, dt=F32):
            return ctx.enter_context(nc.sbuf_tensor(name, shape, dt))

        def sem(name):
            return ctx.enter_context(nc.semaphore(name))

        ring = [sb(f"ring{i}", [P, 8, 512]) for i in range(RING)]
        arena = sb("arena", [P, 28300])
        used = [0]

        def take(n):
            used[0] += n
            assert used[0] <= 28300, used
            return arena[:, used[0] - n:used[0]]

        x_sb = take(2048).rearrange("p (t d) -> p t d", t=NT)
        xn_f = take(2048)
        xn = xn_f.rearrange("p (t d) -> p t d", t=NT)
        hT = take(2048).rearrange("p (k t) -> p k t", k=KD)
        yT_f = take(4096)
        y_f, T_f = yT_f[:, 0:2048], yT_f[:, 2048:4096]
        hvo_f = take(4096)
        hmT = hvo_f[:, 0:2048].rearrange("p (k t) -> p k t", k=KD)
        vb = hvo_f[:, 2048:3072].rearrange("p (t d) -> p t d", t=NT)
        ob = hvo_f[:, 3072:4096].rearrange("p (t d) -> p t d", t=NT)
        uck_f = take(2072 + 2048)
        u_f, ckT_f = uck_f[:, 0:2072], uck_f[:, 2072:4120]
        ckT = ckT_f.rearrange("p (c t) -> p c t", c=8)
        zp_f = take(4096)
        Z_f, PT_f = zp_f[:, 0:2048], zp_f[:, 2048:4096]
        cv_f = take(2048)
        cv = cv_f.rearrange("p (t d) -> p t d", t=NT)
        qkv_f = take(1024 + 256 + 256)
        qaT = qkv_f[:, 0:1024].rearrange("p (c t) -> p c t", c=4)
        kaT = qkv_f[:, 1024:1280]
        va = qkv_f[:, 1280:1536].rearrange("p (t d) -> p t d", t=NT)
        wg8 = take(64).rearrange("p (k c) -> p k c", k=KD)
        wr = take(8 * 36).rearrange("p (k c) -> p k c", k=KD)
        cst = take(K_ALL)
        vecs = take(R_ALL)
        tiny_f = take(400)

        mem_sb = PT_f.rearrange("p (t d) -> p t d", t=NT)
        rows = Z_f[0:R_ALL, 0:128]
        bands = Z_f[0:33, 128:512]
        table = Z_f[0:33, 512:520]
        bias_sb = Z_f[0:8, 520:904]
        silu_e = Z_f[:, 1024:2048]
        u = u_f.rearrange("p (c t) -> p c t", c=8)
        y = y_f.rearrange("p (c t) -> p c t", c=8)
        Tb = T_f.rearrange("p (h j) -> p h j", h=HA)
        Dg = [xn_f[:, 0:512], xn_f[:, 512:1024]]
        Rm = xn_f[:, 1024:1536]
        kct = xn_f[:, 1536:2048]
        Dm = [u_f[:, 0:512], u_f[:, 512:1024]]
        Pm = [u_f[:, 1024:1536], u_f[:, 1536:2048]]
        Cs = Rm
        aib = Dg[1]
        cqT = u_f[:, 0:2048].rearrange("p (c t) -> p c t", c=8)

        tiny_used = [0]

        def tiny(n):
            tiny_used[0] += n
            assert tiny_used[0] <= 400
            return tiny_f[:, tiny_used[0] - n:tiny_used[0]]

        ss, ms, rs = tiny(10), tiny(10), tiny(10)
        mhalf = tiny(8)
        small = tiny(B_ALL)
        gbias, sinks, rbias = small[:, 0:8], small[:, 8:16], small[:, 16:52]
        gl, az, lf = tiny(16), tiny(16), tiny(8)
        b_sb, bL, a_sb = tiny(8), tiny(4), tiny(8)
        M, mp1, w0 = tiny(8), tiny(4), tiny(4)
        em, dd, hss, hms, hrs = tiny(8), tiny(8), tiny(8), tiny(8), tiny(8)
        n_sb = tiny(4)
        amax, anm, asum, ask, ard = tiny(16), tiny(16), tiny(16), tiny(16), tiny(16)
        cmax, csum = tiny(8), tiny(8)
        oms, mark = tiny(4), tiny(2)

        def c3(ap, a):
            return ap.rearrange("p (a b) -> p a b", a=a)

        ident = cst[:, K_ID:K_ID + 128]
        ones = cst[:, K_ONES:K_ONES + 128]

        def over(ap, n):
            return ap.unsqueeze(2).to_broadcast([ap.shape[0], ap.shape[1], n])

        def again(ap, m):
            return ap.unsqueeze(1).to_broadcast([ap.shape[0], m, ap.shape[1]])

        bank = [ctx.enter_context(nc.psum_tensor(f"bank{i}", [P, 512], F32)) for i in range(8)]

        skew = nc.dram_tensor("skew_dram", [HA, P, 384], F32, kind="Internal").ap()

        s_x = [sem(f"s_x{t}") for t in range(NT)]
        s_mem, s_rows, s_cst, s_small = sem("s_mem"), sem("s_rows"), sem("s_cst"), sem("s_small")
        s_table = sem("s_table")
        s_wgates, s_router = sem("s_wgates"), sem("s_router")
        s_ring = [sem(f"s_ring{i}") for i in range(RING)]
        s_slot_used = sem("s_slot_used")
        s_filled = [sem(f"s_filled{i}") for i in range(8)]
        s_freed = {(i, e): sem(f"s_freed{i}_{e}") for i in range(8) for e in ("dve", "act")}
        s_skew, s_T = sem("s_skew"), sem("s_T")
        c_dve, c_act, c_pool, c_pe = sem("c_dve"), sem("c_act"), sem("c_pool"), sem("c_pe")
        s_mean, s_root = sem("s_mean"), sem("s_root")
        s_mhalf = sem("s_mhalf")
        s_xn, s_vecs, s_hT, s_memn, s_hmT = sem("s_xn"), sem("s_vecs"), sem("s_hT"), sem("s_memn"), sem("s_hmT")
        s_pad, s_table1 = sem("s_pad"), sem("s_table1")
        s_bias = sem("s_bias")
        s_unit = sem("s_unit")
        s_conv, s_silu_e, s_qk = sem("s_conv"), sem("s_silu_e"), sem("s_qk")
        s_az, s_l, s_logf = sem("s_az"), sem("s_l"), sem("s_logf")
        s_diag = sem("s_diag")
        s_dpre, s_D = sem("s_dpre"), sem("s_D")
        s_P = sem("s_P")
        s_kct, s_vw, s_q1, s_C = sem("s_kct"), sem("s_vw"), sem("s_q1"), sem("s_C")
        s_empre, s_em = sem("s_empre"), sem("s_em")
        s_sig, s_hb = sem("s_sig"), sem("s_hb")
        s_z, s_pe_a, s_pn = sem("s_z"), sem("s_pe_a"), sem("s_pn")
        s_pt, s_mixA, s_mixB = sem("s_pt"), sem("s_mixA"), sem("s_mixB")
        s_hc, s_cm, s_cp, s_cpn, s_cpt, s_co = (
            sem("s_hc"), sem("s_cm"), sem("s_cp"), sem("s_cpn"), sem("s_cpt"), sem("s_co"))
        s_x1n, s_x2n, s_hz = sem("s_x1n"), sem("s_x2n"), sem("s_hz")
        s_out = sem("s_out")

        def filled(eng, name):
            b, before, _ = jobs[name]
            eng.wait_ge(s_filled[b], before + 1)
            return bank[b]

        def freed(name, by):
            assert (name, jobs[name][0], by) in JOBS
            return s_freed[jobs[name][0], by]

        def w_cols(w, c0, n):
            return w[0, :, c0:c0 + n].rearrange("(k p) n -> p k n", p=P)

        def as_slot(ap):
            return ap[:, 0:4096].rearrange("p (a b) -> p a b", a=8)

        places = [as_slot(yT_f), ring[4], ring[5], ring[0], as_slot(uck_f), ring[1], as_slot(hvo_f), as_slot(zp_f),
                  ring[2], ring[3]]
        N_PL = len(places)
        HVO = 6
        gain_f = hvo_f[:, 0:1024]
        hT_f = hT.rearrange("p k t -> p (k t)")
        xe, gu = hT_f[:, 0:1024].rearrange("p (k s) -> p k s", k=KD), [hT_f[:, 1024:1536], hT_f[:, 1536:2048]]
        posm = cv_f[:, 0:2 * (BLOCKS * NE + 2)].rearrange("p (t n) -> p t n", t=NT)
        comb = cv_f[:, 260:516].rearrange("p (t n) -> p t n", t=NT)
        Pg = cv_f[:, 516:772].rearrange("p (t s) -> p t s", t=NT)
        O = cv_f[:, 772:1796]
        Sg = qkv_f[:, 1280:1536].rearrange("p (t s) -> p t s", t=NT)
        zeros = O[:, 0:512]
        E_f = [qkv_f[:, 0:256], qkv_f[:, 256:512]]
        hE = [qkv_f[:, 512:768], qkv_f[:, 768:1024]]
        ST = qkv_f[:, 1024:1280]
        at = [0]

        def r3(n):
            at[0] += 2 * n
            return qkv_f[:, at[0] - 2 * n:at[0]].rearrange("p (t n) -> p t n", t=NT)

        lg, gx, gq, ohg, el, eq, oh1, oh2, sel, posr = (
            r3(36), r3(4), r3(4), r3(4), r3(32), r3(32), r3(32), r3(32), r3(32), r3(32))
        gmax, gsum, mr, e1, e2, rr, g1, g2 = (r3(1) for _ in range(8))
        cmaxf = qkv_f[:, at[0]:at[0] + 1]
        cmaxi = sb("cmaxi", [P, 1], I32)
        PAIRS = NE // 2

        s_zero = sem("s_zero")
        s_left = sem("s_left")
        s_we = [[sem(f"s_we{i}_{h}") for h in range(2)] for i in range(N_PL)]
        s_gain = sem("s_gain")
        s_logit_e, s_route, s_route_e, s_M, s_cnt = sem("s_logit_e"), sem("s_route"), sem("s_route_e"), sem("s_M"), sem("s_cnt")
        s_pos = sem("s_pos")
        s_y = sem("s_y")
        s_all_o, s_all_st = sem("s_all_o"), sem("s_all_st")
        s_sum, s_sq, s_outn = sem("s_sum"), sem("s_sq"), sem("s_outn")
        s_pg, s_sg = sem("s_pg"), sem("s_sg")
        s_gat, s_xe = sem("s_gat"), sem("s_xe")
        s_gu, s_gue = sem("s_gu"), sem("s_gue")
        s_t, s_ee, s_h = sem("s_t"), sem("s_ee"), sem("s_h")
        s_stt, s_st = sem("s_stt"), sem("s_st")
        s_down, s_o, s_comb = sem("s_down"), sem("s_o"), sem("s_comb")
        c_moe = sem("c_moe")

        def all_pairs(eng, one_pair, steps=1):
            def block_of(blk, G0):
                one_pair(G0, blk, first=True)
                with eng.Fori(0, (PAIRS - 1) // steps) as r:
                    for i in range(steps):
                        one_pair(G0 + steps * r + i + 1, blk, r, i)

            block_of(0, 0)
            eng.wait_ge(s_cnt, 1)
            most = eng.value_load(cmaxi[0:1, 0:1], min_val=0, max_val=T)
            with eng.If(most > SLOTS):
                with eng.Fori(1, BLOCKS) as blk:
                    block_of(blk, PAIRS * blk)

        def load_half(sp, e, which, place, half):
            w, k, n = ((w_exp_gate, 8, 512), (w_exp_up, 8, 512), (w_exp_down, 4, 1024))[which]
            rows_of = slice(half * k // 2 * P, (half + 1) * k // 2 * P)
            src = w[0, bass.ds(e, 1), rows_of, :].rearrange("o (k p) n -> p (o k) n", p=P)
            dst = places[place % N_PL][:, 4 * half:4 * half + 4, :].rearrange("p a b -> p (a b)").rearrange("p (k n) -> p k n", k=k // 2)
            sp.dma_start(dst, src).then_inc(s_we[place % N_PL][half], 16)

        def reached(eng, sem_, n):
            if not isinstance(n, int) or n > 0:
                eng.wait_ge(sem_, n)

        ORDER = ((0, 0), (0, 1), (1, 0), (1, 1), (0, 2), (1, 2))

        LAP = N_PL // 2

        def moe_sync(sp):
            def load(pair, j, n, halves=(0, 1)):
                e, which = ORDER[j]
                for half in halves:
                    load_half(sp, 2 * pair + e, which, n, half)

            for n, sem_, count in ((1, s_slot_used, 11), (2, s_slot_used, 12), (3, s_slot_used, 13),
                                   (5, s_slot_used, 14),
                                   (4, s_slot_used, 14),
                                   (6, s_slot_used, 14),
                                   (7, s_co, 1),
                                   (8, s_slot_used, 15), (9, s_slot_used, 16)):
                sp.wait_ge(sem_, count)
                load(n // 6, n % 6, n)

            def one_pair(G, pair, i, first_j=0):
                for j in range(first_j, 6, 2):
                    for half in range(2):
                        for jj in (j, j + 1):
                            if half == 0:
                                sem_, count = ((s_gu, 2 * G - 2), (s_down, G - 1), (s_gu, 2 * G - 1))[j // 2]
                                reached(sp, sem_, count)
                            load(pair, jj, 6 * (i + 1) + jj, (half,))

            for i in range(LAP):
                one_pair(i + 1, i + 1, i, first_j=0 if i else 4)
            with sp.Fori(1, 3) as r:
                for i in range(LAP):
                    one_pair(LAP * r + i + 1, LAP * r + i + 1, i)
            sp.wait_ge(s_cnt, 1)
            with sp.If(sp.value_load(cmaxi[0:1, 0:1], min_val=0, max_val=T) > SLOTS):
                with sp.Fori(1, BLOCKS) as blk:
                    sp.wait_ge(s_down, PAIRS * blk)
                    for j in range(6):
                        load(0, j, j)
                    with sp.Fori(0, 3) as r:
                        for i in range(LAP):
                            one_pair(PAIRS * blk + LAP * r + i + 1, LAP * r + i + 1, i)
                sp.wait_ge(s_down, PAIRS * BLOCKS - 1)
            sp.wait_ge(s_down, PAIRS - 1)
            sp.dma_start(gain_f, norm_final.partition_broadcast(P)).then_inc(s_gain, 16)
            for t in range(NT):
                for half in range(2):
                    cols = slice(half * 512, (half + 1) * 512)
                    sp.wait_ge(s_outn, 2 * t + half + 1)
                    sp.dma_start(out[0, t * P:(t + 1) * P, cols], xn[:, t, cols]).then_inc(s_out, 16)
            sp.wait_ge(s_out, 64)

        def moe_act(act, lane):
            did, settle = lane.did, lane.settle
            act.wait_ge(s_route, 1)
            did(nc.scalar.activation(gq, gx, ACT.Exp), s_logit_e)
            act.wait_ge(s_route, 2)
            did(nc.scalar.activation(rr, rr, ACT.Exp), s_route_e)

            def one_pair(G, blk, r=None, i=None, first=False):
                for e in range(2):
                    n = 2 * G + e + 1
                    act.wait_ge(s_gu, n)
                    act.wait_ge(s_t, n)
                    nc.scalar.copy(gu[e], bank[6][:, :]).then_inc(s_gue, 1)
                    act.wait_ge(s_t, n + 2)
                    g_t = bank[7][:, :].rearrange("p (f s) -> p f s", f=4)[:, :, 0:64]
                    nc.scalar.activation(E_f[e].rearrange("p (f s) -> p f s", f=4), g_t, ACT.Exp, scale=-1.0).then_inc(s_ee, 1)
                reached(act, s_down, G + 1)
                reached(act, s_comb, G)
                nc.scalar.copy(O[:, 0:512], bank[4][:, :])
                nc.scalar.copy(O[:, 512:1024], bank[5][:, :]).then_inc(s_o, 1)

            all_pairs(act, one_pair)
            nc.scalar.copy(mark[:, 0:1], ones[:, 0:1]).then_inc(s_all_o, 1)
            for t in range(NT):
                for half in range(2):
                    act.wait_ge(s_sum, 2 * t + half + 1)
                    cols = slice(half * 512, (half + 1) * 512)
                    did(nc.scalar.activation(xn[:, t, cols], x_sb[:, t, cols], ACT.Square, scale=D ** -0.5,
                                             accum_out=oms[:, 2 * t + half:2 * t + half + 1]), s_sq)

        def moe_pe(pe, open_job, close_job, transposes):
            pe.wait_ge(s_zero, 1)

            def clear_y(t):
                for i in (2 * t, 2 * t + 1):
                    before = last_of_bank[i]
                    pe.wait_ge(s_freed[i, before[0]], before[1])
                    nc.tensor.matmul(bank[i][:, :], zeros[:, 0:P], zeros, start=True, stop=True)

            for t in range(NT):
                pe.wait_ge(s_x2n, t + 1)
                for half in range(2):
                    transposes(f"zT{t}{'ab'[half]}", [xn[:, t, (4 * half + k) * P:(4 * half + k + 1) * P] for k in range(4)])
                if t == 0:
                    clear_y(0)
            pe.wait_ge(s_hz, 4)
            pe.wait_ge(s_router, 16)
            b = open_job("logit")
            for t in range(NT):
                for k in range(KD):
                    mm = nc.tensor.matmul(b[:, t * 36:(t + 1) * 36], hT[:, k, t * P:(t + 1) * P], wr[:, k, :],
                                          start=(k == 0), stop=(k == KD - 1))
            close_job("logit", mm)
            clear_y(1)
            pe.wait_ge(s_M, 1)
            b = open_job("pos")
            strict = cst[:, K_STRICT:K_STRICT + 128]
            nc.tensor.matmul(b[:, 0:32], strict, sel[:, 0, :], start=True, stop=True)
            nc.tensor.matmul(b[:, 32:64], ones, sel[:, 0, :], start=True, stop=False)
            nc.tensor.matmul(b[:, 32:64], strict, sel[:, 1, :], start=False, stop=True)
            nc.tensor.matmul(b[:, 64:96], ones, sel[:, 0, :], start=True, stop=False)
            close_job("pos", nc.tensor.matmul(b[:, 64:96], ones, sel[:, 1, :], start=False, stop=True))
            for i in (6, 7):
                before = last_of_bank[i]
                pe.wait_ge(s_freed[i, before[0]], before[1])
            for i in range(2):
                pe.nop().then_inc(s_t, 1)

            def expert_half(blk, r, i, j, half):
                n = j if r is None else 6 * (i + 1) + j
                before = (10 if n % N_PL < 6 else 9) * blk
                lap = 0 if r is None else 3 * r
                pe.wait_ge(s_we[n % N_PL][half], 16 * (before + lap + n // N_PL + 1))
                return places[n % N_PL]

            def gather(G):
                reached(pe, s_pg, G + 1)
                for k in range(KD):
                    for t in range(NT):
                        mm = nc.tensor.matmul(bank[4 + k // 4][:, (k % 4) * P:(k % 4 + 1) * P], xn[:, t, k * P:(k + 1) * P],
                                              Pg[:, t, :], start=(t == 0), stop=(t == NT - 1))
                mm.then_inc(s_gat, 1)

            def gate_up(blk, r, i, e):
                for k in range(KD):
                    if k % 4 == 0:
                        w = [expert_half(blk, r, i, 2 * e + m, k // 4) for m in range(2)]
                    for half in range(2):
                        mm = nc.tensor.matmul(bank[6][64 * half:64 * half + 64, :], xe[:, k, 64 * e:64 * e + 64], w[half][:, k, :],
                                              start=(k == 0), stop=(k == KD - 1))
                mm.then_inc(s_gu, 1)

            def turn(G, e):
                reached(pe, s_gue, 2 * G + e + 1)
                reached(pe, s_h, 2 * G + e)
                for f in range(4):
                    mm = nc.tensor.transpose(bank[7][:, f * P:(f + 1) * P], gu[e][:, f * P:(f + 1) * P], ident)
                mm.then_inc(s_t, 1)

            def combine(t, half):
                return nc.tensor.matmul(bank[2 * t + half][:, :], ST[:, t * P:(t + 1) * P], O[:, half * 512:(half + 1) * 512],
                                        start=False, stop=False, skip_group_check=True)

            pe.wait_ge(s_pos, 1)
            gather(0)

            def one_pair(G, blk, r=None, i=None, first=False):
                reached(pe, s_xe, G + 1)
                reached(pe, s_st, G)
                gate_up(blk, r, i, 0)
                reached(pe, s_o, G)
                gather(G + 1)
                turn(G, 0)
                gate_up(blk, r, i, 1)
                turn(G, 1)
                reached(pe, s_sg, G + 1)
                for t in range(NT):
                    mm = nc.tensor.transpose(bank[6][:, t * P:(t + 1) * P], Sg[:, t, :], ident)
                mm.then_inc(s_stt, 1)
                if not (first and isinstance(G, int)):
                    reached(pe, s_o, G)
                    reached(pe, s_st, G)
                    for t in range(NT):
                        for half in range(2):
                            mm = combine(t, half)
                    mm.then_inc(s_comb, 1)
                reached(pe, s_h, 2 * G + 2)
                reached(pe, s_xe, G + 2)
                for f in range(4):
                    if f % 2 == 0:
                        w = [expert_half(blk, r, i, 4 + e, f // 2)[:, :, :].rearrange("p a b -> p (a b)") for e in range(2)]
                    for half in range(2):
                        for e in range(2):
                            lo = f * 1024 + half * 512
                            mm = nc.tensor.matmul(bank[4 + half][64 * e:64 * e + 64, :], hE[e][:, f * 64:(f + 1) * 64],
                                                  w[e][:, lo:lo + 512], start=(f == 0), stop=(f == 3))
                mm.then_inc(s_down, 1)

            all_pairs(pe, one_pair, steps=LAP)
            pe.wait_ge(s_all_o, 1)
            pe.wait_ge(s_all_st, 1)
            for t in range(NT):
                for half in range(2):
                    mm = combine(t, half)
                mm.then_inc(s_y, 1)

        def moe_dve(dve, lane, rms_rows, to_feature_major):
            did, settle = lane.did, lane.settle
            V = nc.vector
            to_feature_major("zT", hT, R_MOE, s_hz)

            def tt(o, a, b, op, sem_=None):
                did(V.tensor_tensor(o, a, b, op), sem_)
                settle()

            def wide(ap, n):
                return ap.to_broadcast([P, NT, n])

            def first_of(values, top, ranks, onehot):
                n = values.shape[2]
                tt(onehot, values, wide(top, n), ALU.is_equal)
                tt(onehot, onehot, again(ranks, NT), ALU.mult)
                did(V.tensor_reduce(mr, onehot, AX_X, ALU.max))
                settle()
                tt(onehot, onehot, wide(mr, n), ALU.is_equal)

            ranks_g, ranks_e = cst[:, K_RG:K_RG + 4], cst[:, K_RE:K_RE + 32]
            b = filled(dve, "logit")
            did(V.tensor_tensor(lg, c3(b[:, 0:72], 2), again(rbias, NT), ALU.add), freed("logit", "dve"))
            settle()
            did(V.tensor_reduce(gmax, lg[:, :, 0:4], AX_X, ALU.max))
            settle()
            did(V.tensor_tensor(gx, lg[:, :, 0:4], wide(gmax, 4), ALU.subtract), s_route)
            first_of(lg[:, :, 0:4], gmax, ranks_g, ohg)
            did(V.tensor_scalar(ohg, ohg, 1.0, -NEG, ALU.subtract, ALU.mult))
            settle()
            for t in range(NT):
                did(V.tensor_tensor(c3(el[:, t, :], 4), c3(lg[:, t, 4:36], 4), over(ohg[:, t, :], EG), ALU.add))
            settle()
            did(V.tensor_reduce(e1, el, AX_X, ALU.max))
            settle()
            first_of(el, e1, ranks_e, oh1)
            did(V.scalar_tensor_tensor(eq, oh1, 2 * NEG, el, ALU.mult, ALU.add))
            settle()
            did(V.tensor_reduce(e2, eq, AX_X, ALU.max))
            settle()
            did(V.tensor_tensor(rr, e2, e1, ALU.subtract), s_route)
            first_of(eq, e2, ranks_e, oh2)
            tt(sel, oh1, oh2, ALU.add, s_M)
            b = filled(dve, "pos")
            did(V.tensor_reduce(cmaxf, b[:, 64:96], AX_X, ALU.max))
            did(V.scalar_tensor_tensor(posr, c3(b[:, 0:64], 2), 1.0, sel, ALU.add, ALU.mult), s_pos)
            settle()
            did(V.tensor_scalar(posm[:, :, 0:NE], posr, -1.0, None, ALU.add))
            settle()

            def gates_and_blocks():
                for blk in range(1, BLOCKS + 1):
                    n = NE if blk < BLOCKS else 2
                    did(V.tensor_scalar(posm[:, :, blk * NE:blk * NE + n], posr[:, :, 0:n], -1.0 - blk * SLOTS, None, ALU.add))
                did(V.tensor_copy(cmaxi[:, :], cmaxf), s_cnt)
                dve.wait_ge(s_logit_e, 1)
                did(V.tensor_reduce(gsum, gq, AX_X, ALU.add))
                dve.wait_ge(s_route_e, 1)
                did(V.tensor_scalar(g1, rr, 1.0, None, ALU.add))
                settle()
                tt(g1, g1, gsum, ALU.mult)
                did(V.reciprocal(g1, g1))
                settle()
                tt(g2, g1, rr, ALU.mult)
                tt(oh1, oh1, wide(g1, 32), ALU.mult)
                tt(oh2, oh2, wide(g2, 32), ALU.mult)
                for blk in range(BLOCKS):
                    did(V.tensor_tensor(comb[:, :, blk * NE:(blk + 1) * NE], oh1, oh2, ALU.add))
                settle()

            slots = cst[:, K_SLOT:K_SLOT + 64]

            def select(G):
                for e in range(2):
                    for t in range(NT):
                        ins = V.tensor_scalar(Pg[:, t, 64 * e:64 * e + 64], slots, posm[:, t, bass.ds(2 * G + e, 1)], None, ALU.is_equal)
                ins.then_inc(s_pg, 1)

            def evacuate_gathered(G):
                reached(dve, s_gat, G + 1)
                for half in range(2):
                    ins = V.tensor_tensor(xe[:, 4 * half:4 * half + 4, :], c3(bank[4 + half][:, :], 4),
                                          over(vecs[:, R_MOE + 4 * half:R_MOE + 4 * half + 4], P), ALU.mult)
                ins.then_inc(s_xe, 1)

            select(0)
            gates_and_blocks()
            evacuate_gathered(0)

            PER = 6

            def one_pair(G, blk, r=None, i=None, first=False):
                step = [0]

                def chain(ins):
                    step[0] += 1
                    ins.then_inc(c_moe, 1)
                    dve.wait_ge(c_moe, PER * G + step[0])

                reached(dve, s_gat, G + 1)
                select(G + 1)
                reached(dve, s_stt, G)
                for e in range(2):
                    for t in range(NT):
                        ins = V.tensor_scalar(Sg[:, t, 64 * e:64 * e + 64], slots, posm[:, t, bass.ds(2 * G + e, 1)],
                                              comb[:, t, bass.ds(2 * G + e, 1)], ALU.is_equal, ALU.mult)
                ins.then_inc(s_sg, 1)
                for e in range(2):
                    if e:
                        reached(dve, s_gu, 2 * G + 2)
                        evacuate_gathered(G + 1)
                    reached(dve, s_ee, 2 * G + e + 1)
                    turned = bank[7][:, :].rearrange("p (f s) -> p f s", f=4)
                    E4 = E_f[e].rearrange("p (f s) -> p f s", f=4)
                    chain(V.tensor_scalar(E_f[e], E_f[e], 1.0, None, ALU.add))
                    chain(V.reciprocal(E_f[e], E_f[e]))
                    chain(V.tensor_tensor(E4, E4, turned[:, :, 0:64], ALU.mult))
                    reached(dve, s_down, G)
                    V.tensor_tensor(hE[e].rearrange("p (f s) -> p f s", f=4), E4, turned[:, :, 64:128], ALU.mult).then_inc(s_h, 1)
                reached(dve, s_stt, G + 1)
                reached(dve, s_comb, G)
                V.tensor_copy(ST, bank[6][:, 0:256]).then_inc(s_st, 1)
                assert step[0] == PER

            all_pairs(dve, one_pair)
            V.tensor_copy(mark[:, 1:2], ones[:, 0:1]).then_inc(s_all_st, 1)
            for t in range(NT):
                dve.wait_ge(s_y, t + 1)
                for half in range(2):
                    xs = x_sb[:, t, half * 512:(half + 1) * 512]
                    did(V.tensor_tensor(xs, xs, bank[2 * t + half][:, :], ALU.add), s_sum)
            dve.wait_ge(s_gain, 16)
            for t in range(NT):
                dve.wait_ge(s_sq, 2 * t + 2)
                did(V.scalar_tensor_tensor(ms[:, 8 + t:9 + t], oms[:, 2 * t:2 * t + 1], EPS, oms[:, 2 * t + 1:2 * t + 2],
                                           ALU.add, ALU.add), s_mean)
                dve.wait_ge(s_root, 10 + t)
                for half in range(2):
                    cols = slice(half * 512, (half + 1) * 512)
                    did(V.scalar_tensor_tensor(xn[:, t, cols], x_sb[:, t, cols], rs[:, 8 + t:9 + t], gain_f[:, cols],
                                               ALU.mult, ALU.mult), s_outn)

        block = ctx.enter_context(nc.Block())

        @block.sync
        def _(sp):
            sp.dma_start(x_sb[:, 0, :], x[0, 0:P, :]).then_inc(s_x[0], 16)
            sp.dma_start(cst, const_tile).then_inc(s_cst, 16)
            sp.dma_start(x_sb[:, 1, :], x[0, P:T, :]).then_inc(s_x[1], 16)
            sp.dma_start(rows, vectors).then_inc(s_rows, 16)
            sp.dma_start(wg8, w_cols(w_in, C_G, 8)).then_inc(s_wgates, 16)
            sp.dma_start(small, biases.partition_broadcast(P)).then_inc(s_small, 16)
            front = [w_cols(w_in, C_QB, 512), w_cols(w_in, C_KB, 512), w_cols(w_in, C_QA, 512),
                     w_cols(w_in, C_KA, 256), w_cols(w_in, C_VB, 512), w_cols(w_in, C_OB, 512),
                     w_cols(w_ck, 0, 512), w_cols(w_ck, 512, 512), w_cols(w_cv, 0, 512),
                     w_cols(w_out, 0, 512), w_cols(w_out, 512, 512), w_cols(w_cq, 0, 512), w_cols(w_cq, 512, 512),
                     w_cols(w_cv, 512, 512), w_cols(w_co, 0, 512), w_cols(w_co, 512, 512)]
            assert len(front) == FRONT
            for q, src in enumerate(front):
                if q >= RING:
                    sp.wait_ge(s_slot_used, q - RING + 1)
                sp.dma_start(ring[q % RING][:, :, 0:src.shape[2]], src).then_inc(s_ring[q % RING], 16)
                if q == 0:
                    sp.wait_ge(s_table1, 1)
                    sp.dma_start(table[0:32, :], rel_bias_table).then_inc(s_table, 16)
                    sp.dma_start(bands, const_bands).then_inc(s_table, 16)
                    sp.dma_start(mem_sb, mem[0].rearrange("(t p) d -> p t d", p=P)).then_inc(s_mem, 16)
                if q == 13:
                    sp.wait_ge(s_left, 1)
                    for half in range(2):
                        load_half(sp, 0, 0, 0, half)
                if q == 3:
                    sp.dma_start(wr, routers.rearrange("(k p) c -> p k c", p=P)).then_inc(s_router, 16)
            moe_sync(sp)

        @block.scalar
        def _(act):
            lane = Lane(act, c_act)
            did, settle = lane.did, lane.settle
            act.wait_ge(s_az, 1)
            did(nc.scalar.activation(az[:, 8:16], az[:, 0:8], ACT.Exp, scale=-1.0))
            settle()
            did(nc.scalar.activation(az[:, 0:8], az[:, 8:16], ACT.Ln, bias=1.0), s_l)

            def unit(n, dst):
                b = filled(act, f"U{n}")
                did(nc.scalar.copy(dst, b[:, :].rearrange("p (a b) -> p a b", a=2) if len(dst.shape) == 3 else b[:, :]),
                    freed(f"U{n}", "act"))

            def unit_done():
                settle()
                did(act.nop(), s_unit)

            act.wait_ge(s_pad, 1)
            unit(0, u[:, 0:2, 3:259])
            unit(1, u[:, 2:4, 3:259])
            unit_done()
            bk = filled(act, "bias")
            did(nc.scalar.copy(bias_sb, bk[0:8, 0:384]), freed("bias", "act"))
            settle()
            act.dma_start(skew, bias_sb.unsqueeze(1).to_broadcast([8, P, 384])).then_inc(s_skew, 16)
            unit(2, u[:, 4:6, 3:259])
            act.wait_ge(s_conv, 1)
            did(nc.scalar.activation(silu_e, y_f[:, 0:1024], ACT.Exp, scale=-1.0), s_silu_e)
            act.wait_ge(s_dpre, 1)
            did(nc.scalar.activation(Dm[0], Dm[0], ACT.Exp), s_D)
            act.wait_ge(s_dpre, 2)
            did(nc.scalar.activation(w0, w0, ACT.Exp), s_D)
            unit(3, u[:, 6:8, 3:259])
            unit_done()
            act.wait_ge(s_skew, 16)
            act.dma_start(Tb, bass.AP(tensor=skew.tensor, offset=127,
                                      ap=[[383, P], [P * 384, HA], [1, 256]])).then_inc(s_T, 16)
            act.wait_ge(s_empre, 1)
            did(nc.scalar.activation(em, em, ACT.Exp, scale=-1.0), s_em)
            act.wait_ge(s_dpre, 3)
            did(nc.scalar.activation(Dm[1], Dm[1], ACT.Exp), s_D)
            act.wait_ge(s_dpre, 4)
            did(nc.scalar.activation(aib, aib, ACT.Exp), s_D)
            unit(4, qaT[:, 0:2, :])
            act.wait_ge(s_conv, 2)
            act.wait_ge(s_qk, 1)
            did(nc.scalar.activation(silu_e, y_f[:, 1024:2048], ACT.Exp, scale=-1.0), s_silu_e)
            unit(5, qaT[:, 2:4, :])
            b6 = filled(act, "U6")
            did(nc.scalar.copy(kaT, b6[:, 0:256]))
            did(nc.scalar.copy(va, b6[:, 256:512].rearrange("p (t d) -> p t d", t=NT)), freed("U6", "act"))
            unit_done()

            def attn_exp(t):
                act.wait_ge(s_z, t + 1)
                n = 128 if t == 0 else 256
                for h in range(HA):
                    zt = Z_f[:, h * n:(h + 1) * n]
                    did(nc.scalar.activation(zt, zt, ACT.Exp, bias=anm[:, 8 * t + h:8 * t + h + 1],
                                             accum_out=asum[:, 8 * t + h:8 * t + h + 1]))
                did(nc.scalar.activation(ask[:, 8 * t:8 * t + 8], ask[:, 8 * t:8 * t + 8], ACT.Exp), s_pe_a)

            b = filled(act, "kct")
            act.wait_ge(s_qk, 2)
            did(nc.scalar.copy(kct, b[:, :]), freed("kct", "act"))
            settle()
            did(act.nop(), s_kct)
            attn_exp(0)
            unit(7, vb[:, 0, :])
            unit(8, vb[:, 1, :])
            unit_done()

            def sigmoid_e(n, t):
                b = filled(act, f"U{n}")
                did(nc.scalar.activation(ob[:, t, :], b[:, :], ACT.Exp, scale=-1.0), freed(f"U{n}", "act"))
                settle()
                did(act.nop(), s_sig)

            sigmoid_e(9, 0)

            def pt_copy(name, dst):
                b = filled(act, name)
                did(nc.scalar.copy(dst, b[:, :]), freed(name, "act"))

            pt_copy("tA0a", PT_f[:, 0:512])
            pt_copy("tA0b", PT_f[:, 512:1024])
            settle()
            did(act.nop(), s_pt)
            sigmoid_e(10, 1)

            def mix_a(t):
                b = filled(act, f"oA{t}")
                did(nc.scalar.copy(hT[:, 0:4, t * P:(t + 1) * P], b[:, :].rearrange("p (c i) -> p c i", c=4)),
                    freed(f"oA{t}", "act"))
                settle()
                did(act.nop(), s_mixA)

            mix_a(0)
            unit(11, ckT[:, 0:2, :])
            attn_exp(1)
            unit(12, ckT[:, 2:4, :])
            pt_copy("tA1a", PT_f[:, 0:512])
            pt_copy("tA1b", PT_f[:, 512:1024])
            unit(13, ckT[:, 4:6, :])
            pt_copy("tA1c", PT_f[:, 1024:1536])
            pt_copy("tA1d", PT_f[:, 1536:2048])
            settle()
            did(act.nop(), s_pt)
            unit(14, ckT[:, 6:8, :])
            mix_a(1)
            unit(15, cv[:, 0, 0:512])
            unit(16, cv[:, 1, 0:512])
            for i in range(4):
                unit(23 + i, cqT[:, 2 * i:2 * i + 2, :])
            unit_done()
            for t in range(NT):
                for half in range(2):
                    act.wait_ge(s_cm, 2 * t + half + 1)
                    b = filled(act, f"sX{t}{'ab'[half]}")
                    for g in range(2):
                        h = 2 * half + g
                        ins = nc.scalar.activation(
                            Z_f[:, (t * 4 + h) * 256:(t * 4 + h + 1) * 256], b[:, g * 256:(g + 1) * 256], ACT.Exp,
                            bias=cmax[:, t * 4 + h:t * 4 + h + 1], scale=DX ** -0.5,
                            accum_out=csum[:, t * 4 + h:t * 4 + h + 1])
                        did(ins, freed(f"sX{t}{'ab'[half]}", "act") if g else None)
                settle()
                did(act.nop(), s_cp)
            unit(17, cv[:, 0, 512:1024])
            unit(18, cv[:, 1, 512:1024])
            unit_done()
            for i in range(4):
                pt_copy(f"TX{i}", PT_f[:, i * 512:(i + 1) * 512])
                settle()
                did(act.nop(), s_cpt)
            for i in range(4):
                b = filled(act, f"oX{i}")
                did(nc.scalar.copy(hT[:, 2 * i:2 * i + 2, :], b[:, :].rearrange("p (c i) -> p c i", c=2)),
                    freed(f"oX{i}", "act"))
            settle()
            did(act.nop(), s_co)
            moe_act(act, lane)

        @block.tensor
        def _(pe):
            def open_job(name):
                b, _, before = jobs[name]
                if before:
                    pe.wait_ge(s_freed[b, before[0]], before[1])
                return bank[b]

            def close_job(name, mm):
                mm.then_inc(s_filled[jobs[name][0]], 1)

            def slot(q):
                pe.wait_ge(s_ring[q % RING], 16 * (q // RING + 1))
                return ring[q % RING]

            def transposes(name, parts, n=128):
                b = open_job(name)
                for i, src in enumerate(parts):
                    mm = nc.tensor.transpose(b[:, i * n:(i + 1) * n], src, ident)
                close_job(name, mm)

            def unit_T(n, q, c0, src):
                w = slot(q)
                b = open_job(f"U{n}")
                for c in range(2):
                    for k in range(KD):
                        mm = nc.tensor.matmul(b[:, c * 256:(c + 1) * 256], w[:, k, c0 + c * 128:c0 + (c + 1) * 128],
                                              src[:, k, :], start=(k == 0), stop=(k == KD - 1))
                close_job(f"U{n}", mm)
                return mm

            def unit_N(n, q, t, src):
                w = slot(q)
                b = open_job(f"U{n}")
                for k in range(KD):
                    mm = nc.tensor.matmul(b[:, :], src[:, k, t * P:(t + 1) * P], w[:, k, :],
                                          start=(k == 0), stop=(k == KD - 1))
                close_job(f"U{n}", mm)

            def used_after(name, slots=1):
                b, before, _ = jobs[name]
                pe.wait_ge(s_filled[b], before + 1)
                for _ in range(slots):
                    pe.nop().then_inc(s_slot_used, 1)

            pe.wait_ge(s_cst, 16)
            pe.wait_ge(s_rows, 16)
            b = open_job("rows")
            close_job("rows", nc.tensor.transpose(b[:, 0:R_ALL], rows, ident[0:R_ALL, 0:R_ALL]))
            for t in range(NT):
                pe.wait_ge(s_xn, t + 1)
                for half in range(2):
                    transposes(f"xT{t}{'ab'[half]}", [xn[:, t, (4 * half + k) * P:(4 * half + k + 1) * P] for k in range(4)])
            pe.wait_ge(s_hT, 4)
            pe.wait_ge(s_wgates, 16)
            b = open_job("gates")
            for t in range(NT):
                for k in range(KD):
                    mm = nc.tensor.matmul(b[:, t * 8:(t + 1) * 8], hT[:, k, t * P:(t + 1) * P], wg8[:, k, :],
                                          start=(k == 0), stop=(k == KD - 1))
            close_job("gates", mm)

            def row_of(name, diag, n):
                pe.wait_ge(s_diag, n)
                b = open_job(name)
                close_job(name, nc.tensor.matmul(b[:, :], ones, diag, start=True, stop=True))

            unit_T(0, 0, 0, hT)
            pe.wait_ge(s_logf, 1)
            b = open_job("bcum")
            for t in range(NT):
                nc.tensor.matmul(b[:, t * 4:(t + 1) * 4], cst[:, K_TRIU:K_TRIU + 128], lf[:, t * 4:(t + 1) * 4],
                                 start=True, stop=True)
            close_job("bcum", nc.tensor.matmul(b[:, 8:12], ones, lf[:, 0:4], start=True, stop=True))
            unit_T(1, 0, 256, hT)
            used_after("U1")
            pe.wait_ge(s_table1, 1)
            pe.wait_ge(s_table, 32)
            b = open_job("bias")
            close_job("bias", nc.tensor.matmul(b[0:8, 0:384], table, bands, start=True, stop=True))
            row_of("R0", Dg[0], 1)
            row_of("R1", Dg[1], 2)
            unit_T(2, 1, 0, hT)
            row_of("Mb0", Dg[0], 3)
            unit_T(3, 1, 256, hT)
            used_after("U3")
            row_of("Mb1", Dg[1], 4)

            def unit_qa(n, c0):
                w = slot(2)
                b = open_job(f"U{n}")
                for c in range(2):
                    for k in range(KD):
                        for half in range(2):
                            h = 4 * half + c0 + c
                            mm = nc.tensor.matmul(b[64 * half:64 * half + 64, c * 256:(c + 1) * 256],
                                                  w[:, k, h * DA:(h + 1) * DA], hT[:, k, :],
                                                  start=(k == 0), stop=(k == KD - 1))
                close_job(f"U{n}", mm)

            unit_qa(4, 0)
            unit_qa(5, 2)
            used_after("U5")
            w = slot(3)
            b = open_job("U6")
            for k in range(KD):
                nc.tensor.matmul(b[:, 0:256], w[:, k, 0:128], hT[:, k, :], start=(k == 0), stop=(k == KD - 1))
            for t in range(NT):
                for k in range(KD):
                    mm = nc.tensor.matmul(b[:, 256 + t * P:256 + (t + 1) * P], hT[:, k, t * P:(t + 1) * P],
                                          w[:, k, 128:256], start=(k == 0), stop=(k == KD - 1))
            close_job("U6", mm)
            used_after("U6")
            pe.wait_ge(s_unit, 3)
            for g in range(2):
                name = f"sA0{'ab'[g]}"
                b = open_job(name)
                for c in range(4):
                    mm = nc.tensor.matmul(b[:, c * 128:(c + 1) * 128], qaT[64 * g:64 * g + 64, c, 0:P],
                                          kaT[64 * g:64 * g + 64, 0:P], start=True, stop=True)
                close_job(name, mm)

            def scores_b(t):
                b = open_job(f"sc{t}")
                for h in range(HB):
                    mm = nc.tensor.matmul(b[:, h * P:(h + 1) * P], y[:, 4 + h, t * P:(t + 1) * P],
                                          y[:, h, t * P:(t + 1) * P], start=True, stop=True)
                close_job(f"sc{t}", mm)

            pe.wait_ge(s_qk, 2)
            transposes("kct", [y[:, 4 + h, 0:P] for h in range(HB)])
            scores_b(0)
            scores_b(1)
            unit_N(7, 4, 0, hT)
            pe.wait_ge(s_memn, 1)
            for t in range(NT):
                for half in range(2):
                    transposes(f"mT{t}{'ab'[half]}", [mem_sb[:, t, (4 * half + k) * P:(4 * half + k + 1) * P] for k in range(4)])
            unit_N(8, 4, 1, hT)
            used_after("U8")
            unit_N(9, 5, 0, hT)

            def numerator(t):
                pe.wait_ge(s_P, t + 1)
                pe.wait_ge(s_unit, 4)
                if t:
                    pe.wait_ge(s_C, 1)
                    pe.wait_ge(s_q1, 1)
                b = open_job(f"num{t}")
                for h in range(HB):
                    mm = nc.tensor.matmul(b[:, h * P:(h + 1) * P], Pm[t][:, h * P:(h + 1) * P], vb[:, t, h * P:(h + 1) * P],
                                          start=True, stop=(t == 0))
                    if t:
                        mm = nc.tensor.matmul(b[:, h * P:(h + 1) * P], y[:, h, P:T], Cs[:, h * P:(h + 1) * P],
                                              start=False, stop=True)
                close_job(f"num{t}", mm)
                b = open_job(f"den{t}")
                for h in range(HB):
                    mm = nc.tensor.matmul(b[:, h:h + 1], Pm[t][:, h * P:(h + 1) * P], ones[:, 0:1],
                                          start=True, stop=(t == 0))
                    if t:
                        mm = nc.tensor.matmul(b[:, h:h + 1], y[:, h, P:T], n_sb[:, h:h + 1], start=False, stop=True)
                close_job(f"den{t}", mm)

            numerator(0)

            def p_transposes(names, per):
                for i, name in enumerate(names):
                    transposes(name, [Z_f[:, (4 * i + j) * P:(4 * i + j + 1) * P] for j in range(4)])

            pe.wait_ge(s_pn, 1)
            p_transposes(["tA0a", "tA0b"], 4)
            unit_N(10, 5, 1, hT)
            used_after("U10")
            pe.wait_ge(s_vw, 1)
            pe.wait_ge(s_kct, 1)
            b = open_job("Cst")
            for h in range(HB):
                mm = nc.tensor.matmul(b[:, h * P:(h + 1) * P], kct[:, h * P:(h + 1) * P], vb[:, 0, h * P:(h + 1) * P],
                                      start=True, stop=True)
            close_job("Cst", mm)
            b = open_job("nst")
            for h in range(HB):
                mm = nc.tensor.matmul(b[:, h:h + 1], kct[:, h * P:(h + 1) * P], w0[:, h:h + 1], start=True, stop=True)
            close_job("nst", mm)

            def scores_a1(i):
                name = f"sA1{'abcd'[i]}"
                b = open_job(name)
                for g in range(2):
                    h = 2 * i + g
                    lo = 64 * (h // 4)
                    mm = nc.tensor.matmul(b[:, g * 256:(g + 1) * 256], qaT[lo:lo + 64, h % 4, P:T], kaT[lo:lo + 64, :],
                                          start=True, stop=True)
                close_job(name, mm)

            def out_a(t):
                pe.wait_ge(s_pt, t + 1)
                b = open_job(f"oA{t}")
                for h in range(HA):
                    kv = h // 4
                    for j in range(t + 1):
                        blk = h if t == 0 else 2 * h + j
                        mm = nc.tensor.matmul(b[64 * (h % 2):64 * (h % 2) + 64, (h // 2) * P:(h // 2 + 1) * P],
                                              va[:, j, kv * DA:(kv + 1) * DA], PT_f[:, blk * P:(blk + 1) * P],
                                              start=(j == 0), stop=(j == t))
                close_job(f"oA{t}", mm)

            def mix_b(t):
                pe.wait_ge(s_hb, t + 1)
                transposes(f"hb{t}T", [ob[:, t, h * P:(h + 1) * P] for h in range(HB)])

            for i in range(4):
                scores_a1(i)
            out_a(0)
            mix_b(0)
            pe.wait_ge(s_hmT, 4)
            unit_T(11, 6, 0, hmT)
            numerator(1)
            unit_T(12, 6, 256, hmT)
            used_after("U12")
            pe.wait_ge(s_pn, 2)
            transposes("tA1a", [Z_f[:, j * P:(j + 1) * P] for j in range(4)])
            transposes("tA1b", [Z_f[:, (4 + j) * P:(5 + j) * P] for j in range(4)])
            unit_T(13, 7, 0, hmT)
            transposes("tA1c", [Z_f[:, (8 + j) * P:(9 + j) * P] for j in range(4)])
            transposes("tA1d", [Z_f[:, (12 + j) * P:(13 + j) * P] for j in range(4)])
            mix_b(1)
            unit_T(14, 7, 256, hmT)
            used_after("U14")
            out_a(1)
            unit_N(15, 8, 0, hmT)
            pe.wait_ge(s_mixA, 2)
            pe.wait_ge(s_mixB, 2)
            for i, (q, t) in enumerate(((9, 0), (10, 0), (9, 1), (10, 1))):
                unit_N(19 + i, q, t, hT)

            def c_transposes(t):
                pe.wait_ge(s_x1n, t + 1)
                for half in range(2):
                    transposes(f"cT{t}{'ab'[half]}", [xn[:, t, (4 * half + k) * P:(4 * half + k + 1) * P] for k in range(4)])

            c_transposes(0)
            unit_N(16, 8, 1, hmT)
            used_after("U16", 3)
            c_transposes(1)
            pe.wait_ge(s_hc, 4)
            for i, (q, c) in enumerate(((11, 0), (11, 256), (12, 0), (12, 256))):
                unit_T(23 + i, q, c, hT)
                if c:
                    used_after(f"U{23 + i}")
            pe.wait_ge(s_unit, 5)
            for t in range(NT):
                for half in range(2):
                    name = f"sX{t}{'ab'[half]}"
                    b = open_job(name)
                    for g in range(2):
                        h = 2 * half + g
                        for c in range(2):
                            mm = nc.tensor.matmul(b[:, g * 256:(g + 1) * 256], cqT[:, 2 * h + c, t * P:(t + 1) * P],
                                                  ckT[:, 2 * h + c, :], start=(c == 0), stop=(c == 1))
                    close_job(name, mm)
            unit_N(17, 13, 0, hmT)
            unit_N(18, 13, 1, hmT)
            used_after("U18")
            for i in range(4):
                j, hp = i % 2, i // 2
                if i == 0:
                    pe.wait_ge(s_cpn, 2)
                transposes(f"TX{i}", [Z_f[:, (t * 4 + 2 * hp + g) * 256 + j * P:(t * 4 + 2 * hp + g) * 256 + (j + 1) * P]
                                      for g in range(2) for t in range(NT)])
            pe.wait_ge(s_unit, 6)
            for h in range(HX):
                pe.wait_ge(s_cpt, 2 * (h // 2) + 2)
                name = f"oX{h}"
                b = open_job(name)
                for c in range(2):
                    for j in range(NT):
                        i = 2 * (h // 2) + j
                        mm = nc.tensor.matmul(b[:, c * 256:(c + 1) * 256], cv[:, j, h * DX + c * P:h * DX + (c + 1) * P],
                                              PT_f[:, i * 512 + (h % 2) * 256:i * 512 + (h % 2 + 1) * 256],
                                              start=(j == 0), stop=(j == NT - 1))
                close_job(name, mm)
            pe.wait_ge(s_co, 1)
            for i, (q, t) in enumerate(((14, 0), (15, 0), (14, 1), (15, 1))):
                unit_N(27 + i, q, t, hT)
                if t:
                    used_after(f"U{27 + i}")
            moe_pe(pe, open_job, close_job, transposes)

        @block.gpsimd
        def _(pool):
            nc.gpsimd.memset(mhalf, -0.5).then_inc(s_mhalf, 1)
            nc.gpsimd.memset(table, 1.0).then_inc(s_table1, 1)
            nc.gpsimd.memset(u[:, :, 0:3], 0.0).then_inc(s_pad, 1)
            pool.wait_ge(s_mhalf, 1)
            roots = [(ms, rs, 0, 1), (ms, rs, 1, 1), (ms, rs, 2, 2), (hms, hrs, 0, 4), (hms, hrs, 4, 4)]
            roots += [(ms, rs, i, 1) for i in range(4, 10)]
            for i, (src, dst, lo, n) in enumerate(roots):
                pool.wait_ge(s_mean, i + 1)
                nc.gpsimd.tensor_tensor(dst[:, lo:lo + n], src[:, lo:lo + n], mhalf[:, 0:n], ALU.pow).then_inc(s_root, 1)

        @block.vector
        def _(dve):
            lane = Lane(dve, c_dve)
            did, settle = lane.did, lane.settle
            V = nc.vector

            def rms_rows(src, dst, lo, roots_before, data_sem, ready):
                for t in range(NT):
                    ready(t)
                    did(V.tensor_tensor_reduce(dst[:, t, :], src[:, t, :], src[:, t, :], 1.0, 0.0, ALU.mult, ALU.add,
                                               ss[:, lo + t:lo + t + 1]))
                    settle()
                    did(V.tensor_scalar(ms[:, lo + t:lo + t + 1], ss[:, lo + t:lo + t + 1], 1.0 / D, EPS, ALU.mult, ALU.add), s_mean)
                    dve.wait_ge(s_root, roots_before + t + 1)
                    did(V.tensor_scalar(dst[:, t, :], src[:, t, :], rs[:, lo + t:lo + t + 1], None, ALU.mult), data_sem)

            def to_feature_major(names, dst, r, data_sem):
                for t in range(NT):
                    for half in range(2):
                        name = names + f"{t}{'ab'[half]}"
                        b = filled(dve, name)
                        did(V.tensor_tensor(dst[:, 4 * half:4 * half + 4, t * P:(t + 1) * P], c3(b[:, :], 4),
                                            over(vecs[:, r + 4 * half:r + 4 * half + 4], P), ALU.mult), freed(name, "dve"))
                        settle()
                        did(dve.nop(), data_sem)

            rms_rows(x_sb, xn, 0, 0, s_xn, lambda t: dve.wait_ge(s_x[t], 16))
            b = filled(dve, "rows")
            did(V.tensor_copy(vecs, b[:, 0:R_ALL]), freed("rows", "dve"))
            settle()
            to_feature_major("xT", hT, R_MIX, s_hT)
            dve.wait_ge(s_small, 16)
            b = filled(dve, "gates")
            did(V.tensor_tensor(c3(gl, 2), c3(b[:, 0:16], 2), again(gbias, 2), ALU.add), freed("gates", "dve"))
            settle()
            did(V.scalar_tensor_tensor(c3(az[:, 0:8], 2), c3(gl, 2)[:, :, 4:8], -1.0, c3(gl, 2)[:, :, 4:8], ALU.mult, ALU.max), s_az)
            dve.wait_ge(s_l, 1)
            did(V.scalar_tensor_tensor(c3(lf, 2), c3(gl, 2)[:, :, 4:8], 0.0, c3(az[:, 0:8], 2), ALU.min, ALU.subtract), s_logf)
            b = filled(dve, "bcum")
            did(V.tensor_copy(b_sb, b[:, 0:8]))
            did(V.tensor_copy(bL, b[:, 8:12]), freed("bcum", "dve"))
            settle()
            did(V.tensor_tensor(c3(a_sb, 2), c3(gl, 2)[:, :, 0:4], c3(b_sb, 2), ALU.subtract))
            settle()
            for t in range(NT):
                did(V.tensor_tensor(c3(Dg[t], 4), again(ident, 4), over(a_sb[:, 4 * t:4 * t + 4], P), ALU.mult), s_diag)
            dve.wait_ge(s_mem, 16)
            for t in range(NT):
                did(V.tensor_tensor_reduce(Z_f[:, 1024:2048], mem_sb[:, t, :], mem_sb[:, t, :], 1.0, 0.0, ALU.mult, ALU.add,
                                           ss[:, 2 + t:3 + t]))
                settle()
            did(V.tensor_scalar(ms[:, 2:4], ss[:, 2:4], 1.0 / D, EPS, ALU.mult, ALU.add), s_mean)
            dve.wait_ge(s_root, 3)
            for t in range(NT):
                did(V.tensor_scalar(mem_sb[:, t, :], mem_sb[:, t, :], rs[:, 2 + t:3 + t], None, ALU.mult))
            settle()
            did(dve.nop(), s_memn)

            def conv(c0, n):
                dve.wait_ge(s_unit, n)
                for c in range(c0, c0 + 4):
                    did(V.tensor_scalar(y[:, c, :], u[:, c, 0:256], vecs[:, R_CW + c:R_CW + c + 1],
                                        vecs[:, R_CB + c:R_CB + c + 1], ALU.mult, ALU.add))
                for w in range(1, CONV):
                    settle()
                    for c in range(c0, c0 + 4):
                        did(V.scalar_tensor_tensor(y[:, c, :], u[:, c, w:w + 256],
                                                   vecs[:, R_CW + 8 * w + c:R_CW + 8 * w + c + 1], y[:, c, :],
                                                   ALU.mult, ALU.add))
                settle()
                did(dve.nop(), s_conv)

            def silu(c0, n, scale):
                yy = y_f[:, c0 * 256:(c0 + 4) * 256]
                dve.wait_ge(s_silu_e, n)
                did(V.tensor_scalar(silu_e, silu_e, 1.0, None, ALU.add))
                settle()
                did(V.reciprocal(silu_e, silu_e))
                settle()
                did(V.scalar_tensor_tensor(yy, yy, scale, silu_e, ALU.mult, ALU.mult))
                settle()
                did(dve.nop(), s_qk)

            def row_max(t):
                b = filled(dve, f"R{t}")
                did(V.tensor_tensor(c3(Rm, 4), c3(b[:, :], 4), again(cst[:, K_MTS:K_MTS + 128], 4), ALU.add), freed(f"R{t}", "dve"))
                settle()
                did(V.tensor_reduce(M[:, 4 * t:4 * t + 4], c3(Rm, 4), AX_X, ALU.max))
                settle()

            row_max(0)
            did(V.tensor_scalar(M[:, 0:4], M[:, 0:4], 0.0, None, ALU.max))
            settle()
            did(V.tensor_tensor(c3(Dg[0], 4), again(ident, 4), over(M[:, 0:4], P), ALU.mult), s_diag)
            row_max(1)
            conv(0, 1)
            def decay_pre(t):
                b = filled(dve, f"Mb{t}")
                did(V.scalar_tensor_tensor(c3(Dm[t], 4), c3(b[:, :], 4), -1.0, again(cst[:, K_MST:K_MST + 128], 4),
                                           ALU.mult, ALU.add))
                settle()
                did(V.tensor_tensor(c3(Dm[t], 4), c3(Dm[t], 4), over(a_sb[:, 4 * t:4 * t + 4], P), ALU.add), s_dpre)
                return b

            b = decay_pre(0)
            mlast = c3(b[:, :], 4)[:, :, 127]
            did(V.tensor_tensor(w0, a_sb[:, 0:4], mlast, ALU.subtract), s_dpre)
            did(V.tensor_tensor(mp1, bL, mlast, ALU.add), freed("Mb0", "dve"))
            settle()
            did(V.tensor_tensor(M[:, 4:8], M[:, 4:8], mp1, ALU.max))
            settle()
            did(V.tensor_tensor(c3(Dg[1], 4), again(ident, 4), over(M[:, 4:8], P), ALU.mult), s_diag)
            did(V.tensor_tensor(em, b_sb, M, ALU.add), s_empre)
            silu(0, 1, DB ** -0.5)
            b = decay_pre(1)
            did(V.scalar_tensor_tensor(c3(aib, 4), c3(b[:, :], 4), -1.0, over(mp1, P), ALU.mult, ALU.add), freed("Mb1", "dve"))
            settle()
            did(dve.nop(), s_dpre)
            conv(4, 2)
            silu(4, 2, 1.0)

            def attn_z(name, lo, n, heads):
                b = filled(dve, name)
                did(V.scalar_tensor_tensor(Z_f[:, lo:lo + 512].rearrange("p (h j) -> p h j", j=n), b[:, :].rearrange("p (h j) -> p h j", j=n),
                                           DA ** -0.5, Tb[:, heads:heads + 512 // n, 256 - n:256], ALU.mult, ALU.add), freed(name, "dve"))

            def attn_max(t, n):
                settle()
                o = 8 * t
                did(V.tensor_reduce(amax[:, o:o + 8], Z_f[:, 0:8 * n].rearrange("p (h j) -> p h j", j=n), AX_X, ALU.max))
                settle()
                did(V.tensor_tensor(amax[:, o:o + 8], amax[:, o:o + 8], sinks, ALU.max))
                settle()
                did(V.tensor_scalar(anm[:, o:o + 8], amax[:, o:o + 8], -1.0, None, ALU.mult))
                did(V.tensor_tensor(ask[:, o:o + 8], sinks, amax[:, o:o + 8], ALU.subtract))
                settle()
                did(dve.nop(), s_z)

            def attn_normalise(t, n):
                dve.wait_ge(s_pe_a, t + 1)
                o = 8 * t
                did(V.tensor_tensor(ard[:, o:o + 8], asum[:, o:o + 8], ask[:, o:o + 8], ALU.add))
                settle()
                did(V.reciprocal(ard[:, o:o + 8], ard[:, o:o + 8]))
                settle()
                z = Z_f[:, 0:8 * n].rearrange("p (h j) -> p h j", j=n)
                did(V.tensor_tensor(z, z, over(ard[:, o:o + 8], n), ALU.mult))
                settle()
                did(dve.nop(), s_pn)

            dve.wait_ge(s_T, 16)
            attn_z("sA0a", 0, 128, 0)
            attn_z("sA0b", 512, 128, 4)
            attn_max(0, 128)

            def weights_b(t, n):
                dve.wait_ge(s_D, n)
                b = filled(dve, f"sc{t}")
                did(V.tensor_tensor(Pm[t], b[:, :], Dm[t], ALU.mult), freed(f"sc{t}", "dve"))
                settle()
                did(dve.nop(), s_P)

            weights_b(0, 1)
            weights_b(1, 3)
            dve.wait_ge(s_D, 4)
            q1 = y[:, 0:4, P:T]
            did(V.tensor_tensor(q1, q1, c3(aib, 4), ALU.mult), s_q1)
            to_feature_major("mT", hmT, R_MEM, s_hmT)
            attn_normalise(0, 128)

            b0 = filled(dve, "num0")
            did(V.tensor_tensor(c3(vb[:, 0, :], 4), c3(vb[:, 0, :], 4), over(w0, P), ALU.mult), s_vw)

            def head_out(t, sig_done):
                o = ob[:, t, :]
                dve.wait_ge(s_sig, t + 1)
                did(V.tensor_scalar(o, o, 1.0, None, ALU.add))
                settle()
                did(V.reciprocal(o, o))
                nb = filled(dve, f"num{t}")
                db = filled(dve, f"den{t}")
                dve.wait_ge(s_em, 1)
                h4 = slice(4 * t, 4 * t + 4)
                did(V.tensor_copy(dd[:, h4], db[:, 0:4]), freed(f"den{t}", "dve"))
                settle()
                did(V.scalar_tensor_tensor(dd[:, h4], dd[:, h4], -1.0, dd[:, h4], ALU.mult, ALU.max))
                settle()
                did(V.tensor_tensor(dd[:, h4], dd[:, h4], em[:, h4], ALU.max))
                settle()
                did(V.reciprocal(dd[:, h4], dd[:, h4]))
                settle()
                did(V.tensor_tensor(c3(o, 4), c3(o, 4), over(dd[:, h4], P), ALU.mult))
                settle()
                did(V.tensor_tensor(o, o, nb[:, :], ALU.mult), freed(f"num{t}", "dve"))
                settle()
                did(V.tensor_tensor(Dg[0], o, o, ALU.mult))
                settle()
                did(V.tensor_reduce(hss[:, h4], c3(Dg[0], 4), AX_X, ALU.add))
                settle()
                did(V.tensor_scalar(hms[:, h4], hss[:, h4], 1.0 / DB, EPS, ALU.mult, ALU.add), s_mean)
                dve.wait_ge(s_root, 4 + t)
                did(V.tensor_tensor(c3(o, 4), c3(o, 4), over(hrs[:, h4], P), ALU.mult), s_hb)

            head_out(0, 1)
            b = filled(dve, "Cst")
            did(V.tensor_copy(Cs, b[:, :]), freed("Cst", "dve"))
            b = filled(dve, "nst")
            did(V.tensor_copy(n_sb, b[:, 0:4]), freed("nst", "dve"))
            settle()
            did(dve.nop(), s_C)
            dve.wait_ge(s_filled[jobs["tA0b"][0]], jobs["tA0b"][1] + 1)
            attn_z("sA1a", 0, 256, 0)
            attn_z("sA1b", 512, 256, 2)
            attn_z("sA1c", 1024, 256, 4)
            attn_z("sA1d", 1536, 256, 6)
            attn_max(1, 256)

            def mix_b(t):
                name = f"hb{t}T"
                b = filled(dve, name)
                did(V.tensor_tensor(hT[:, 4:8, t * P:(t + 1) * P], c3(b[:, :], 4), over(vecs[:, R_MLSTM:R_MLSTM + 4], P),
                                    ALU.mult), freed(name, "dve"))
                settle()
                did(dve.nop(), s_mixB)

            mix_b(0)
            attn_normalise(1, 256)
            head_out(1, 2)
            mix_b(1)
            did(dve.nop(), s_left)

            def residual(n0, t):
                for half in range(2):
                    name = f"U{n0 + 2 * t + half}"
                    b = filled(dve, name)
                    xs = x_sb[:, t, half * 512:(half + 1) * 512]
                    did(V.tensor_tensor(xs, xs, b[:, :], ALU.add), freed(name, "dve"))
                settle()

            rms_rows(x_sb, xn, 4, 5, s_x1n, lambda t: residual(19, t))
            to_feature_major("cT", hT, R_CROSS, s_hc)
            for t in range(NT):
                for half in range(2):
                    b = filled(dve, f"sX{t}{'ab'[half]}")
                    o = slice(t * 4 + 2 * half, t * 4 + 2 * half + 2)
                    did(V.tensor_reduce(cmax[:, o], c3(b[:, :], 2), AX_X, ALU.max))
                    settle()
                    did(V.tensor_scalar(cmax[:, o], cmax[:, o], -DX ** -0.5, None, ALU.mult), s_cm)
            for t in range(NT):
                dve.wait_ge(s_cp, t + 1)
                o = slice(t * 4, t * 4 + 4)
                did(V.reciprocal(csum[:, o], csum[:, o]))
                settle()
                z = Z_f[:, t * 1024:(t + 1) * 1024].rearrange("p (h j) -> p h j", h=HX)
                did(V.tensor_tensor(z, z, over(csum[:, o], 256), ALU.mult), s_cpn)

            def residual_co(t):
                residual(27, t)
                if t == 0:
                    did(V.memset(zeros, 0.0), s_zero)

            rms_rows(x_sb, xn, 6, 7, s_x2n, residual_co)
            moe_dve(dve, lane, rms_rows, to_feature_major)


_INS = ["x", "mem", "rel_bias_table", "w_in", "w_out", "w_cq", "w_ck", "w_cv", "w_co",
        "w_exp_gate", "w_exp_up", "w_exp_down", "norm_final"]


def constants():
    import math
    import numpy as np

    i, j = np.arange(P)[:, None], np.arange(P)[None, :]
    c = np.zeros((P, K_ALL), np.float32)
    c[:, K_ID:K_ID + 128] = i == j
    c[:, K_TRIU:K_TRIU + 128] = i <= j
    c[:, K_STRICT:K_STRICT + 128] = i < j
    c[:, K_MTS:K_MTS + 128] = np.where(j <= i, 0.0, NEG)
    c[:, K_MST:K_MST + 128] = np.where(i <= j, 0.0, NEG)
    c[:, K_ONES:K_ONES + 128] = 1.0
    c[:, K_SLOT:K_SLOT + 128] = j % SLOTS
    c[:, K_RG:K_RG + 4] = NG - np.arange(NG)
    c[:, K_RE:K_RE + 32] = NE - np.arange(NE)
    bands = np.zeros((33, 384), np.float32)
    for m in range(384):
        n = 255 - m
        if 0 <= n < 128:
            big = 16 + int(np.float32(np.log(np.float32(max(n, 1)) / np.float32(16))) / np.float32(math.log(8.0)) * np.float32(16))
            bands[n if n < 16 else min(big, 31), m] = 1.0
        else:
            bands[32, m] = NEG
    return c, bands


def kernel(**inputs):
    import numpy as _np
    import concourse.bacc as _bacc
    from concourse import mybir as _mybir
    from concourse.bass_utils import run_bass_kernel_spmd as _run

    nc = _bacc.Bacc("TRN2", target_bir_lowering=False, num_devices=1)
    arrays, args = {}, []
    flat = {name: _np.asarray(inputs[name]).reshape(-1) for name in inputs}
    groups = {
        "vectors": _np.concatenate([flat[n] for n in ("norm_mix", "norm_cross", "norm_mem", "norm_moe", "mlstm_norm",
                                                      "conv_w", "conv_b")]).reshape(R_ALL, P),
        "biases": _np.concatenate([flat[n] for n in ("gate_bias_i", "gate_bias_f", "attn_sinks", "b_router_group",
                                                     "b_router_expert")]),
        "routers": _np.concatenate([_np.asarray(inputs["w_router_group"])[0], _np.asarray(inputs["w_router_expert"])[0]], axis=1),
    }
    for name in [*_INS, *groups]:
        a = _np.ascontiguousarray(groups[name] if name in groups else inputs[name])
        arrays[f"in_{name}_dram"] = a
        args.append(nc.dram_tensor(f"in_{name}_dram", a.shape, _mybir.dt.from_np(a.dtype), kind="ExternalInput").ap())
    for name, a in zip(("tile", "bands"), constants()):
        arrays[f"const_{name}_dram"] = a
        args.append(nc.dram_tensor(f"const_{name}_dram", a.shape, _mybir.dt.from_np(a.dtype), kind="ExternalInput").ap())
    args.append(nc.dram_tensor("out_0_dram", (1, T, D), _mybir.dt.from_np(_np.dtype("float32")), kind="ExternalOutput").ap())
    hymba_layer(nc, *args)
    r = _run(nc, [arrays], core_ids=[0])
    return r.results[0]["out_0_dram"]
```

```python
from contextlib import ExitStack

import concourse.bass as bass
from concourse import mybir

F32 = mybir.dt.float32
I32 = mybir.dt.int32
ALU = mybir.AluOpType
ACT = mybir.ActivationFunctionType
AX_X = mybir.AxisListType.X

P = 128
T = 256
NT = T // P
D = 1024
KD = D // P
HA, DA = 8, 64
HB, DB = 4, 128
HX, DX = 4, 256
CONV = 4
NG, EG = 4, 8
NE = NG * EG
SLOTS = 64
BLOCKS = T // SLOTS
NEG = -1e30
EPS = 1e-6
RING = 6
FRONT = 16

C_QA, C_KA, C_VA = 0, 512, 640
C_QB, C_KB, C_VB, C_OB, C_G = 768, 1280, 1792, 2304, 2816

K_ID, K_TRIU, K_STRICT, K_MTS, K_MST, K_ONES, K_SLOT, K_RG, K_RE = (
    0, 128, 256, 384, 512, 640, 768, 896, 900)
K_ALL = 932
R_MIX, R_CROSS, R_MEM, R_MOE, R_MLSTM, R_CW, R_CB, R_ALL = 0, 8, 16, 24, 32, 36, 68, 76
B_ALL = 8 + 8 + 36

ORDER_OF_JOBS = """
    dve rows xT0a xT0b xT1a xT1b    act U0    dve gates    act U1    dve bcum    act bias U2
    dve R0 R1    act U3    dve Mb0    act U4    dve Mb1    act U5 U6    dve sA0a sA0b    act U7 kct    dve sc0 sc1
    dve mT0a mT0b mT1a mT1b    act U8 U9    dve num0 den0    act tA0a tA0b U10
    dve Cst nst sA1a sA1c sA1b sA1d    act oA0    dve hb0T    act U11    dve num1 den1
    act U12 tA1a tA1b U13 tA1c tA1d    dve hb1T    act U14 oA1 U15    dve U19 U20 U21    act cT0a cT0b
    dve U22    act U16    dve cT1a    act cT1b    U23 U24 U25 U26 sX0a sX0b sX1a sX1b U17 U18 TX0 TX1 TX2 TX3
    oX0 oX1 oX2 oX3    dve U27 U28 U29    act zT0a zT0b    dve U30 logit0 zT1a    act zT1b
    dve logit1 pos"""
FIXED_BANK = {"zT0a": 6, "zT0b": 7, "logit0": 4, "zT1a": 6, "zT1b": 7, "logit1": 5, "pos": 6}


def list_jobs():
    turn, by, out = {True: 0, False: 0}, None, []
    for word in ORDER_OF_JOBS.split():
        if word in ("dve", "act"):
            by = word
            continue
        wide = word[0] in "UTx"
        bank = FIXED_BANK.get(word, turn[wide] % 4 + (0 if wide else 4))
        turn[wide] += 1
        out.append((word, bank, by))
    return out


JOBS = list_jobs()
LAST_UNIT = ["U1", "U3", "U5", "U6", "U8", "U10", "U12", "U14", "U16", "U21", "U22", "U24", "U26", "U18", "U29", "U30"]


def job_table():
    seen, freed, last, out = {}, {}, {}, {}
    for name, bank, by in JOBS:
        out[name] = (bank, seen.get(bank, 0), last.get(bank))
        seen[bank] = seen.get(bank, 0) + 1
        freed[bank, by] = freed.get((bank, by), 0) + 1
        last[bank] = (by, freed[bank, by])
    return out, last


class Lane:

    def __init__(self, eng, chain):
        self.eng, self.chain, self.count, self.last = eng, chain, {}, None

    def did(self, ins, sem=None):
        sem = self.chain if sem is None else sem
        self.count[sem.name] = self.count.get(sem.name, 0) + 1
        ins.then_inc(sem, 1)
        self.last = (sem, self.count[sem.name])

    def settle(self):
        self.eng.wait_ge(*self.last)


def hymba_layer(nc, x, mem, rel_bias_table, w_in, w_out, w_cq, w_ck, w_cv, w_co, w_exp_gate, w_exp_up,
                w_exp_down, norm_final, vectors, biases, routers, const_tile, const_bands, out):
    jobs, last_of_bank = job_table()
    with ExitStack() as ctx:
        def sb(name, shape, dt=F32):
            return ctx.enter_context(nc.sbuf_tensor(name, shape, dt))

        def sem(name):
            return ctx.enter_context(nc.semaphore(name))

        ring = [sb(f"ring{i}", [P, 8, 512]) for i in range(RING)]
        arena = sb("arena", [P, 28300])
        used = [0]

        def take(n):
            used[0] += n
            assert used[0] <= 28300, used
            return arena[:, used[0] - n:used[0]]

        x_sb = take(2048).rearrange("p (t d) -> p t d", t=NT)
        xn_f = take(2048)
        xn = xn_f.rearrange("p (t d) -> p t d", t=NT)
        hT = take(2048).rearrange("p (k t) -> p k t", k=KD)
        yT_f = take(4096)
        y_f, T_f = yT_f[:, 0:2048], yT_f[:, 2048:4096]
        hvo_f = take(4096)
        hmT = hvo_f[:, 0:2048].rearrange("p (k t) -> p k t", k=KD)
        vb = hvo_f[:, 2048:3072].rearrange("p (t d) -> p t d", t=NT)
        ob = hvo_f[:, 3072:4096].rearrange("p (t d) -> p t d", t=NT)
        uck_f = take(2072 + 2048)
        u_f, ckT_f = uck_f[:, 0:2072], uck_f[:, 2072:4120]
        ckT = ckT_f.rearrange("p (c t) -> p c t", c=8)
        zp_f = take(4096)
        Z_f, PT_f = zp_f[:, 0:2048], zp_f[:, 2048:4096]
        cv_f = take(2048)
        cv = cv_f.rearrange("p (t d) -> p t d", t=NT)
        qkv_f = take(1024 + 256 + 256)
        qaT = qkv_f[:, 0:1024].rearrange("p (c t) -> p c t", c=4)
        kaT = qkv_f[:, 1024:1280]
        va = qkv_f[:, 1280:1536].rearrange("p (t d) -> p t d", t=NT)
        wg8 = take(64).rearrange("p (k c) -> p k c", k=KD)
        wr = take(8 * 36).rearrange("p (k c) -> p k c", k=KD)
        cst = take(K_ALL)
        vecs = take(R_ALL)
        tiny_f = take(400)

        mem_sb = PT_f.rearrange("p (t d) -> p t d", t=NT)
        rows = Z_f[0:R_ALL, 0:128]
        bands = Z_f[0:33, 128:512]
        table = Z_f[0:33, 512:520]
        bias_sb = Z_f[0:8, 520:904]
        silu_e = Z_f[:, 1024:2048]
        u = u_f.rearrange("p (c t) -> p c t", c=8)
        y = y_f.rearrange("p (c t) -> p c t", c=8)
        Tb = T_f.rearrange("p (h j) -> p h j", h=HA)
        Dg = [xn_f[:, 0:512], xn_f[:, 512:1024]]
        Rm = xn_f[:, 1024:1536]
        kct = xn_f[:, 1536:2048]
        Dm = [u_f[:, 0:512], u_f[:, 512:1024]]
        Pm = [u_f[:, 1024:1536], u_f[:, 1536:2048]]
        Cs = Rm
        aib = Dg[1]
        cqT = u_f[:, 0:2048].rearrange("p (c t) -> p c t", c=8)

        tiny_used = [0]

        def tiny(n):
            tiny_used[0] += n
            assert tiny_used[0] <= 400
            return tiny_f[:, tiny_used[0] - n:tiny_used[0]]

        ss, ms, rs = tiny(20), tiny(10), tiny(10)
        mhalf = tiny(8)
        small = tiny(B_ALL)
        gbias, sinks, rbias = small[:, 0:8], small[:, 8:16], small[:, 16:52]
        gl, az, lf = tiny(16), tiny(16), tiny(8)
        b_sb, bL, a_sb = tiny(8), tiny(4), tiny(8)
        M, mp1, w0 = tiny(8), tiny(4), tiny(4)
        em, dd, hss, hms, hrs = tiny(8), tiny(8), tiny(8), tiny(8), tiny(8)
        n_sb = tiny(4)
        amax, anm, asum, ask, ard = tiny(16), tiny(16), tiny(16), tiny(16), tiny(16)
        cmax, csum = tiny(8), tiny(8)
        oms, mark = tiny(4), tiny(2)

        def c3(ap, a):
            return ap.rearrange("p (a b) -> p a b", a=a)

        ident = cst[:, K_ID:K_ID + 128]
        ones = cst[:, K_ONES:K_ONES + 128]

        def over(ap, n):
            return ap.unsqueeze(2).to_broadcast([ap.shape[0], ap.shape[1], n])

        def again(ap, m):
            return ap.unsqueeze(1).to_broadcast([ap.shape[0], m, ap.shape[1]])

        bank = [ctx.enter_context(nc.psum_tensor(f"bank{i}", [P, 512], F32)) for i in range(8)]

        skew = nc.dram_tensor("skew_dram", [HA, P, 384], F32, kind="Internal").ap()

        s_x = [sem(f"s_x{t}") for t in range(NT)]
        s_ident, s_cst, s_mem, s_rows = sem("s_ident"), sem("s_cst"), sem("s_mem"), sem("s_rows")
        s_small, s_table, s_wgates, s_router = sem("s_small"), sem("s_table"), sem("s_wgates"), sem("s_router")
        s_ring = [sem(f"s_ring{i}") for i in range(RING)]
        s_skew, s_T = sem("s_skew"), sem("s_T")
        s_out = sem("s_out")
        s_filled = [sem(f"s_filled{i}") for i in range(8)]
        s_freed = {(i, e): sem(f"s_freed{i}_{e}") for i in range(8) for e in ("dve", "act")}
        c_dve, c_act = sem("c_dve"), sem("c_act")
        s_mhalf, s_pad, s_table1 = sem("s_mhalf"), sem("s_pad"), sem("s_table1")
        s_mean, s_root = sem("s_mean"), sem("s_root")
        s_xn, s_memn, s_x1n, s_x2n = sem("s_xn"), sem("s_memn"), sem("s_x1n"), sem("s_x2n")
        s_hT, s_hmT, s_hc, s_hz = sem("s_hT"), sem("s_hmT"), sem("s_hc"), sem("s_hz")
        s_hc_act, s_hz_act = sem("s_hc_act"), sem("s_hz_act")
        s_unit = sem("s_unit")
        s_conv, s_silu_e, s_qk = sem("s_conv"), sem("s_silu_e"), sem("s_qk")
        s_az, s_l, s_logf = sem("s_az"), sem("s_l"), sem("s_logf")
        s_diag = sem("s_diag")
        s_dpre, s_D = sem("s_dpre"), sem("s_D")
        s_P = sem("s_P")
        s_kct, s_vw, s_q1, s_C = sem("s_kct"), sem("s_vw"), sem("s_q1"), sem("s_C")
        s_empre, s_em = sem("s_empre"), sem("s_em")
        s_sig, s_hb = sem("s_sig"), sem("s_hb")
        s_z, s_pe_a, s_pn, s_pt = sem("s_z"), sem("s_pe_a"), sem("s_pn"), sem("s_pt")
        s_mixA, s_mixB = sem("s_mixA"), sem("s_mixB")
        s_cm, s_cp, s_cpn, s_cpt, s_co = sem("s_cm"), sem("s_cp"), sem("s_cpn"), sem("s_cpt"), sem("s_co")

        def filled(eng, name):
            b, before, _ = jobs[name]
            eng.wait_ge(s_filled[b], before + 1)
            return bank[b]

        def freed(name, by):
            assert (name, jobs[name][0], by) in JOBS
            return s_freed[jobs[name][0], by]

        def w_cols(w, c0, n):
            return w[0, :, c0:c0 + n].rearrange("(k p) n -> p k n", p=P)

        def as_slot(ap):
            return ap[:, 0:4096].rearrange("p (a b) -> p a b", a=8)

        places = [as_slot(yT_f), ring[4], ring[5], ring[0], as_slot(uck_f), ring[1], as_slot(hvo_f), as_slot(zp_f),
                  ring[2], ring[3]]
        N_PL = len(places)
        gain_f = hvo_f[:, 0:1024]
        hT_f = hT.rearrange("p k t -> p (k t)")
        xe, gu = hT_f[:, 0:1024].rearrange("p (k s) -> p k s", k=KD), [hT_f[:, 1024:1536], hT_f[:, 1536:2048]]
        posm = cv_f[:, 0:2 * (BLOCKS * NE + 2)].rearrange("p (t n) -> p t n", t=NT)
        comb = cv_f[:, 260:516].rearrange("p (t n) -> p t n", t=NT)
        Pg = cv_f[:, 516:772].rearrange("p (t s) -> p t s", t=NT)
        O = cv_f[:, 772:1796]
        Sg = qkv_f[:, 1280:1536].rearrange("p (t s) -> p t s", t=NT)
        E_f = [qkv_f[:, 0:256], qkv_f[:, 256:512]]
        hE = [qkv_f[:, 512:768], qkv_f[:, 768:1024]]
        ST = qkv_f[:, 1024:1280]
        at = [0]

        def r3(n):
            at[0] += 2 * n
            return qkv_f[:, at[0] - 2 * n:at[0]].rearrange("p (t n) -> p t n", t=NT)

        lg, gx, gq, ohg, el, eq, oh1, oh2, sel, posr = (
            r3(36), r3(4), r3(4), r3(4), r3(32), r3(32), r3(32), r3(32), r3(32), r3(32))
        gmax, gsum, mr, e1, e2, rr, g1, g2 = (r3(1) for _ in range(8))
        cmaxf = qkv_f[:, at[0]:at[0] + 1]
        cmaxi = sb("cmaxi", [P, 1], I32)
        PAIRS = NE // 2

        s_left = sem("s_left")
        s_we = [[sem(f"s_we{i}_{h}") for h in range(2)] for i in range(N_PL)]
        s_gain = sem("s_gain")
        s_logit_e, s_route, s_route_e, s_M, s_cnt = sem("s_logit_e"), sem("s_route"), sem("s_route_e"), sem("s_M"), sem("s_cnt")
        s_pos = sem("s_pos")
        s_y = sem("s_y")
        s_all_o, s_all_st = sem("s_all_o"), sem("s_all_st")
        s_sq, s_outn = sem("s_sq"), sem("s_outn")
        s_pg, s_sg = sem("s_pg"), sem("s_sg")
        s_gat, s_xe = sem("s_gat"), sem("s_xe")
        s_gat_half, s_xe_half = sem("s_gat_half"), sem("s_xe_half")
        s_gu_half, s_down_half = sem("s_gu_half"), sem("s_down_half")
        s_gu, s_gue = sem("s_gu"), sem("s_gue")
        s_t, s_ee, s_h = sem("s_t"), sem("s_ee"), sem("s_h")
        s_stt, s_st = sem("s_stt"), sem("s_st")
        s_down, s_o, s_comb = sem("s_down"), sem("s_o"), sem("s_comb")
        c_moe = sem("c_moe")

        def all_pairs(eng, one_pair, steps=1):
            def block_of(blk, G0):
                one_pair(G0, blk, first=True)
                with eng.Fori(0, (PAIRS - 1) // steps) as r:
                    for i in range(steps):
                        one_pair(G0 + steps * r + i + 1, blk, r, i)

            block_of(0, 0)
            eng.wait_ge(s_cnt, 1)
            most = eng.value_load(cmaxi[0:1, 0:1], min_val=0, max_val=T)
            with eng.If(most > SLOTS):
                with eng.Fori(1, BLOCKS) as blk:
                    block_of(blk, PAIRS * blk)

        def load_half(sp, e, which, place, half):
            w, k, n = ((w_exp_gate, 8, 512), (w_exp_up, 8, 512), (w_exp_down, 4, 1024))[which]
            rows_of = slice(half * k // 2 * P, (half + 1) * k // 2 * P)
            src = w[0, bass.ds(e, 1), rows_of, :].rearrange("o (k p) n -> p (o k) n", p=P)
            dst = places[place % N_PL][:, 4 * half:4 * half + 4, :].rearrange("p a b -> p (a b)").rearrange("p (k n) -> p k n", k=k // 2)
            sp.dma_start(dst, src).then_inc(s_we[place % N_PL][half], 16)

        def reached(eng, sem_, n):
            if not isinstance(n, int) or n > 0:
                eng.wait_ge(sem_, n)

        ORDER = ((0, 0), (0, 1), (1, 0), (1, 1), (0, 2), (1, 2))

        LAP = N_PL // 2
        LAPS = (PAIRS - 1) // LAP

        def moe_sync(sp):
            def load(pair, j, n, halves=(0, 1)):
                e, which = ORDER[j]
                for half in halves:
                    load_half(sp, 2 * pair + e, which, n, half)

            for n, q in ((1, 10), (2, 11), (3, 12), (5, 13),
                         (4, 13),
                         (6, 13),
                         (7, None), (8, 14), (9, 15)):
                if q is None:
                    sp.wait_ge(s_co, HX)
                else:
                    filled(sp, LAST_UNIT[q])
                load(n // 6, n % 6, n)

            def one_pair(G, pair, i, first_j=0):
                for j in range(first_j, 6, 2):
                    for half in range(2):
                        for jj in (j, j + 1):
                            gu_, down_ = ((s_gu_half, s_down_half), (s_gu, s_down))[half]
                            sem_, count = ((gu_, 2 * G - 2), (down_, G - 1), (gu_, 2 * G - 1))[j // 2]
                            reached(sp, sem_, count)
                            load(pair, jj, 6 * (i + 1) + jj, (half,))

            for i in range(LAP):
                one_pair(i + 1, i + 1, i, first_j=0 if i else 4)
            with sp.Fori(1, LAPS) as r:
                for i in range(LAP):
                    one_pair(LAP * r + i + 1, LAP * r + i + 1, i)
            sp.wait_ge(s_cnt, 1)
            with sp.If(sp.value_load(cmaxi[0:1, 0:1], min_val=0, max_val=T) > SLOTS):
                with sp.Fori(1, BLOCKS) as blk:
                    sp.wait_ge(s_down, PAIRS * blk)
                    for j in range(6):
                        load(0, j, j)
                    with sp.Fori(0, LAPS) as r:
                        for i in range(LAP):
                            one_pair(PAIRS * blk + LAP * r + i + 1, LAP * r + i + 1, i)
                sp.wait_ge(s_down, PAIRS * BLOCKS - 1)
            sp.wait_ge(s_down, PAIRS - 1)
            sp.dma_start(gain_f, norm_final.partition_broadcast(P)).then_inc(s_gain, 16)
            for t in range(NT):
                for half in range(2):
                    cols = slice(half * 512, (half + 1) * 512)
                    sp.wait_ge(s_outn, 2 * t + half + 1)
                    sp.dma_start(out[0, t * P:(t + 1) * P, cols], xn[:, t, cols]).then_inc(s_out, 16)
            sp.wait_ge(s_out, 64)

        def moe_act(act, lane, evacuate):
            did, settle = lane.did, lane.settle
            for name in ("zT0a", "zT0b", "zT1b"):
                evacuate(name, hT, R_MOE, s_hz_act)
            act.wait_ge(s_route, 1)
            did(nc.scalar.activation(gq, gx, ACT.Exp), s_logit_e)
            act.wait_ge(s_route, 2)
            did(nc.scalar.activation(rr, rr, ACT.Exp), s_route_e)

            def one_pair(G, blk, r=None, i=None, first=False):
                for e in range(2):
                    n = 2 * G + e + 1
                    act.wait_ge(s_gu, n)
                    act.wait_ge(s_t, n)
                    nc.scalar.copy(gu[e], bank[6][:, :]).then_inc(s_gue, 1)
                    act.wait_ge(s_t, n + 2)
                    g_t = bank[7][:, :].rearrange("p (f s) -> p f s", f=4)[:, :, 0:64]
                    nc.scalar.activation(E_f[e].rearrange("p (f s) -> p f s", f=4), g_t, ACT.Exp, scale=-1.0).then_inc(s_ee, 1)
                reached(act, s_down, G + 1)
                reached(act, s_comb, G)
                nc.scalar.copy(O[:, 0:512], bank[4][:, :])
                nc.scalar.copy(O[:, 512:1024], bank[5][:, :]).then_inc(s_o, 1)

            all_pairs(act, one_pair)
            nc.scalar.copy(mark[:, 0:1], ones[:, 0:1]).then_inc(s_all_o, 1)
            for t in range(NT):
                act.wait_ge(s_y, t + 1)
                for half in range(2):
                    did(nc.scalar.activation(xn[:, t, half * 512:(half + 1) * 512], bank[2 * t + half][:, :], ACT.Square,
                                             scale=D ** -0.5, accum_out=oms[:, 2 * t + half:2 * t + half + 1]), s_sq)

        def moe_pe(pe, open_job, close_job, z_transposes):

            def begin_y(t):
                for half in range(2):
                    i = 2 * t + half
                    before = last_of_bank[i]
                    pe.wait_ge(s_freed[i, before[0]], before[1])
                    nc.tensor.matmul(bank[i][:, :], ident, x_sb[:, t, half * 512:(half + 1) * 512], start=True, stop=True)

            for t in range(NT):
                if t:
                    z_transposes(1)
                b = open_job(f"logit{t}")
                for k in range(KD):
                    if k == 0:
                        pe.wait_ge(*((s_hz, 1) if t else (s_hz_act, 2)))
                    if k == 4 and t:
                        pe.wait_ge(s_hz_act, 3)
                    mm = nc.tensor.matmul(b[:, 0:36], hT[:, k, t * P:(t + 1) * P], wr[:, k, :], start=(k == 0), stop=(k == KD - 1))
                close_job(f"logit{t}", mm)
            begin_y(0)
            begin_y(1)
            pe.wait_ge(s_M, 1)
            b = open_job("pos")
            strict = cst[:, K_STRICT:K_STRICT + 128]
            nc.tensor.matmul(b[:, 0:32], strict, sel[:, 0, :], start=True, stop=True)
            nc.tensor.matmul(b[:, 32:64], ones, sel[:, 0, :], start=True, stop=False)
            nc.tensor.matmul(b[:, 32:64], strict, sel[:, 1, :], start=False, stop=True)
            nc.tensor.matmul(b[:, 64:96], ones, sel[:, 0, :], start=True, stop=False)
            close_job("pos", nc.tensor.matmul(b[:, 64:96], ones, sel[:, 1, :], start=False, stop=True))
            pe.wait_ge(s_freed[7, last_of_bank[7][0]], last_of_bank[7][1])
            for i in range(2):
                pe.nop().then_inc(s_t, 1)

            def expert_half(blk, r, i, j, half):
                n = j if r is None else 6 * (i + 1) + j
                before = (LAPS * 6 * LAP // N_PL + (n % N_PL < 6)) * blk
                lap = 0 if r is None else 6 * LAP // N_PL * r
                pe.wait_ge(s_we[n % N_PL][half], 16 * (before + lap + n // N_PL + 1))
                return places[n % N_PL]

            def gather(G):
                reached(pe, s_pg, G + 1)
                for k in range(KD):
                    for t in range(NT):
                        mm = nc.tensor.matmul(bank[4 + k // 4][:, (k % 4) * P:(k % 4 + 1) * P], xn[:, t, k * P:(k + 1) * P],
                                              Pg[:, t, :], start=(t == 0), stop=(t == NT - 1))
                    if k == 3:
                        mm.then_inc(s_gat_half, 1)
                mm.then_inc(s_gat, 1)

            def gate_up(G, blk, r, i, e):
                for k in range(KD):
                    if k % 4 == 0:
                        reached(pe, s_xe if k else s_xe_half, G + 1)
                        w = [expert_half(blk, r, i, 2 * e + m, k // 4) for m in range(2)]
                    for half in range(2):
                        mm = nc.tensor.matmul(bank[6][64 * half:64 * half + 64, :], xe[:, k, 64 * e:64 * e + 64], w[half][:, k, :],
                                              start=(k == 0), stop=(k == KD - 1))
                    if k == 3:
                        mm.then_inc(s_gu_half, 1)
                mm.then_inc(s_gu, 1)

            def turn(G, e):
                reached(pe, s_gue, 2 * G + e + 1)
                reached(pe, s_h, 2 * G + e)
                for f in range(4):
                    mm = nc.tensor.transpose(bank[7][:, f * P:(f + 1) * P], gu[e][:, f * P:(f + 1) * P], ident)
                mm.then_inc(s_t, 1)

            def combine(t, half):
                return nc.tensor.matmul(bank[2 * t + half][:, :], ST[:, t * P:(t + 1) * P], O[:, half * 512:(half + 1) * 512],
                                        start=False, stop=False, skip_group_check=True)

            pe.wait_ge(s_pos, 1)
            gather(0)

            def one_pair(G, blk, r=None, i=None, first=False):
                reached(pe, s_st, G)
                gate_up(G, blk, r, i, 0)
                reached(pe, s_o, G)
                gather(G + 1)
                turn(G, 0)
                gate_up(G, blk, r, i, 1)
                turn(G, 1)
                reached(pe, s_sg, G + 1)
                for t in range(NT):
                    mm = nc.tensor.transpose(bank[6][:, t * P:(t + 1) * P], Sg[:, t, :], ident)
                mm.then_inc(s_stt, 1)
                if not (first and isinstance(G, int)):
                    reached(pe, s_o, G)
                    reached(pe, s_st, G)
                    for t in range(NT):
                        for half in range(2):
                            mm = combine(t, half)
                    mm.then_inc(s_comb, 1)
                reached(pe, s_h, 2 * G + 2)
                reached(pe, s_xe, G + 2)
                for f in range(4):
                    if f % 2 == 0:
                        w = [expert_half(blk, r, i, 4 + e, f // 2)[:, :, :].rearrange("p a b -> p (a b)") for e in range(2)]
                    for half in range(2):
                        for e in range(2):
                            lo = f * 1024 + half * 512
                            mm = nc.tensor.matmul(bank[4 + half][64 * e:64 * e + 64, :], hE[e][:, f * 64:(f + 1) * 64],
                                                  w[e][:, lo:lo + 512], start=(f == 0), stop=(f == 3))
                    if f == 1:
                        mm.then_inc(s_down_half, 1)
                mm.then_inc(s_down, 1)

            all_pairs(pe, one_pair, steps=LAP)
            pe.wait_ge(s_all_o, 1)
            pe.wait_ge(s_all_st, 1)
            for t in range(NT):
                for half in range(2):
                    mm = combine(t, half)
                mm.then_inc(s_y, 1)

        def moe_dve(dve, lane, rms_rows, evacuate):
            did, settle = lane.did, lane.settle
            V = nc.vector
            evacuate("zT1a", hT, R_MOE, s_hz)

            def tt(o, a, b, op, sem_=None):
                did(V.tensor_tensor(o, a, b, op), sem_)
                settle()

            def wide(ap, n):
                return ap.to_broadcast([P, NT, n])

            def first_of(values, top, ranks, onehot):
                n = values.shape[2]
                for t in range(NT):
                    did(V.scalar_tensor_tensor(onehot[:, t, :], values[:, t, :], top[:, t, :], ranks, ALU.is_equal, ALU.mult))
                settle()
                did(V.tensor_reduce(mr, onehot, AX_X, ALU.max))
                settle()
                tt(onehot, onehot, wide(mr, n), ALU.is_equal)

            ranks_g, ranks_e = cst[:, K_RG:K_RG + 4], cst[:, K_RE:K_RE + 32]
            for t in range(NT):
                b = filled(dve, f"logit{t}")
                did(V.tensor_tensor(lg[:, t, :], b[:, 0:36], rbias, ALU.add), freed(f"logit{t}", "dve"))
            settle()
            did(V.tensor_reduce(gmax, lg[:, :, 0:4], AX_X, ALU.max))
            settle()
            did(V.tensor_tensor(gx, lg[:, :, 0:4], wide(gmax, 4), ALU.subtract), s_route)
            first_of(lg[:, :, 0:4], gmax, ranks_g, ohg)
            did(V.tensor_scalar(ohg, ohg, 1.0, -NEG, ALU.subtract, ALU.mult))
            settle()
            for t in range(NT):
                did(V.tensor_tensor(c3(el[:, t, :], 4), c3(lg[:, t, 4:36], 4), over(ohg[:, t, :], EG), ALU.add))
            settle()
            did(V.tensor_reduce(e1, el, AX_X, ALU.max))
            settle()
            first_of(el, e1, ranks_e, oh1)
            did(V.scalar_tensor_tensor(eq, oh1, 2 * NEG, el, ALU.mult, ALU.add))
            settle()
            did(V.tensor_reduce(e2, eq, AX_X, ALU.max))
            settle()
            did(V.tensor_tensor(rr, e2, e1, ALU.subtract), s_route)
            first_of(eq, e2, ranks_e, oh2)
            tt(sel, oh1, oh2, ALU.add, s_M)
            b = filled(dve, "pos")
            did(V.tensor_reduce(cmaxf, b[:, 64:96], AX_X, ALU.max))
            did(V.scalar_tensor_tensor(posr, c3(b[:, 0:64], 2), 1.0, sel, ALU.add, ALU.mult), s_pos)
            settle()
            did(V.tensor_scalar(posm[:, :, 0:NE], posr, -1.0, None, ALU.add))
            settle()

            def gates_and_blocks():
                for blk in range(1, BLOCKS + 1):
                    n = NE if blk < BLOCKS else 2
                    did(V.tensor_scalar(posm[:, :, blk * NE:blk * NE + n], posr[:, :, 0:n], -1.0 - blk * SLOTS, None, ALU.add))
                did(V.tensor_copy(cmaxi[:, :], cmaxf), s_cnt)
                dve.wait_ge(s_logit_e, 1)
                did(V.tensor_reduce(gsum, gq, AX_X, ALU.add))
                dve.wait_ge(s_route_e, 1)
                did(V.tensor_scalar(g1, rr, 1.0, None, ALU.add))
                settle()
                tt(g1, g1, gsum, ALU.mult)
                did(V.reciprocal(g1, g1))
                settle()
                tt(g2, g1, rr, ALU.mult)
                tt(oh1, oh1, wide(g1, 32), ALU.mult)
                tt(oh2, oh2, wide(g2, 32), ALU.mult)
                for blk in range(BLOCKS):
                    did(V.tensor_tensor(comb[:, :, blk * NE:(blk + 1) * NE], oh1, oh2, ALU.add))
                settle()

            slots = cst[:, K_SLOT:K_SLOT + 64]

            def select(G):
                for e in range(2):
                    for t in range(NT):
                        ins = V.tensor_scalar(Pg[:, t, 64 * e:64 * e + 64], slots, posm[:, t, bass.ds(2 * G + e, 1)], None, ALU.is_equal)
                ins.then_inc(s_pg, 1)

            def evacuate_gathered(G):
                for half, (got, sent) in enumerate(((s_gat_half, s_xe_half), (s_gat, s_xe))):
                    reached(dve, got, G + 1)
                    V.tensor_tensor(xe[:, 4 * half:4 * half + 4, :], c3(bank[4 + half][:, :], 4),
                                    over(vecs[:, R_MOE + 4 * half:R_MOE + 4 * half + 4], P), ALU.mult).then_inc(sent, 1)

            select(0)
            gates_and_blocks()
            evacuate_gathered(0)

            PER = 6

            def one_pair(G, blk, r=None, i=None, first=False):
                step = [0]

                def chain(ins):
                    step[0] += 1
                    ins.then_inc(c_moe, 1)
                    dve.wait_ge(c_moe, PER * G + step[0])

                reached(dve, s_gat, G + 1)
                select(G + 1)
                reached(dve, s_stt, G)
                for e in range(2):
                    for t in range(NT):
                        ins = V.tensor_scalar(Sg[:, t, 64 * e:64 * e + 64], slots, posm[:, t, bass.ds(2 * G + e, 1)],
                                              comb[:, t, bass.ds(2 * G + e, 1)], ALU.is_equal, ALU.mult)
                ins.then_inc(s_sg, 1)
                for e in range(2):
                    if e:
                        reached(dve, s_gu, 2 * G + 2)
                        evacuate_gathered(G + 1)
                    reached(dve, s_ee, 2 * G + e + 1)
                    turned = bank[7][:, :].rearrange("p (f s) -> p f s", f=4)
                    E4 = E_f[e].rearrange("p (f s) -> p f s", f=4)
                    chain(V.tensor_scalar(E_f[e], E_f[e], 1.0, None, ALU.add))
                    chain(V.reciprocal(E_f[e], E_f[e]))
                    chain(V.tensor_tensor(E4, E4, turned[:, :, 0:64], ALU.mult))
                    reached(dve, s_down, G)
                    V.tensor_tensor(hE[e].rearrange("p (f s) -> p f s", f=4), E4, turned[:, :, 64:128], ALU.mult).then_inc(s_h, 1)
                reached(dve, s_stt, G + 1)
                reached(dve, s_comb, G)
                V.tensor_copy(ST, bank[6][:, 0:256]).then_inc(s_st, 1)
                assert step[0] == PER

            all_pairs(dve, one_pair)
            V.tensor_copy(mark[:, 1:2], ones[:, 0:1]).then_inc(s_all_st, 1)
            dve.wait_ge(s_gain, 16)
            for t in range(NT):
                dve.wait_ge(s_sq, 2 * t + 2)
                did(V.scalar_tensor_tensor(ms[:, 8 + t:9 + t], oms[:, 2 * t:2 * t + 1], EPS, oms[:, 2 * t + 1:2 * t + 2],
                                           ALU.add, ALU.add), s_mean)
                dve.wait_ge(s_root, 10 + t)
                for half in range(2):
                    cols = slice(half * 512, (half + 1) * 512)
                    did(V.scalar_tensor_tensor(xn[:, t, cols], bank[2 * t + half][:, :], rs[:, 8 + t:9 + t], gain_f[:, cols],
                                               ALU.mult, ALU.mult), s_outn)

        block = ctx.enter_context(nc.Block())

        @block.sync
        def _(sp):
            sp.dma_start(x_sb[:, 0, :], x[0, 0:P, :]).then_inc(s_x[0], 16)
            sp.dma_start(ident, const_tile[:, K_ID:K_ID + 128]).then_inc(s_ident, 16)
            sp.dma_start(x_sb[:, 1, :], x[0, P:T, :]).then_inc(s_x[1], 16)
            sp.dma_start(rows, vectors).then_inc(s_rows, 16)
            front = [w_cols(w_in, C_QB, 512), w_cols(w_in, C_KB, 512), w_cols(w_in, C_QA, 512),
                     w_cols(w_in, C_KA, 256), w_cols(w_in, C_VB, 512), w_cols(w_in, C_OB, 512),
                     w_cols(w_ck, 0, 512), w_cols(w_ck, 512, 512), w_cols(w_cv, 0, 512),
                     w_cols(w_out, 0, 512), w_cols(w_out, 512, 512), w_cols(w_cq, 0, 512), w_cols(w_cq, 512, 512),
                     w_cols(w_cv, 512, 512), w_cols(w_co, 0, 512), w_cols(w_co, 512, 512)]
            assert len(front) == FRONT
            for q, src in enumerate(front):
                if q >= RING:
                    filled(sp, LAST_UNIT[q - RING])
                sp.dma_start(ring[q % RING][:, :, 0:src.shape[2]], src).then_inc(s_ring[q % RING], 16)
                if q == 0:
                    sp.dma_start(wg8, w_cols(w_in, C_G, 8)).then_inc(s_wgates, 16)
                    sp.dma_start(small, biases.partition_broadcast(P)).then_inc(s_small, 16)
                    sp.dma_start(cst[:, K_TRIU:], const_tile[:, K_TRIU:]).then_inc(s_cst, 16)
                    sp.wait_ge(s_table1, 1)
                    sp.dma_start(table[0:32, :], rel_bias_table).then_inc(s_table, 16)
                    sp.dma_start(bands, const_bands).then_inc(s_table, 16)
                    sp.dma_start(mem_sb, mem[0].rearrange("(t p) d -> p t d", p=P)).then_inc(s_mem, 16)
                if q == 13:
                    sp.wait_ge(s_left, 1)
                    for half in range(2):
                        load_half(sp, 0, 0, 0, half)
                if q == 3:
                    sp.dma_start(wr, routers.rearrange("(k p) c -> p k c", p=P)).then_inc(s_router, 16)
            moe_sync(sp)

        @block.scalar
        def _(act):
            lane = Lane(act, c_act)
            did, settle = lane.did, lane.settle
            def unit(n, dst):
                b = filled(act, f"U{n}")
                did(nc.scalar.copy(dst, b[:, :].rearrange("p (a b) -> p a b", a=2) if len(dst.shape) == 3 else b[:, :]),
                    freed(f"U{n}", "act"))

            def unit_done():
                settle()
                did(act.nop(), s_unit)

            act.wait_ge(s_pad, 1)
            unit(0, u[:, 0:2, 3:259])
            act.wait_ge(s_az, 1)
            did(nc.scalar.activation(az[:, 8:16], az[:, 0:8], ACT.Exp, scale=-1.0))
            settle()
            did(nc.scalar.activation(az[:, 0:8], az[:, 8:16], ACT.Ln, bias=1.0), s_l)
            unit(1, u[:, 2:4, 3:259])
            unit_done()
            bk = filled(act, "bias")
            did(nc.scalar.copy(bias_sb, bk[0:8, 0:384]), freed("bias", "act"))
            settle()
            act.dma_start(skew, bias_sb.unsqueeze(1).to_broadcast([8, P, 384])).then_inc(s_skew, 16)
            unit(2, u[:, 4:6, 3:259])
            act.wait_ge(s_conv, 1)
            did(nc.scalar.activation(silu_e, y_f[:, 0:1024], ACT.Exp, scale=-1.0), s_silu_e)
            unit(3, u[:, 6:8, 3:259])
            unit_done()
            act.wait_ge(s_dpre, 1)
            did(nc.scalar.activation(Dm[0], Dm[0], ACT.Exp), s_D)
            act.wait_ge(s_dpre, 2)
            did(nc.scalar.activation(w0, w0, ACT.Exp), s_D)
            act.wait_ge(s_skew, 16)
            act.dma_start(Tb, bass.AP(tensor=skew.tensor, offset=127,
                                      ap=[[383, P], [P * 384, HA], [1, 256]])).then_inc(s_T, 16)
            act.wait_ge(s_empre, 1)
            did(nc.scalar.activation(em, em, ACT.Exp, scale=-1.0), s_em)
            unit(4, qaT[:, 0:2, :])
            act.wait_ge(s_conv, 2)
            act.wait_ge(s_qk, 1)
            did(nc.scalar.activation(silu_e, y_f[:, 1024:2048], ACT.Exp, scale=-1.0), s_silu_e)
            act.wait_ge(s_dpre, 3)
            did(nc.scalar.activation(Dm[1], Dm[1], ACT.Exp), s_D)
            act.wait_ge(s_dpre, 4)
            did(nc.scalar.activation(aib, aib, ACT.Exp), s_D)
            unit(5, qaT[:, 2:4, :])
            b6 = filled(act, "U6")
            did(nc.scalar.copy(kaT, b6[:, 0:256]))
            did(nc.scalar.copy(va, b6[:, 256:512].rearrange("p (t d) -> p t d", t=NT)), freed("U6", "act"))
            unit_done()

            def attn_exp(t):
                act.wait_ge(s_z, t + 1)
                n = 128 if t == 0 else 256
                for h in range(HA):
                    zt = Z_f[:, h * n:(h + 1) * n]
                    did(nc.scalar.activation(zt, zt, ACT.Exp, bias=anm[:, 8 * t + h:8 * t + h + 1],
                                             accum_out=asum[:, 8 * t + h:8 * t + h + 1]))
                did(nc.scalar.activation(ask[:, 8 * t:8 * t + 8], ask[:, 8 * t:8 * t + 8], ACT.Exp), s_pe_a)

            attn_exp(0)
            unit(7, vb[:, 0, :])
            b = filled(act, "kct")
            did(nc.scalar.copy(kct, b[:, :]), freed("kct", "act"))
            settle()
            did(act.nop(), s_kct)
            unit(8, vb[:, 1, :])
            unit_done()

            def sigmoid_e(n, t):
                b = filled(act, f"U{n}")
                did(nc.scalar.activation(ob[:, t, :], b[:, :], ACT.Exp, scale=-1.0), freed(f"U{n}", "act"))
                settle()
                did(act.nop(), s_sig)

            sigmoid_e(9, 0)

            def pt_copy(name, dst):
                b = filled(act, name)
                did(nc.scalar.copy(dst, b[:, :]), freed(name, "act"))

            pt_copy("tA0a", PT_f[:, 0:512])
            pt_copy("tA0b", PT_f[:, 512:1024])
            settle()
            did(act.nop(), s_pt)
            sigmoid_e(10, 1)

            def mix_a(t):
                b = filled(act, f"oA{t}")
                did(nc.scalar.copy(hT[:, 0:4, t * P:(t + 1) * P], b[:, :].rearrange("p (c i) -> p c i", c=4)),
                    freed(f"oA{t}", "act"))
                settle()
                did(act.nop(), s_mixA)

            mix_a(0)
            unit(11, ckT[:, 0:2, :])
            attn_exp(1)
            unit(12, ckT[:, 2:4, :])
            pt_copy("tA1a", PT_f[:, 0:512])
            pt_copy("tA1b", PT_f[:, 512:1024])
            unit(13, ckT[:, 4:6, :])
            pt_copy("tA1c", PT_f[:, 1024:1536])
            pt_copy("tA1d", PT_f[:, 1536:2048])
            settle()
            did(act.nop(), s_pt)
            unit(14, ckT[:, 6:8, :])
            mix_a(1)
            unit(15, cv[:, 0, 0:512])
            def evacuate(name, dst, r, data_sem):
                t, half = int(name[2]), "ab".index(name[3])
                b = filled(act, name)
                for k in range(4):
                    ins = nc.scalar.activation(dst[:, 4 * half + k, t * P:(t + 1) * P], b[:, k * P:(k + 1) * P], ACT.Copy,
                                               scale=vecs[:, r + 4 * half + k:r + 4 * half + k + 1])
                    did(ins, freed(name, "act") if k == 3 else None)
                settle()
                did(act.nop(), data_sem)

            evacuate("cT0a", hT, R_CROSS, s_hc_act)
            evacuate("cT0b", hT, R_CROSS, s_hc_act)
            unit(16, cv[:, 1, 0:512])
            evacuate("cT1b", hT, R_CROSS, s_hc_act)
            for i in range(4):
                unit(23 + i, cqT[:, 2 * i:2 * i + 2, :])
                if i % 2:
                    unit_done()
            for t in range(NT):
                for half in range(2):
                    act.wait_ge(s_cm, 2 * t + half + 1)
                    b = filled(act, f"sX{t}{'ab'[half]}")
                    for g in range(2):
                        h = 2 * half + g
                        ins = nc.scalar.activation(
                            Z_f[:, (t * 4 + h) * 256:(t * 4 + h + 1) * 256], b[:, g * 256:(g + 1) * 256], ACT.Exp,
                            bias=cmax[:, t * 4 + h:t * 4 + h + 1], scale=DX ** -0.5,
                            accum_out=csum[:, t * 4 + h:t * 4 + h + 1])
                        did(ins, freed(f"sX{t}{'ab'[half]}", "act") if g else None)
                settle()
                did(act.nop(), s_cp)
            unit(17, cv[:, 0, 512:1024])
            unit(18, cv[:, 1, 512:1024])
            unit_done()
            for i in range(4):
                pt_copy(f"TX{i}", PT_f[:, i * 512:(i + 1) * 512])
                settle()
                did(act.nop(), s_cpt)
            for i in range(4):
                b = filled(act, f"oX{i}")
                did(nc.scalar.copy(hT[:, 2 * i:2 * i + 2, :], b[:, :].rearrange("p (c i) -> p c i", c=2)),
                    freed(f"oX{i}", "act"))
                settle()
                did(act.nop(), s_co)
            moe_act(act, lane, evacuate)

        @block.tensor
        def _(pe):
            def open_job(name):
                b, _, before = jobs[name]
                if before:
                    pe.wait_ge(s_freed[b, before[0]], before[1])
                return bank[b]

            def close_job(name, mm):
                mm.then_inc(s_filled[jobs[name][0]], 1)

            def slot(q):
                pe.wait_ge(s_ring[q % RING], 16 * (q // RING + 1))
                return ring[q % RING]

            def transposes(name, parts, n=128):
                b = open_job(name)
                for i, src in enumerate(parts):
                    mm = nc.tensor.transpose(b[:, i * n:(i + 1) * n], src, ident)
                close_job(name, mm)

            def unit_T(n, q, c0, src, late={}):
                w = slot(q)
                b = open_job(f"U{n}")
                for c in range(2):
                    for k in range(KD):
                        if c == 0 and k in late:
                            pe.wait_ge(*late[k])
                        mm = nc.tensor.matmul(b[:, c * 256:(c + 1) * 256], w[:, k, c0 + c * 128:c0 + (c + 1) * 128],
                                              src[:, k, :], start=(k == 0), stop=(k == KD - 1))
                close_job(f"U{n}", mm)
                return mm

            def unit_N(n, q, t, src, late={}):
                w = slot(q)
                b = open_job(f"U{n}")
                for k in range(KD):
                    if k in late:
                        pe.wait_ge(*late[k])
                    mm = nc.tensor.matmul(b[:, :], src[:, k, t * P:(t + 1) * P], w[:, k, :],
                                          start=(k == 0), stop=(k == KD - 1))
                close_job(f"U{n}", mm)

            pe.wait_ge(s_ident, 16)
            pe.wait_ge(s_rows, 16)
            b = open_job("rows")
            close_job("rows", nc.tensor.transpose(b[:, 0:R_ALL], rows, ident[0:R_ALL, 0:R_ALL]))
            for t in range(NT):
                pe.wait_ge(s_xn, t + 1)
                for half in range(2):
                    transposes(f"xT{t}{'ab'[half]}", [xn[:, t, (4 * half + k) * P:(4 * half + k + 1) * P] for k in range(4)])
            pe.wait_ge(s_hT, 3)
            def row_of(name, diag, n):
                pe.wait_ge(s_diag, n)
                b = open_job(name)
                close_job(name, nc.tensor.matmul(b[:, :], ones, diag, start=True, stop=True))

            unit_T(0, 0, 0, hT, late={4: (s_hT, 4)})
            pe.wait_ge(s_wgates, 16)
            b = open_job("gates")
            for t in range(NT):
                for k in range(KD):
                    mm = nc.tensor.matmul(b[:, t * 8:(t + 1) * 8], hT[:, k, t * P:(t + 1) * P], wg8[:, k, :],
                                          start=(k == 0), stop=(k == KD - 1))
            close_job("gates", mm)
            unit_T(1, 0, 256, hT)
            pe.wait_ge(s_cst, 16)
            pe.wait_ge(s_logf, 1)
            b = open_job("bcum")
            for t in range(NT):
                nc.tensor.matmul(b[:, t * 4:(t + 1) * 4], cst[:, K_TRIU:K_TRIU + 128], lf[:, t * 4:(t + 1) * 4],
                                 start=True, stop=True)
            close_job("bcum", nc.tensor.matmul(b[:, 8:12], ones, lf[:, 0:4], start=True, stop=True))
            pe.wait_ge(s_table1, 1)
            pe.wait_ge(s_table, 32)
            b = open_job("bias")
            close_job("bias", nc.tensor.matmul(b[0:8, 0:384], table, bands, start=True, stop=True))
            unit_T(2, 1, 0, hT)
            row_of("R0", Dg[0], 1)
            row_of("R1", Dg[1], 2)
            unit_T(3, 1, 256, hT)
            row_of("Mb0", Dg[0], 3)

            def unit_qa(n, c0):
                w = slot(2)
                b = open_job(f"U{n}")
                for c in range(2):
                    for k in range(KD):
                        for half in range(2):
                            h = 4 * half + c0 + c
                            mm = nc.tensor.matmul(b[64 * half:64 * half + 64, c * 256:(c + 1) * 256],
                                                  w[:, k, h * DA:(h + 1) * DA], hT[:, k, :],
                                                  start=(k == 0), stop=(k == KD - 1))
                close_job(f"U{n}", mm)

            unit_qa(4, 0)
            row_of("Mb1", Dg[1], 4)
            unit_qa(5, 2)
            w = slot(3)
            b = open_job("U6")
            for k in range(KD):
                nc.tensor.matmul(b[:, 0:256], w[:, k, 0:128], hT[:, k, :], start=(k == 0), stop=(k == KD - 1))
            for t in range(NT):
                for k in range(KD):
                    mm = nc.tensor.matmul(b[:, 256 + t * P:256 + (t + 1) * P], hT[:, k, t * P:(t + 1) * P],
                                          w[:, k, 128:256], start=(k == 0), stop=(k == KD - 1))
            close_job("U6", mm)
            pe.wait_ge(s_unit, 3)
            b = [open_job("sA0a"), open_job("sA0b")]
            for c in range(4):
                for g in range(2):
                    mm = nc.tensor.matmul(b[g][:, c * 128:(c + 1) * 128], qaT[64 * g:64 * g + 64, c, 0:P],
                                          kaT[64 * g:64 * g + 64, 0:P], start=True, stop=True)
                    if c == 3:
                        close_job(f"sA0{'ab'[g]}", mm)

            def scores_b(t):
                b = open_job(f"sc{t}")
                for h in range(HB):
                    mm = nc.tensor.matmul(b[:, h * P:(h + 1) * P], y[:, 4 + h, t * P:(t + 1) * P],
                                          y[:, h, t * P:(t + 1) * P], start=True, stop=True)
                close_job(f"sc{t}", mm)

            unit_N(7, 4, 0, hT)
            pe.wait_ge(s_qk, 2)
            transposes("kct", [y[:, 4 + h, 0:P] for h in range(HB)])
            scores_b(0)
            scores_b(1)
            pe.wait_ge(s_memn, 1)
            for t in range(NT):
                for half in range(2):
                    transposes(f"mT{t}{'ab'[half]}", [mem_sb[:, t, (4 * half + k) * P:(4 * half + k + 1) * P] for k in range(4)])
            unit_N(8, 4, 1, hT)
            unit_N(9, 5, 0, hT)

            def numerator(t):
                pe.wait_ge(s_P, t + 1)
                pe.wait_ge(s_unit, 4)
                if t:
                    pe.wait_ge(s_C, 1)
                    pe.wait_ge(s_q1, 1)
                b = open_job(f"num{t}")
                for h in range(HB):
                    mm = nc.tensor.matmul(b[:, h * P:(h + 1) * P], Pm[t][:, h * P:(h + 1) * P], vb[:, t, h * P:(h + 1) * P],
                                          start=True, stop=(t == 0))
                    if t:
                        mm = nc.tensor.matmul(b[:, h * P:(h + 1) * P], y[:, h, P:T], Cs[:, h * P:(h + 1) * P],
                                              start=False, stop=True)
                close_job(f"num{t}", mm)
                b = open_job(f"den{t}")
                for h in range(HB):
                    mm = nc.tensor.matmul(b[:, h:h + 1], Pm[t][:, h * P:(h + 1) * P], ones[:, 0:1],
                                          start=True, stop=(t == 0))
                    if t:
                        mm = nc.tensor.matmul(b[:, h:h + 1], y[:, h, P:T], n_sb[:, h:h + 1], start=False, stop=True)
                close_job(f"den{t}", mm)

            numerator(0)

            def p_transposes(names, per):
                for i, name in enumerate(names):
                    transposes(name, [Z_f[:, (4 * i + j) * P:(4 * i + j + 1) * P] for j in range(4)])

            pe.wait_ge(s_pn, 1)
            p_transposes(["tA0a", "tA0b"], 4)
            unit_N(10, 5, 1, hT)
            pe.wait_ge(s_vw, 1)
            pe.wait_ge(s_kct, 1)
            b = open_job("Cst")
            for h in range(HB):
                mm = nc.tensor.matmul(b[:, h * P:(h + 1) * P], kct[:, h * P:(h + 1) * P], vb[:, 0, h * P:(h + 1) * P],
                                      start=True, stop=True)
            close_job("Cst", mm)
            b = open_job("nst")
            for h in range(HB):
                mm = nc.tensor.matmul(b[:, h:h + 1], kct[:, h * P:(h + 1) * P], w0[:, h:h + 1], start=True, stop=True)
            close_job("nst", mm)

            def scores_a1(i):
                names = [f"sA1{'abcd'[i + 2 * kv]}" for kv in range(2)]
                b = [open_job(name) for name in names]
                for g in range(2):
                    for kv in range(2):
                        mm = nc.tensor.matmul(b[kv][:, g * 256:(g + 1) * 256], qaT[64 * kv:64 * kv + 64, 2 * i + g, P:T],
                                              kaT[64 * kv:64 * kv + 64, :], start=True, stop=True)
                        if g == 1:
                            close_job(names[kv], mm)

            def out_a(t):
                pe.wait_ge(s_pt, t + 1)
                b = open_job(f"oA{t}")
                for h, j in [(2 * c + g, j) for c in range(HA // 2) for j in range(t + 1) for g in range(2)]:
                    kv = h // 4
                    blk = h if t == 0 else 2 * h + j
                    mm = nc.tensor.matmul(b[64 * (h % 2):64 * (h % 2) + 64, (h // 2) * P:(h // 2 + 1) * P],
                                          va[:, j, kv * DA:(kv + 1) * DA], PT_f[:, blk * P:(blk + 1) * P],
                                          start=(j == 0), stop=(j == t))
                close_job(f"oA{t}", mm)

            def mix_b(t):
                pe.wait_ge(s_hb, t + 1)
                transposes(f"hb{t}T", [ob[:, t, h * P:(h + 1) * P] for h in range(HB)])

            for i in range(2):
                scores_a1(i)
            out_a(0)
            mix_b(0)
            pe.wait_ge(s_hmT, 4)
            unit_T(11, 6, 0, hmT)
            numerator(1)
            unit_T(12, 6, 256, hmT)
            pe.wait_ge(s_pn, 2)
            transposes("tA1a", [Z_f[:, j * P:(j + 1) * P] for j in range(4)])
            transposes("tA1b", [Z_f[:, (4 + j) * P:(5 + j) * P] for j in range(4)])
            unit_T(13, 7, 0, hmT)
            transposes("tA1c", [Z_f[:, (8 + j) * P:(9 + j) * P] for j in range(4)])
            transposes("tA1d", [Z_f[:, (12 + j) * P:(13 + j) * P] for j in range(4)])
            mix_b(1)
            unit_T(14, 7, 256, hmT)
            out_a(1)
            unit_N(15, 8, 0, hmT)
            pe.wait_ge(s_mixA, 2)
            pe.wait_ge(s_mixB, 2)
            def c_transposes(t):
                pe.wait_ge(s_x1n, t + 1)
                for half in range(2):
                    transposes(f"cT{t}{'ab'[half]}", [xn[:, t, (4 * half + k) * P:(4 * half + k + 1) * P] for k in range(4)])

            unit_N(19, 9, 0, hT)
            unit_N(20, 10, 0, hT)
            unit_N(21, 9, 1, hT)
            c_transposes(0)
            unit_N(22, 10, 1, hT)
            unit_N(16, 8, 1, hmT)
            c_transposes(1)
            pe.wait_ge(s_hc, 1)
            pe.wait_ge(s_hc_act, 2)
            for i, (q, c) in enumerate(((11, 0), (11, 256), (12, 0), (12, 256))):
                unit_T(23 + i, q, c, hT, late={} if i else {4: (s_hc_act, 3)})
            for t in range(NT):
                for half in range(2):
                    pe.wait_ge(s_unit, 6 if t else 5 + half)
                    name = f"sX{t}{'ab'[half]}"
                    b = open_job(name)
                    for g in range(2):
                        h = 2 * half + g
                        for c in range(2):
                            mm = nc.tensor.matmul(b[:, g * 256:(g + 1) * 256], cqT[:, 2 * h + c, t * P:(t + 1) * P],
                                                  ckT[:, 2 * h + c, :], start=(c == 0), stop=(c == 1))
                    close_job(name, mm)
            unit_N(17, 13, 0, hmT)
            unit_N(18, 13, 1, hmT)
            for i in range(4):
                j, hp = i % 2, i // 2
                if i == 0:
                    pe.wait_ge(s_cpn, 2)
                transposes(f"TX{i}", [Z_f[:, (t * 4 + 2 * hp + g) * 256 + j * P:(t * 4 + 2 * hp + g) * 256 + (j + 1) * P]
                                      for g in range(2) for t in range(NT)])
            pe.wait_ge(s_unit, 7)
            for h in range(HX):
                pe.wait_ge(s_cpt, 2 * (h // 2) + 2)
                name = f"oX{h}"
                b = open_job(name)
                for c in range(2):
                    for j in range(NT):
                        i = 2 * (h // 2) + j
                        mm = nc.tensor.matmul(b[:, c * 256:(c + 1) * 256], cv[:, j, h * DX + c * P:h * DX + (c + 1) * P],
                                              PT_f[:, i * 512 + (h % 2) * 256:i * 512 + (h % 2 + 1) * 256],
                                              start=(j == 0), stop=(j == NT - 1))
                close_job(name, mm)

            def z_transposes(t):
                pe.wait_ge(s_x2n, t + 1)
                for half in range(2):
                    transposes(f"zT{t}{'ab'[half]}", [xn[:, t, (4 * half + k) * P:(4 * half + k + 1) * P] for k in range(4)])

            unit_N(27, 14, 0, hT, late={2 * h: (s_co, h + 1) for h in range(HX)})
            unit_N(28, 15, 0, hT)
            unit_N(29, 14, 1, hT)
            z_transposes(0)
            unit_N(30, 15, 1, hT)
            moe_pe(pe, open_job, close_job, z_transposes)

        @block.gpsimd
        def _(pool):
            nc.gpsimd.memset(mhalf, -0.5).then_inc(s_mhalf, 1)
            nc.gpsimd.memset(table, 1.0).then_inc(s_table1, 1)
            nc.gpsimd.memset(u[:, :, 0:3], 0.0).then_inc(s_pad, 1)
            pool.wait_ge(s_mhalf, 1)
            roots = [(ms, rs, 0, 1), (ms, rs, 1, 1), (ms, rs, 2, 2), (hms, hrs, 0, 4), (hms, hrs, 4, 4)]
            roots += [(ms, rs, i, 1) for i in range(4, 10)]
            for i, (src, dst, lo, n) in enumerate(roots):
                pool.wait_ge(s_mean, i + 1)
                nc.gpsimd.tensor_tensor(dst[:, lo:lo + n], src[:, lo:lo + n], mhalf[:, 0:n], ALU.pow).then_inc(s_root, 1)

        @block.vector
        def _(dve):
            lane = Lane(dve, c_dve)
            did, settle = lane.did, lane.settle
            V = nc.vector

            def rms_rows(src, dst, lo, roots_before, data_sem, ready):
                for t in range(NT):
                    for half in range(2):
                        cols = slice(half * 512, (half + 1) * 512)
                        ready(t, half)
                        did(V.tensor_tensor_reduce(dst[:, t, cols], src[:, t, cols], src[:, t, cols], 1.0 / D, 0.0,
                                                   ALU.mult, ALU.add, ss[:, 2 * (lo + t) + half:2 * (lo + t) + half + 1]))
                    settle()
                    did(V.scalar_tensor_tensor(ms[:, lo + t:lo + t + 1], ss[:, 2 * (lo + t):2 * (lo + t) + 1], EPS,
                                               ss[:, 2 * (lo + t) + 1:2 * (lo + t) + 2], ALU.add, ALU.add), s_mean)
                    dve.wait_ge(s_root, roots_before + t + 1)
                    did(V.tensor_scalar(dst[:, t, :], src[:, t, :], rs[:, lo + t:lo + t + 1], None, ALU.mult), data_sem)

            def evacuate(name, dst, r, data_sem):
                t, half = int(name[2]), "ab".index(name[3])
                b = filled(dve, name)
                did(V.tensor_tensor(dst[:, 4 * half:4 * half + 4, t * P:(t + 1) * P], c3(b[:, :], 4),
                                    over(vecs[:, r + 4 * half:r + 4 * half + 4], P), ALU.mult), freed(name, "dve"))
                settle()
                did(dve.nop(), data_sem)

            def to_feature_major(names, dst, r, data_sem):
                for t in range(NT):
                    for half in "ab":
                        evacuate(f"{names}{t}{half}", dst, r, data_sem)

            rms_rows(x_sb, xn, 0, 0, s_xn, lambda t, half: dve.wait_ge(s_x[t], 16))
            b = filled(dve, "rows")
            did(V.tensor_copy(vecs, b[:, 0:R_ALL]), freed("rows", "dve"))
            settle()
            to_feature_major("xT", hT, R_MIX, s_hT)
            dve.wait_ge(s_mem, 16)
            for t in range(NT):
                did(V.tensor_tensor_reduce(Z_f[:, 1024:2048], mem_sb[:, t, :], mem_sb[:, t, :], 1.0, 0.0, ALU.mult, ALU.add,
                                           ss[:, 4 + t:5 + t]))
                settle()
            did(V.tensor_scalar(ms[:, 2:4], ss[:, 4:6], 1.0 / D, EPS, ALU.mult, ALU.add), s_mean)
            dve.wait_ge(s_root, 3)
            for t in range(NT):
                did(V.tensor_scalar(mem_sb[:, t, :], mem_sb[:, t, :], rs[:, 2 + t:3 + t], None, ALU.mult))
            settle()
            did(dve.nop(), s_memn)
            dve.wait_ge(s_small, 16)
            b = filled(dve, "gates")
            did(V.tensor_tensor(c3(gl, 2), c3(b[:, 0:16], 2), again(gbias, 2), ALU.add), freed("gates", "dve"))
            settle()
            did(V.scalar_tensor_tensor(c3(az[:, 0:8], 2), c3(gl, 2)[:, :, 4:8], -1.0, c3(gl, 2)[:, :, 4:8], ALU.mult, ALU.max), s_az)
            dve.wait_ge(s_l, 1)
            did(V.scalar_tensor_tensor(c3(lf, 2), c3(gl, 2)[:, :, 4:8], 0.0, c3(az[:, 0:8], 2), ALU.min, ALU.subtract), s_logf)
            b = filled(dve, "bcum")
            did(V.tensor_copy(b_sb, b[:, 0:8]))
            did(V.tensor_copy(bL, b[:, 8:12]), freed("bcum", "dve"))
            settle()
            did(V.tensor_tensor(c3(a_sb, 2), c3(gl, 2)[:, :, 0:4], c3(b_sb, 2), ALU.subtract))
            settle()
            for t in range(NT):
                did(V.tensor_tensor(c3(Dg[t], 4), again(ident, 4), over(a_sb[:, 4 * t:4 * t + 4], P), ALU.mult), s_diag)
            def conv(c0, n):
                dve.wait_ge(s_unit, n)
                for c in range(c0, c0 + 4):
                    did(V.tensor_scalar(y[:, c, :], u[:, c, 0:256], vecs[:, R_CW + c:R_CW + c + 1],
                                        vecs[:, R_CB + c:R_CB + c + 1], ALU.mult, ALU.add))
                for w in range(1, CONV):
                    settle()
                    for c in range(c0, c0 + 4):
                        did(V.scalar_tensor_tensor(y[:, c, :], u[:, c, w:w + 256],
                                                   vecs[:, R_CW + 8 * w + c:R_CW + 8 * w + c + 1], y[:, c, :],
                                                   ALU.mult, ALU.add))
                settle()
                did(dve.nop(), s_conv)

            def silu(c0, n, scale):
                yy = y_f[:, c0 * 256:(c0 + 4) * 256]
                dve.wait_ge(s_silu_e, n)
                did(V.tensor_scalar(silu_e, silu_e, 1.0, None, ALU.add))
                settle()
                did(V.reciprocal(silu_e, silu_e))
                settle()
                did(V.scalar_tensor_tensor(yy, yy, scale, silu_e, ALU.mult, ALU.mult))
                settle()
                did(dve.nop(), s_qk)

            def row_max(t):
                b = filled(dve, f"R{t}")
                did(V.tensor_tensor(c3(Rm, 4), c3(b[:, :], 4), again(cst[:, K_MTS:K_MTS + 128], 4), ALU.add), freed(f"R{t}", "dve"))
                settle()
                did(V.tensor_reduce(M[:, 4 * t:4 * t + 4], c3(Rm, 4), AX_X, ALU.max))
                settle()

            conv(0, 1)
            row_max(0)
            did(V.tensor_scalar(M[:, 0:4], M[:, 0:4], 0.0, None, ALU.max))
            settle()
            did(V.tensor_tensor(c3(Dg[0], 4), again(ident, 4), over(M[:, 0:4], P), ALU.mult), s_diag)
            row_max(1)
            def decay_pre(t):
                b = filled(dve, f"Mb{t}")
                did(V.scalar_tensor_tensor(c3(Dm[t], 4), c3(b[:, :], 4), -1.0, again(cst[:, K_MST:K_MST + 128], 4),
                                           ALU.mult, ALU.add))
                settle()
                did(V.tensor_tensor(c3(Dm[t], 4), c3(Dm[t], 4), over(a_sb[:, 4 * t:4 * t + 4], P), ALU.add), s_dpre)
                return b

            b = decay_pre(0)
            mlast = c3(b[:, :], 4)[:, :, 127]
            did(V.tensor_tensor(w0, a_sb[:, 0:4], mlast, ALU.subtract), s_dpre)
            did(V.tensor_tensor(mp1, bL, mlast, ALU.add), freed("Mb0", "dve"))
            settle()
            did(V.tensor_tensor(M[:, 4:8], M[:, 4:8], mp1, ALU.max))
            settle()
            did(V.tensor_tensor(c3(Dg[1], 4), again(ident, 4), over(M[:, 4:8], P), ALU.mult), s_diag)
            did(V.tensor_tensor(em, b_sb, M, ALU.add), s_empre)
            silu(0, 1, DB ** -0.5)
            conv(4, 2)
            b = decay_pre(1)
            did(V.scalar_tensor_tensor(c3(aib, 4), c3(b[:, :], 4), -1.0, over(mp1, P), ALU.mult, ALU.add), freed("Mb1", "dve"))
            settle()
            did(dve.nop(), s_dpre)
            silu(4, 2, 1.0)

            def attn_z(name, lo, n, heads):
                b = filled(dve, name)
                did(V.scalar_tensor_tensor(Z_f[:, lo:lo + 512].rearrange("p (h j) -> p h j", j=n), b[:, :].rearrange("p (h j) -> p h j", j=n),
                                           DA ** -0.5, Tb[:, heads:heads + 512 // n, 256 - n:256], ALU.mult, ALU.add), freed(name, "dve"))

            def attn_max(t, n):
                settle()
                o = 8 * t
                did(V.tensor_reduce(amax[:, o:o + 8], Z_f[:, 0:8 * n].rearrange("p (h j) -> p h j", j=n), AX_X, ALU.max))
                settle()
                did(V.tensor_tensor(amax[:, o:o + 8], amax[:, o:o + 8], sinks, ALU.max))
                settle()
                did(V.tensor_scalar(anm[:, o:o + 8], amax[:, o:o + 8], -1.0, None, ALU.mult))
                did(V.tensor_tensor(ask[:, o:o + 8], sinks, amax[:, o:o + 8], ALU.subtract))
                settle()
                did(dve.nop(), s_z)

            def attn_normalise(t, n):
                dve.wait_ge(s_pe_a, t + 1)
                o = 8 * t
                did(V.tensor_tensor(ard[:, o:o + 8], asum[:, o:o + 8], ask[:, o:o + 8], ALU.add))
                settle()
                did(V.reciprocal(ard[:, o:o + 8], ard[:, o:o + 8]))
                settle()
                z = Z_f[:, 0:8 * n].rearrange("p (h j) -> p h j", j=n)
                did(V.tensor_tensor(z, z, over(ard[:, o:o + 8], n), ALU.mult))
                settle()
                did(dve.nop(), s_pn)

            dve.wait_ge(s_T, 16)
            attn_z("sA0a", 0, 128, 0)
            attn_z("sA0b", 512, 128, 4)
            attn_max(0, 128)

            def weights_b(t, n):
                dve.wait_ge(s_D, n)
                b = filled(dve, f"sc{t}")
                did(V.tensor_tensor(Pm[t], b[:, :], Dm[t], ALU.mult), freed(f"sc{t}", "dve"))
                settle()
                did(dve.nop(), s_P)

            weights_b(0, 1)
            weights_b(1, 3)
            dve.wait_ge(s_D, 4)
            q1 = y[:, 0:4, P:T]
            did(V.tensor_tensor(q1, q1, c3(aib, 4), ALU.mult), s_q1)
            to_feature_major("mT", hmT, R_MEM, s_hmT)
            attn_normalise(0, 128)

            b0 = filled(dve, "num0")
            did(V.tensor_tensor(c3(vb[:, 0, :], 4), c3(vb[:, 0, :], 4), over(w0, P), ALU.mult), s_vw)

            def head_out(t, sig_done):
                o = ob[:, t, :]
                dve.wait_ge(s_sig, t + 1)
                did(V.tensor_scalar(o, o, 1.0, None, ALU.add))
                settle()
                did(V.reciprocal(o, o))
                nb = filled(dve, f"num{t}")
                db = filled(dve, f"den{t}")
                dve.wait_ge(s_em, 1)
                h4 = slice(4 * t, 4 * t + 4)
                did(V.tensor_copy(dd[:, h4], db[:, 0:4]), freed(f"den{t}", "dve"))
                settle()
                did(V.scalar_tensor_tensor(dd[:, h4], dd[:, h4], -1.0, dd[:, h4], ALU.mult, ALU.max))
                settle()
                did(V.tensor_tensor(dd[:, h4], dd[:, h4], em[:, h4], ALU.max))
                settle()
                did(V.reciprocal(dd[:, h4], dd[:, h4]))
                settle()
                did(V.tensor_tensor(c3(o, 4), c3(o, 4), over(dd[:, h4], P), ALU.mult))
                settle()
                did(V.tensor_tensor(o, o, nb[:, :], ALU.mult), freed(f"num{t}", "dve"))
                settle()
                did(V.tensor_tensor(Dg[0], o, o, ALU.mult))
                settle()
                did(V.tensor_reduce(hss[:, h4], c3(Dg[0], 4), AX_X, ALU.add))
                settle()
                did(V.tensor_scalar(hms[:, h4], hss[:, h4], 1.0 / DB, EPS, ALU.mult, ALU.add), s_mean)
                dve.wait_ge(s_root, 4 + t)
                did(V.tensor_tensor(c3(o, 4), c3(o, 4), over(hrs[:, h4], P), ALU.mult), s_hb)

            head_out(0, 1)
            b = filled(dve, "Cst")
            did(V.tensor_copy(Cs, b[:, :]), freed("Cst", "dve"))
            b = filled(dve, "nst")
            did(V.tensor_copy(n_sb, b[:, 0:4]), freed("nst", "dve"))
            settle()
            did(dve.nop(), s_C)
            dve.wait_ge(s_filled[jobs["tA0b"][0]], jobs["tA0b"][1] + 1)
            attn_z("sA1a", 0, 256, 0)
            attn_z("sA1c", 1024, 256, 4)
            attn_z("sA1b", 512, 256, 2)
            attn_z("sA1d", 1536, 256, 6)
            attn_max(1, 256)

            def mix_b(t):
                name = f"hb{t}T"
                b = filled(dve, name)
                did(V.tensor_tensor(hT[:, 4:8, t * P:(t + 1) * P], c3(b[:, :], 4), over(vecs[:, R_MLSTM:R_MLSTM + 4], P),
                                    ALU.mult), freed(name, "dve"))
                settle()
                did(dve.nop(), s_mixB)

            mix_b(0)
            attn_normalise(1, 256)
            head_out(1, 2)
            mix_b(1)
            did(dve.nop(), s_left)

            def residual(n0, t, half):
                name = f"U{n0 + 2 * t + half}"
                b = filled(dve, name)
                xs = x_sb[:, t, half * 512:(half + 1) * 512]
                did(V.tensor_tensor(xs, xs, b[:, :], ALU.add), freed(name, "dve"))
                settle()

            rms_rows(x_sb, xn, 4, 5, s_x1n, lambda t, half: residual(19, t, half))
            evacuate("cT1a", hT, R_CROSS, s_hc)
            for t in range(NT):
                for half in range(2):
                    b = filled(dve, f"sX{t}{'ab'[half]}")
                    o = slice(t * 4 + 2 * half, t * 4 + 2 * half + 2)
                    did(V.tensor_reduce(cmax[:, o], c3(b[:, :], 2), AX_X, ALU.max))
                    settle()
                    did(V.tensor_scalar(cmax[:, o], cmax[:, o], -DX ** -0.5, None, ALU.mult), s_cm)
            for t in range(NT):
                dve.wait_ge(s_cp, t + 1)
                o = slice(t * 4, t * 4 + 4)
                did(V.reciprocal(csum[:, o], csum[:, o]))
                settle()
                z = Z_f[:, t * 1024:(t + 1) * 1024].rearrange("p (h j) -> p h j", h=HX)
                did(V.tensor_tensor(z, z, over(csum[:, o], 256), ALU.mult), s_cpn)

            rms_rows(x_sb, xn, 6, 7, s_x2n, lambda t, half: residual(27, t, half))
            moe_dve(dve, lane, rms_rows, evacuate)


_INS = ["x", "mem", "rel_bias_table", "w_in", "w_out", "w_cq", "w_ck", "w_cv", "w_co",
        "w_exp_gate", "w_exp_up", "w_exp_down", "norm_final"]


def constants():
    import math
    import numpy as np

    i, j = np.arange(P)[:, None], np.arange(P)[None, :]
    c = np.zeros((P, K_ALL), np.float32)
    c[:, K_ID:K_ID + 128] = i == j
    c[:, K_TRIU:K_TRIU + 128] = i <= j
    c[:, K_STRICT:K_STRICT + 128] = i < j
    c[:, K_MTS:K_MTS + 128] = np.where(j <= i, 0.0, NEG)
    c[:, K_MST:K_MST + 128] = np.where(i <= j, 0.0, NEG)
    c[:, K_ONES:K_ONES + 128] = 1.0
    c[:, K_SLOT:K_SLOT + 128] = j % SLOTS
    c[:, K_RG:K_RG + 4] = NG - np.arange(NG)
    c[:, K_RE:K_RE + 32] = NE - np.arange(NE)
    bands = np.zeros((33, 384), np.float32)
    for m in range(384):
        n = 255 - m
        if 0 <= n < 128:
            big = 16 + int(np.float32(np.log(np.float32(max(n, 1)) / np.float32(16))) / np.float32(math.log(8.0)) * np.float32(16))
            bands[n if n < 16 else min(big, 31), m] = 1.0
        else:
            bands[32, m] = NEG
    return c, bands


def kernel(**inputs):
    import numpy as _np
    import concourse.bacc as _bacc
    from concourse import mybir as _mybir
    from concourse.bass_utils import run_bass_kernel_spmd as _run

    nc = _bacc.Bacc("TRN2", target_bir_lowering=False, num_devices=1)
    arrays, args = {}, []
    flat = {name: _np.asarray(inputs[name]).reshape(-1) for name in inputs}
    groups = {
        "vectors": _np.concatenate([flat[n] for n in ("norm_mix", "norm_cross", "norm_mem", "norm_moe", "mlstm_norm",
                                                      "conv_w", "conv_b")]).reshape(R_ALL, P),
        "biases": _np.concatenate([flat[n] for n in ("gate_bias_i", "gate_bias_f", "attn_sinks", "b_router_group",
                                                     "b_router_expert")]),
        "routers": _np.concatenate([_np.asarray(inputs["w_router_group"])[0], _np.asarray(inputs["w_router_expert"])[0]], axis=1),
    }
    for name in [*_INS, *groups]:
        a = _np.ascontiguousarray(groups[name] if name in groups else inputs[name])
        arrays[f"in_{name}_dram"] = a
        args.append(nc.dram_tensor(f"in_{name}_dram", a.shape, _mybir.dt.from_np(a.dtype), kind="ExternalInput").ap())
    for name, a in zip(("tile", "bands"), constants()):
        arrays[f"const_{name}_dram"] = a
        args.append(nc.dram_tensor(f"const_{name}_dram", a.shape, _mybir.dt.from_np(a.dtype), kind="ExternalInput").ap())
    args.append(nc.dram_tensor("out_0_dram", (1, T, D), _mybir.dt.from_np(_np.dtype("float32")), kind="ExternalOutput").ap())
    hymba_layer(nc, *args)
    r = _run(nc, [arrays], core_ids=[0])
    return r.results[0]["out_0_dram"]
```
